# Optimizing a Trainium2 kernel written in Bass

```python
import math
import jax, jax.numpy as jnp
from jax import lax
import numpy as np

D_MODEL = 1024
BATCH = 1
SEQ = 128
DEPTH = 2
DEC_BATCH = 1
DEC_SEQ = 128
PAST_LEN = 128

GRID_W = 64
N_LAYERS_A = (DEPTH + 1) // 2
N_LAYERS_B = DEPTH // 2
A_HEADS = 8
A_DQK = 128
A_DV = 256
A_QK = A_HEADS * A_DQK
A_VW = A_HEADS * A_DV
A_IN_COLS = 2 * A_QK + 2 * A_VW + 4 * A_HEADS
A_CONV = 5
A_CHUNK = 64
B_CONV = 31
D_FF = 3584
N_EXPERTS = 8
TOP_K = 2
EPS = 1e-6
POS_THETA = 10000.0

kernel_name = 'hybrid_mlstm_conformer_diffusion_step'

def rmsnorm(x, g):
    xf = x.astype(jnp.float32)
    y = xf * lax.rsqrt(jnp.mean(xf * xf, axis=-1, keepdims=True) + EPS)
    return (y * g.astype(jnp.float32)).astype(x.dtype)

def dwconv(x, w):
    W, C = w.shape
    return lax.conv_general_dilated(x, w.reshape(W, 1, C), (1,), [(W // 2, W // 2)],
                                    dimension_numbers=('NWC', 'WIO', 'NWC'), feature_group_count=C)

def grid_pos_embed(rows, dtype):
    r = jnp.repeat(jnp.arange(rows, dtype=jnp.float32), GRID_W)
    col = jnp.tile(jnp.arange(GRID_W, dtype=jnp.float32), rows)
    quarter = D_MODEL // 4
    freqs = POS_THETA ** (-jnp.arange(quarter, dtype=jnp.float32) / quarter)
    ar = r[:, None] * freqs
    ac = col[:, None] * freqs
    pe = jnp.concatenate([jnp.sin(ar), jnp.cos(ar), jnp.sin(ac), jnp.cos(ac)], axis=-1)
    return pe.astype(dtype)

def mlstm_chunkwise(q, k, v, i_pre, logf, C0, n0, m0):
    B, H, L, K = q.shape
    V = v.shape[-1]
    nc = L // A_CHUNK
    qc = q.reshape(B, H, nc, A_CHUNK, K)
    kc = k.reshape(B, H, nc, A_CHUNK, K)
    vc = v.reshape(B, H, nc, A_CHUNK, V)
    ic = i_pre.reshape(B, H, nc, A_CHUNK)
    b = jnp.cumsum(logf.reshape(B, H, nc, A_CHUNK), axis=-1)
    b_last = b[..., -1]
    a = b_last[..., None] - b + ic
    a_max = jnp.max(a, axis=-1)
    ea = jnp.exp(a - a_max[..., None])
    kv = jnp.einsum('bhnjk,bhnjv,bhnj->bhnkv', kc, vc, ea)
    ks = jnp.einsum('bhnjk,bhnj->bhnk', kc, ea)

    def step(carry, inp):
        C, n, m = carry
        kv_c, ks_c, bl, am = inp
        m_new = jnp.maximum(bl + m, am)
        dec = jnp.exp(bl + m - m_new)
        inj = jnp.exp(am - m_new)
        C_new = dec[..., None, None] * C + inj[..., None, None] * kv_c
        n_new = dec[..., None] * n + inj[..., None] * ks_c
        return (C_new, n_new, m_new), (C, n, m)

    xs = (jnp.moveaxis(kv, 2, 0), jnp.moveaxis(ks, 2, 0), jnp.moveaxis(b_last, 2, 0), jnp.moveaxis(a_max, 2, 0))
    (Cf, nf, mf), (Cs, ns, ms) = lax.scan(step, (C0, n0, m0), xs)
    Cs = jnp.moveaxis(Cs, 0, 2)
    ns = jnp.moveaxis(ns, 0, 2)
    ms = jnp.moveaxis(ms, 0, 2)

    causal = jnp.tril(jnp.ones((A_CHUNK, A_CHUNK), dtype=bool))
    Dlog = b[..., :, None] - b[..., None, :] + ic[..., None, :]
    Dlog = jnp.where(causal, Dlog, -jnp.inf)
    inter = b + ms[..., None]
    m_t = jnp.maximum(inter, jnp.max(Dlog, axis=-1))
    s = jnp.einsum('bhntk,bhnjk->bhntj', qc, kc) * jnp.exp(Dlog - m_t[..., None])
    sc = jnp.exp(inter - m_t)
    num = jnp.einsum('bhntj,bhnjv->bhntv', s, vc) + sc[..., None] * jnp.einsum('bhntk,bhnkv->bhntv', qc, Cs)
    den = jnp.sum(s, axis=-1) + sc * jnp.einsum('bhntk,bhnk->bhnt', qc, ns)
    h = num / jnp.maximum(jnp.abs(den), jnp.exp(-m_t))[..., None]
    return h.reshape(B, H, L, V), (Cf, nf, mf)

def mlstm_mixer(h, w_in, w_conv, b_gate, gn_g, w_out, C0, n0, m0):
    B, L, _ = h.shape
    f32 = jnp.float32
    proj = h @ w_in
    qk = proj[..., :2 * A_QK]
    v = proj[..., 2 * A_QK:2 * A_QK + A_VW]
    o = proj[..., 2 * A_QK + A_VW:2 * A_QK + 2 * A_VW]
    g = proj[..., 2 * A_QK + 2 * A_VW:]
    qk = jax.nn.silu(dwconv(qk, w_conv))

    def heads(t, dh):
        return t.reshape(B, L, A_HEADS, dh).transpose(0, 2, 1, 3).astype(f32)

    q = heads(qk[..., :A_QK], A_DQK) * (A_DQK ** -0.5)
    k = heads(qk[..., A_QK:], A_DQK)
    vh = heads(v, A_DV)
    gates = (g.astype(f32).reshape(B, L, 4, A_HEADS) + b_gate.astype(f32)).transpose(0, 2, 3, 1)
    i_f, i_b = gates[:, 0], gates[:, 2]
    logf_f = jax.nn.log_sigmoid(gates[:, 1])
    logf_b = jax.nn.log_sigmoid(gates[:, 3])
    C0 = C0.astype(f32)
    n0 = n0.astype(f32)
    m0 = m0.astype(f32)
    hf, (Cf, nf, mf) = mlstm_chunkwise(q, k, vh, i_f, logf_f, C0[:, 0], n0[:, 0], m0[:, 0])
    flip = lambda t: jnp.flip(t, axis=2)
    hb, (Cb, nb, mb) = mlstm_chunkwise(flip(q), flip(k), flip(vh), flip(i_b), flip(logf_b),
                                       C0[:, 1], n0[:, 1], m0[:, 1])
    hs = hf + flip(hb)
    hs = hs * lax.rsqrt(jnp.mean(hs * hs, axis=-1, keepdims=True) + EPS)
    hs = hs.transpose(0, 2, 1, 3).reshape(B, L, A_VW).astype(h.dtype) * gn_g
    out = (jax.nn.sigmoid(o) * hs) @ w_out
    return out, jnp.stack([Cf, Cb], axis=1), jnp.stack([nf, nb], axis=1), jnp.stack([mf, mb], axis=1)

def conv_mixer(h, w_pw1, w_dw, b_dw, norm_g, w_pw2):
    u = h @ w_pw1
    u = u[..., :D_MODEL] * jax.nn.sigmoid(u[..., D_MODEL:])
    u = dwconv(u, w_dw) + b_dw
    u = jax.nn.silu(rmsnorm(u, norm_g))
    return u @ w_pw2

def swiglu(t, w1, w2):
    u = t @ w1
    return (jax.nn.silu(u[..., :D_FF]) * u[..., D_FF:]) @ w2

def moe_ffn(h, w_router, w1, w2):
    B, L, D = h.shape
    t = h.reshape(B * L, D)
    logits = (t @ w_router).astype(jnp.float32)
    top_v, top_i = lax.top_k(logits, TOP_K)
    probs = jax.nn.softmax(top_v, axis=-1)
    combine = jnp.sum(jax.nn.one_hot(top_i, N_EXPERTS, dtype=jnp.float32) * probs[..., None], axis=1)
    out = jnp.zeros_like(t)
    for e in range(N_EXPERTS):
        out = out + combine[:, e:e + 1].astype(t.dtype) * swiglu(t, w1[e], w2[e])
    return out.reshape(B, L, D)

def trunk(x, cond, st_C, st_n, st_m, w_ada, b_ada, norm_mix, norm_ffn,
          a_w_in, a_w_conv, a_b_gate, a_gn, a_w_out,
          b_w_pw1, b_w_dw, b_b_dw, b_norm, b_w_pw2,
          ff_w1, ff_w2, moe_router, moe_w1, moe_w2, norm_out):
    new_C, new_n, new_m = [], [], []
    silu_c = jax.nn.silu(cond)
    for i in range(DEPTH):
        j = i // 2
        mod = (silu_c @ w_ada[i] + b_ada[i]).reshape(cond.shape[0], 6, D_MODEL)
        sh1, sc1, g1, sh2, sc2, g2 = [mod[:, s, None, :] for s in range(6)]
        h = rmsnorm(x, norm_mix[i]) * (1 + sc1) + sh1
        if i % 2 == 0:
            y, Cn, nn_, mn = mlstm_mixer(h, a_w_in[j], a_w_conv[j], a_b_gate[j], a_gn[j], a_w_out[j],
                                         st_C[:, j], st_n[:, j], st_m[:, j])
            new_C.append(Cn)
            new_n.append(nn_)
            new_m.append(mn)
        else:
            y = conv_mixer(h, b_w_pw1[j], b_w_dw[j], b_b_dw[j], b_norm[j], b_w_pw2[j])
        x = x + g1 * y.astype(x.dtype)
        h = rmsnorm(x, norm_ffn[i]) * (1 + sc2) + sh2
        if i % 2 == 0:
            y = swiglu(h, ff_w1[j], ff_w2[j])
        else:
            y = moe_ffn(h, moe_router[j], moe_w1[j], moe_w2[j])
        x = x + g2 * y.astype(x.dtype)
    return rmsnorm(x, norm_out), jnp.stack(new_C, axis=1), jnp.stack(new_n, axis=1), jnp.stack(new_m, axis=1)

def setup_inputs(seed: int = 0) -> dict:
    key = jax.random.key(seed)
    ks = jax.random.split(key, 32)
    nrm = lambda k, shape, s: jax.random.normal(k, shape, jnp.float32) * s
    gain = lambda k, shape: 1.0 + nrm(k, shape, 0.02)
    D = D_MODEL
    return {
        'x_prompt': nrm(ks[0], (BATCH, SEQ, D), 1.0),
        'x_sample': nrm(ks[1], (DEC_BATCH, DEC_SEQ, D), 1.0),
        'state_C': nrm(ks[2], (DEC_BATCH, N_LAYERS_A, 2, A_HEADS, A_DQK, A_DV), 0.5),
        'state_n': nrm(ks[3], (DEC_BATCH, N_LAYERS_A, 2, A_HEADS, A_DQK), 0.5),
        'state_m': nrm(ks[4], (DEC_BATCH, N_LAYERS_A, 2, A_HEADS), 1.0),
        'c': nrm(ks[5], (DEC_BATCH, D), 1.0),
        'c_ctx': nrm(ks[6], (D,), 1.0),
        'w_ada': nrm(ks[7], (DEPTH, D, 6 * D), 0.5 * D ** -0.5),
        'b_ada': nrm(ks[8], (DEPTH, 6 * D), 0.02),
        'norm_mix': gain(ks[9], (DEPTH, D)),
        'norm_ffn': gain(ks[10], (DEPTH, D)),
        'a_w_in': nrm(ks[11], (N_LAYERS_A, D, A_IN_COLS), D ** -0.5),
        'a_w_conv': nrm(ks[12], (N_LAYERS_A, A_CONV, 2 * A_QK), A_CONV ** -0.5),
        'a_b_gate': jnp.array([0.0, 3.0, 0.0, 3.0], jnp.float32)[None, :, None]
                    + nrm(ks[13], (N_LAYERS_A, 4, A_HEADS), 0.1),
        'a_gn': gain(ks[14], (N_LAYERS_A, A_VW)),
        'a_w_out': nrm(ks[15], (N_LAYERS_A, A_VW, D), A_VW ** -0.5),
        'b_w_pw1': nrm(ks[16], (N_LAYERS_B, D, 2 * D), D ** -0.5),
        'b_w_dw': nrm(ks[17], (N_LAYERS_B, B_CONV, D), B_CONV ** -0.5),
        'b_b_dw': nrm(ks[18], (N_LAYERS_B, D), 0.02),
        'b_norm': gain(ks[19], (N_LAYERS_B, D)),
        'b_w_pw2': nrm(ks[20], (N_LAYERS_B, D, D), D ** -0.5),
        'ff_w1': nrm(ks[21], (N_LAYERS_A, D, 2 * D_FF), D ** -0.5),
        'ff_w2': nrm(ks[22], (N_LAYERS_A, D_FF, D), D_FF ** -0.5),
        'moe_router': nrm(ks[23], (N_LAYERS_B, D, N_EXPERTS), D ** -0.5),
        'moe_w1': nrm(ks[24], (N_LAYERS_B, N_EXPERTS, D, 2 * D_FF), D ** -0.5),
        'moe_w2': nrm(ks[25], (N_LAYERS_B, N_EXPERTS, D_FF, D), D_FF ** -0.5),
        'norm_out': gain(ks[26], (D,)),
    }

def reference(x_prompt, x_sample, state_C, state_n, state_m, c, c_ctx, w_ada, b_ada, norm_mix, norm_ffn,
              a_w_in, a_w_conv, a_b_gate, a_gn, a_w_out, b_w_pw1, b_w_dw, b_b_dw, b_norm, b_w_pw2,
              ff_w1, ff_w2, moe_router, moe_w1, moe_w2, norm_out):
    f32 = jnp.float32
    nb = x_prompt.shape[0]
    zC = jnp.zeros((nb, N_LAYERS_A, 2, A_HEADS, A_DQK, A_DV), f32)
    zn = jnp.zeros((nb, N_LAYERS_A, 2, A_HEADS, A_DQK), f32)
    zm = jnp.zeros((nb, N_LAYERS_A, 2, A_HEADS), f32)
    y_prompt, new_state_C, new_state_n, new_state_m = trunk(
        x_prompt, c_ctx[None, :], zC, zn, zm, w_ada, b_ada, norm_mix, norm_ffn,
        a_w_in, a_w_conv, a_b_gate, a_gn, a_w_out, b_w_pw1, b_w_dw, b_b_dw, b_norm, b_w_pw2,
        ff_w1, ff_w2, moe_router, moe_w1, moe_w2, norm_out)
    ROWS = x_sample.shape[1] // GRID_W
    xs = x_sample + grid_pos_embed(ROWS, x_sample.dtype)[None]
    y_sample, _, _, _ = trunk(
        xs, c, state_C, state_n, state_m, w_ada, b_ada, norm_mix, norm_ffn,
        a_w_in, a_w_conv, a_b_gate, a_gn, a_w_out, b_w_pw1, b_w_dw, b_b_dw, b_norm, b_w_pw2,
        ff_w1, ff_w2, moe_router, moe_w1, moe_w2, norm_out)
    return (y_prompt, y_sample, new_state_C, new_state_n, new_state_m)


_drawn_inputs = setup_inputs


def setup_inputs(seed=0):
    import zlib

    import numpy as np

    out = dict(_drawn_inputs(seed))
    spreads = {}
    factors = {'state_C': 4.525,
     'state_n': 8.0,
     'state_m': 6.698,
     'norm_ffn': 4.118,
     'a_gn': 6.973,
     'b_b_dw': 8.0,
     'b_norm': 6.695,
     'norm_out': 2.791}
    for name, (base, spread) in spreads.items():
        noise = np.random.default_rng([zlib.crc32(name.encode()), seed]).standard_normal(out[name].shape)
        drawn = base * np.exp(spread * noise) if base else spread * noise
        out[name] = __import__('jax').numpy.asarray(drawn.astype(out[name].dtype))
    for name, factor in factors.items():
        out[name] = (out[name] * factor).astype(out[name].dtype)
    return out
```

```python
import numpy as np
import concourse.bass as bass
from concourse import mybir
from contextlib import ExitStack

P = 128
D = 1024
KD = D // P
G = 2
T = G * P
HEADS = 8
DV = 256
DVA = DV + 1
DIR = 2
FF = 3584
FC = FF // P
EXPERTS = 8
A_TAPS, B_TAPS = 5, 31
EPS = 1e-6
WORK = 17040
Q_SCALE = float(P) ** -0.5
ROWS = 32 * (DIR - 1) + HEADS
BIG = 1e30

SLOTS = 7
STAGE = 3072
MIX = 2048
ADA_STAGES = 2 * 6 * D // 256
ADA_FIRST = 8
ST_IN = ADA_FIRST
N_IN = 24
ST_ADA = ST_IN + N_IN
ADA_LAST = 3 * 4
ADA_MID = ADA_STAGES - ADA_FIRST - ADA_LAST
ST_OUT = ST_ADA + ADA_MID
N_OUT = 8
ST_FF = ST_OUT + N_OUT
ST_PW1 = ST_FF + FC
N_PW1 = 8


def ada_beside(s):
    return ADA_FIRST + ADA_MID + ADA_LAST * (s + 1) // N_PW1


def pw1_stage(s):
    return ST_PW1 + s + (ada_beside(s - 1) - ADA_FIRST - ADA_MID)


ST_PW2 = ST_PW1 + N_PW1 + ADA_LAST
N_PW2 = 4
ST_MOE = ST_PW2 + N_PW2
ITS = G * HEADS

V_ADA = 0
V_NMIX = V_ADA + 2 * 6 * KD
V_NFFN = V_NMIX + 2 * KD
V_GN = V_NFFN + 2 * KD
V_BDW = V_GN + 2 * KD
V_BNORM = V_BDW + KD
V_ACONV = V_BNORM + KD
V_BCONV = V_ACONV + A_TAPS * 2 * KD
V_COND = V_BCONV + B_TAPS * KD
V_ALL = V_COND + KD * G
C_ID = 0
C_ONE = P
C_MASK = 2 * P
C_DESC = C_MASK + DIR * P
C_EPS = C_DESC + G * EXPERTS
C_TRI = C_EPS + 1
C_IOTA = C_TRI + P
C_ALL = C_IOTA + P

OVER = (2 * G * P - 1) // (P + 1)
ITEMS = EXPERTS + OVER
COLS = ITEMS + 1


def mlstm_conformer_kernel(nc, vecs, consts, rowc, x_in, pos, w_gate, w_router, mix, ff, moe, c0, norm_out,
                           y_out, c_out, m_out):
    f32 = mybir.dt.float32
    ALU = mybir.AluOpType
    ACT = mybir.ActivationFunctionType
    X = mybir.AxisListType.X

    ctx = ExitStack()
    with ctx:
        def sb(name, *shape):
            return ctx.enter_context(nc.sbuf_tensor(name, list(shape), f32))

        def sem(name):
            return ctx.enter_context(nc.semaphore(name))

        ring = sb("ring", P, SLOTS, STAGE)
        x = sb("x", P, G, D)
        xn = sb("xn", P, G, D)
        hT = sb("hT", P, KD, T)
        gate_b = sb("gate_b", P, G * D)
        so = sb("so", P, 2 * HEADS, T)
        vec = sb("vec", P, V_ALL)
        cst = sb("cst", P, C_ALL)
        rc = sb("rc", ROWS, 4)
        wg = sb("wg", P, KD, 2, ROWS)
        wr = sb("wr", P, KD, EXPERTS)
        silu_c = sb("silu_c", P, KD * G)
        ce = sb("ce", P, KD * G)
        cd = sb("cd", P, KD * G)
        mod = sb("mod", P, 12, KD, G)
        scl = sb("scl", P, 4, KD, G)
        ss = sb("ss", P, G)
        rstd = sb("rstd", P, G)
        lnv = sb("lnv", P, G)
        small = sb("small", P, 16)
        root = sb("root", P, 4, G)
        work = sb("work", P, WORK)
        at = [0]

        def carve(*shape, rows=P):
            n = int(np.prod(shape))
            a = work[0:rows, at[0]:at[0] + n]
            at[0] += n
            assert at[0] <= WORK
            if len(shape) == 1:
                return a
            names = "abcd"[:len(shape)]
            return a.rearrange(f"p ({' '.join(names)}) -> p {' '.join(names)}",
                               **{k: v for k, v in zip(names, shape)})

        qkT = carve(2 * HEADS, T)
        vaug = carve(G, HEADS, DVA)
        c0b = carve(2, DIR, DVA)
        stc = carve(2, DIR, DVA)
        row = carve(8, P, rows=ROWS)
        nat = carve(8, P, rows=ROWS)
        col = carve(6, ROWS)
        kscale = carve(2, ROWS)
        kw = carve(DIR, P)
        qcs = carve(DIR, DVA)
        nm = carve(DIR, DVA)
        h0 = carve(DV)
        hs = carve(DV)
        hn = carve(DV)
        hsq = carve(DV)
        shared = at[0]
        tmp = carve(2, DIR, P)
        pe_ = carve(2, DIR, P)
        sT = carve(2, DIR, P)
        at[0] = shared
        ca = carve(2, 2, T)
        eq = carve(2, 2, T)
        rt = xn[0:ROWS, :, :].rearrange("p g d -> p (g d)").rearrange("p (n g t) -> p n g t", g=G, t=P)
        pad = gate_b[:, 0:2 * 2 * G * (P + A_TAPS - 1)].rearrange("p (b j g t) -> p b j g t", b=2, j=2, g=G)
        at[0] = 0
        fe = carve(2, T)
        fd = carve(T)
        ft = carve(2, T)
        fact = carve(2, T)
        acc = carve(G, D)
        pad31 = carve(KD, G, P + B_TAPS - 1)
        cv = carve(KD, T)
        z = carve(KD, T)
        ez = carve(KD, T)
        sqb = carve(2, T)
        rb = carve(T)
        assert at[0] <= WORK
        lg = carve(G, EXPERTS)
        l2 = carve(G, EXPERTS)
        oh = carve(2, G, EXPERTS)
        key = carve(G, EXPERTS)
        comb = carve(G, EXPERTS)
        tk = carve(12, G)
        sel = carve(G, EXPERTS)
        item_pos = carve(G, COLS)
        item_comb = carve(G, COLS)
        over = carve(4, EXPERTS)
        hit = carve(EXPERTS)
        prod = carve(G, EXPERTS)
        rsum = carve(4, G)
        plan_f = carve(8)
        pick = carve(G, P)
        pick_w = carve(G, P)
        back = carve(G, P)
        y_sb = carve(D)
        gate = gate_b[:, 0:G * D].rearrange("p (g d) -> p g d", g=G)
        ident = cst[:, C_ID:C_ID + P]
        ones = cst[:, C_ONE:C_ONE + P]
        mask = cst[:, C_MASK:C_MASK + DIR * P].rearrange("p (d t) -> p d t", d=DIR)
        desc = cst[:, C_DESC:C_DESC + G * EXPERTS].rearrange("p (g e) -> p g e", g=G)
        eps = cst[:, C_EPS:C_EPS + 1]
        tri = cst[:, C_TRI:C_TRI + P]
        iota = cst[:, C_IOTA:C_IOTA + P]
        plan = ctx.enter_context(nc.sbuf_tensor("plan", [1, 8], mybir.dt.int32))
        htok = xn
        hgT = hT[:, :, 0:P]

        ps = ctx.enter_context(nc.psum_tensor("ps", [P, 8, 512], f32))
        MODB, MISC, UB, YB, QB = 0, 1, 2, 4, 6

        vec_in, cst_in, x_in_s, pos_in, late_in = sem("vec_in"), sem("cst_in"), sem("x_in_s"), sem("pos_in"), sem("late_in")
        no_in = sem("no_in")
        loaded = [sem(f"loaded{i}") for i in range(SLOTS)]
        stage_used = sem("stage_used")
        cond_exp, cond_ready = sem("cond_exp"), sem("cond_ready")
        dve_chain, act_chain = sem("dve_chain"), sem("act_chain")
        x_ready, ss_ready, rstd_ready, hs_squared = sem("x_ready"), sem("ss_ready"), sem("rstd_ready"), sem("hs_squared")
        xn0_ready, xn1_ready, turned = sem("xn0_ready"), sem("xn1_ready"), sem("turned")
        hT0_ready, hT1_ready = sem("hT0_ready"), sem("hT1_ready")
        mod_ready = sem("mod_ready")
        gates_psum, gate_raw, gate_abs, gate_ln = sem("gates_psum"), sem("gate_raw"), sem("gate_abs"), sem("gate_ln")
        gate_M, gate_exps, nat_ready, cols_psum, cols_ready = (sem("gate_M"), sem("gate_exps"), sem("nat_ready"),
                                                               sem("cols_psum"), sem("cols_ready"))
        memsets = sem("memsets")
        proj_out, conv_done, qk_exp, qk_done, so_ready = (sem("proj_out"), sem("conv_done"), sem("qk_exp"),
                                                          sem("qk_done"), sem("so_ready"))
        front, tmp_ready, p_ready, s_ready, kw_ready = (sem("front"), sem("tmp_ready"), sem("p_ready"),
                                                        sem("s_ready"), sem("kw_ready"))
        num_done, qc_used, num_used, hn_ready = sem("num_done"), sem("qc_used"), sem("num_used"), sem("hn_ready")
        c0_in = [sem("c0_in0"), sem("c0_in1")]
        c_stored = [sem("c_stored0"), sem("c_stored1")]
        m_stored, m_ready, y_stored = sem("m_stored"), sem("m_ready"), sem("y_stored")
        hT_back, og_ready = sem("hT_back"), sem("og_ready")
        gateb_psum, gateb_ready = sem("gateb_psum"), sem("gateb_ready")
        u_done, e_done, act_done = sem("u_done"), sem("e_done"), sem("act_done")
        glu_exp, glu_done, cv_ready, sq_ready, ssq_done = (sem("glu_exp"), sem("glu_done"), sem("cv_ready"),
                                                           sem("sq_ready"), sem("ssq_done"))
        rb_ready, z_ready, ez_ready, zs_ready = sem("rb_ready"), sem("z_ready"), sem("ez_ready"), sem("zs_ready")
        route_psum, route_gap, route_exp = sem("route_psum"), sem("route_gap"), sem("route_exp")
        fin_ready = sem("fin_ready")
        sel_ready, pos_psum, plan_ready = sem("sel_ready"), sem("pos_psum"), sem("plan_ready")
        htok_psum, htok_ready0, htok_ready1 = sem("htok_psum"), sem("htok_ready0"), sem("htok_ready1")
        pick_ready, gathered, picks_used = sem("pick_ready"), sem("gathered"), sem("picks_used")
        hg0_ready, hg1_ready, back_ready = sem("hg0_ready"), sem("hg1_ready"), sem("back_ready")
        y_ready, scattered, acc0_free, acc1_free = sem("y_ready"), sem("scattered"), sem("acc0_free"), sem("acc1_free")

        block = ctx.enter_context(nc.Block())

        def slot(n):
            return n % SLOTS

        def ada_stage(a):
            if a < ADA_FIRST:
                return a
            if a < ADA_FIRST + ADA_MID:
                return ST_ADA + a - ADA_FIRST
            s = next(s for s in range(N_PW1) if a < ada_beside(s))
            return pw1_stage(s) + 1 + a - ada_beside(s - 1)

        def ada_through(it):
            return ADA_FIRST + ADA_MID * (it + 1) // ITS

        @block.sync
        def _(sp):
            def load(src, base, count, width, first=0):
                def one(n, row, j):
                    sp.wait_ge(stage_used, n - SLOTS + 1)
                    sp.dma_start(ring[:, slot(base + j), 0:width],
                                 src[bass.ds(row, 1), :, :].rearrange("o p n -> (o p) n")
                                 ).then_inc(loaded[slot(base + j)], 16)
                turns = count // SLOTS
                if turns > 1:
                    with sp.Fori(0, turns) as i:
                        for j in range(SLOTS):
                            one(i * SLOTS + (base + j), i * SLOTS + (first + j), j)
                else:
                    turns = 0
                for j in range(turns * SLOTS, count):
                    one(base + j, first + j, j)

            sp.dma_start(vec[:, :], vecs).then_inc(vec_in, 16)
            sp.dma_start(cst[:, :], consts).then_inc(cst_in, 16)
            sp.dma_start(x[:, :, :], x_in).then_inc(x_in_s, 16)
            sp.dma_start(gate[:, 1, :], pos).then_inc(pos_in, 16)
            for n in range(SLOTS):
                sp.dma_start(ring[:, n, 0:MIX], mix[n]).then_inc(loaded[n], 16)
            load(mix, SLOTS, ST_FF - SLOTS, MIX, SLOTS)
            load(ff, ST_FF, FC, STAGE)
            load(mix, ST_PW1, ST_MOE - ST_PW1, MIX, ST_FF)
            load(moe, ST_MOE, (EXPERTS - 1) * FC, STAGE)
            sp.wait_ge(plan_ready, 1)
            items = sp.value_load(plan[0:1, 7:8], min_val=1, max_val=1 + OVER)
            base = ST_MOE + (EXPERTS - 1) * FC
            with sp.Fori(0, items) as k:
                e = sp.value_load(plan[0:1, bass.ds(k + 1, 1)], min_val=0, max_val=EXPERTS - 1)
                with sp.Fori(0, FC // SLOTS) as i:
                    for j in range(SLOTS):
                        sp.wait_ge(stage_used, k * FC + i * SLOTS + (base + j - SLOTS + 1))
                        sp.dma_start(ring[:, slot(base + j), :],
                                     moe[bass.ds(e * FC + i * SLOTS + j, 1), :, :].rearrange("o p n -> (o p) n")
                                     ).then_inc(loaded[slot(base + j)], 16)

        @block.gpsimd
        def _(pool):
            pool.memset(vaug[:, :, :, DV:DVA], 1.0).then_inc(memsets, 1)
            pool.wait_ge(x_ready, 1)
            pool.memset(pad[:, :, :, :, 0:2], 0.0).then_inc(memsets, 1)
            pool.memset(pad[:, :, :, :, P + 2:P + 4], 0.0).then_inc(memsets, 1)
            for h in range(HEADS):
                if h >= 2:
                    pool.wait_ge(num_done, 2 * (h - 2) + 2)
                pool.dma_start(c0b[:, h % 2, :, :], c0[h]).then_inc(c0_in[h % 2], 16)
            pool.wait_ge(x_ready, 3)
            pool.memset(pad31, 0.0).then_inc(memsets, 1)
            pool.memset(acc[:, 0, :], 0.0).then_inc(acc0_free, 1)
            pool.memset(acc[:, 1, :], 0.0).then_inc(acc1_free, 1)

        @block.scalar
        def _(act):
            n_chain = [0]

            def link(ins):
                n_chain[0] += 1
                ins.then_inc(act_chain, 1)
                act.wait_ge(act_chain, n_chain[0])

            act.wait_ge(pos_in, 16)
            act.dma_start(wg[:, :, :, :], w_gate).then_inc(late_in, 16)
            act.dma_start(rc[:, :], rowc).then_inc(late_in, 16)
            act.dma_start(wr[:, :, :], w_router).then_inc(late_in, 16)

            act.activation(ce[:, :], vec[:, V_COND:V_COND + KD * G], ACT.Exp, scale=-1.0).then_inc(cond_exp, 1)

            def square_sum(q):
                act.wait_ge(x_ready, q + 1)
                act.activation(xn[:, 0, :], x[:, 0, :], ACT.Square, accum_out=ss[:, 0:1]).then_inc(ss_ready, 1)
                act.wait_ge(rstd_ready, q + 1)

            def norm_turn(q):
                square_sum(q)
                act.activation(xn[:, 0, :], x[:, 0, :], ACT.Copy, scale=rstd[:, 0:1]).then_inc(xn0_ready, 1)
                for b in range(2):
                    act.wait_ge(turned, 4 * q + b + 1)
                    if b == 0:
                        act.wait_ge(mod_ready, 2 * (3 * q + 2))
                    for i in range(4):
                        k = 4 * b + i
                        act.activation(hT[:, k, 0:P], ps[:, YB + b, i * P:(i + 1) * P], ACT.Identity,
                                       scale=scl[:, q, k, 0:1], bias=mod[:, 3 * q, k, 0:1]).then_inc(hT0_ready, 1)

            def gate_copies(q):
                for i in range(4):
                    act.wait_ge(gateb_psum, 4 * q + i + 1)
                    if i == 0:
                        act.wait_ge(x_ready, q + 1)
                    act.activation(gate[:, i // 2, (i % 2) * 512:(i % 2 + 1) * 512], ps[:, i, :],
                                   ACT.Copy).then_inc(gateb_ready, 1)

            act.wait_ge(cst_in, 16)
            norm_turn(0)

            act.wait_ge(late_in, 48)
            act.wait_ge(gates_psum, 1)
            for w in range(2):
                act.activation(rt[:, w, :, :], ps[0:ROWS, MISC, w * T:(w + 1) * T], ACT.Identity,
                               bias=rc[:, w:w + 1]).then_inc(gate_raw, 1)
            act.wait_ge(gate_abs, 1)
            link(act.activation(rt[:, 5, :, :], rt[:, 4, :, :], ACT.Exp))
            act.activation(rt[:, 6, :, :], rt[:, 5, :, :], ACT.Ln, bias=cst[0:ROWS, C_ONE:C_ONE + 1]).then_inc(gate_ln, 1)
            act.wait_ge(gate_M, 1)
            act.activation(row[:, 2:4, :], rt[:, 4, :, :], ACT.Exp, scale=-1.0).then_inc(gate_exps, 1)
            act.activation(row[:, 4, :], row[:, 7, :], ACT.Exp, scale=-1.0, bias=rc[:, 2:3]).then_inc(gate_exps, 1)
            act.activation(row[:, 5, :], row[:, 0, :], ACT.Exp, bias=small[0:ROWS, 0:1]).then_inc(gate_exps, 1)

            def silu_exp(s):
                act.wait_ge(conv_done, s + 1)
                if s >= 2:
                    act.wait_ge(qk_done, s - 1)
                act.activation(eq[:, s % 2, :, :], ca[:, s % 2, :, :], ACT.Tanh, scale=0.5).then_inc(qk_exp, 1)

            for s in range(N_IN):
                b = UB + s % 2
                act.wait_ge(stage_used, ST_IN + s + 1)
                if s < HEADS:
                    if s == 0:
                        act.wait_ge(memsets, 3)
                    if s >= 2:
                        act.wait_ge(conv_done, s - 1)
                    act.activation(pad[:, s % 2, 0, :, 2:P + 2], ps[:, b, 0:T].rearrange("p (g t) -> p g t", g=G), ACT.Copy)
                    act.activation(pad[:, s % 2, 1, :, 2:P + 2], ps[:, b, T:2 * T].rearrange("p (g t) -> p g t", g=G),
                                   ACT.Copy).then_inc(proj_out, 1)
                elif s < 2 * HEADS:
                    act.activation(vaug[:, :, s - HEADS, 0:DV], ps[:, b, :].rearrange("p (g v) -> p g v", g=G),
                                   ACT.Copy).then_inc(proj_out, 1)
                else:
                    i = 2 * (s - 2 * HEADS)
                    act.activation(so[:, i:i + 2, :], ps[:, b, :].rearrange("p (c t) -> p c t", c=2), ACT.Tanh,
                                   scale=0.5).then_inc(proj_out, 1)
                if 1 <= s <= HEADS:
                    silu_exp(s - 1)

            def decay_scores(it):
                h, g = it // 2, it % 2
                act.wait_ge(tmp_ready, it + 1)
                if it == 0:
                    act.wait_ge(cols_ready, 1)
                for d in range(DIR):
                    r = 32 * d + h
                    ins = act.activation(pe_[:, it % 2, d, :], tmp[:, it % 2, d, :], ACT.Exp, scale=-1.0,
                                         bias=col[:, g, r:r + 1])
                ins.then_inc(p_ready, 1)

            decay_scores(0)
            for it in range(ITS):
                h, g = it // 2, it % 2
                if it + 1 < ITS:
                    decay_scores(it + 1)
                act.wait_ge(num_done, it + 1)
                if g == 0:
                    if h >= 2:
                        act.wait_ge(c_stored[h % 2], 16 * (h // 2))
                    act.activation(stc[:, h % 2, :, :], ps[:, QB:QB + 2, 0:DVA], ACT.Copy).then_inc(qc_used, 1)
                    act.wait_ge(qc_used, it + 1)
                    act.dma_start(c_out[h], stc[:, h % 2, :, :]).then_inc(c_stored[h % 2], 16)
                else:
                    if it >= 2:
                        act.wait_ge(num_used, it)
                    for d in range(DIR):
                        r = 32 * d + h
                        ins = act.activation(qcs[:, d, :], ps[:, QB + d, 0:DVA], ACT.Copy, scale=kscale[:, 0, r:r + 1])
                    ins.then_inc(qc_used, 1)
                act.wait_ge(num_used, it + 1)
                act.activation(hsq, hs, ACT.Square, accum_out=small[:, 4:5]).then_inc(hs_squared, 1)
                act.wait_ge(hs_squared, it + 1)
            act.wait_ge(m_ready, 1)
            act.dma_start(m_out, small[0:ROWS, 1:2]).then_inc(m_stored, 16)
            gate_copies(0)
            norm_turn(1)
            gate_copies(1)

            def hidden_tanh(fc, c, n):
                act.wait_ge(u_done, fc + 1)
                act.activation(fe[:, c % 2, 0:n], ps[:, UB + c % 2, 0:n], ACT.Tanh, scale=0.5).then_inc(e_done, 1)

            with act.Fori(0, FC // 2) as i:
                for c in range(2):
                    hidden_tanh(i * 2 + c, c, T)
            norm_turn(2)
            gate_copies(2)

            for s in range(N_PW1):
                act.wait_ge(stage_used, pw1_stage(s) + 1)
                act.activation(fe[:, s % 2, :], ps[:, UB + s % 2, T:2 * T], ACT.Tanh, scale=0.5).then_inc(glu_exp, 1)
                if s >= 1:
                    act.wait_ge(cv_ready, s)
                    if s >= 3:
                        act.wait_ge(ssq_done, s - 2)
                    act.activation(sqb[:, (s - 1) % 2, :], cv[:, s - 1, :], ACT.Square).then_inc(sq_ready, 1)
            act.wait_ge(cv_ready, N_PW1)
            act.wait_ge(ssq_done, N_PW1 - 2)
            act.activation(sqb[:, (N_PW1 - 1) % 2, :], cv[:, N_PW1 - 1, :], ACT.Square).then_inc(sq_ready, 1)
            act.wait_ge(ssq_done, N_PW1)
            link(act.activation(rb, ps[:, YB, 0:T], ACT.Ln, scale=1.0 / D, bias=eps))
            act.activation(rb, rb, ACT.Exp, scale=-0.5).then_inc(rb_ready, 1)
            act.wait_ge(z_ready, 1)
            for k in range(KD):
                ins = act.activation(ez[:, k, :], z[:, k, :], ACT.Tanh, scale=0.5)
            ins.then_inc(ez_ready, 1)
            norm_turn(3)
            gate_copies(3)
            act.wait_ge(route_gap, 1)
            act.activation(tk[:, 3, :], tk[:, 2, :], ACT.Exp).then_inc(route_exp, 1)
            for b in range(2):
                act.wait_ge(htok_psum, b + 1)
                act.activation(htok[:, 0, b * 512:(b + 1) * 512], ps[:, YB + b, :], ACT.Copy).then_inc(htok_ready0, 1)

            def evict_gather(i):
                act.wait_ge(gathered, i + 1)
                act.activation(hgT[:, 0:4, :], ps[:, 0, :].rearrange("p (k t) -> p k t", k=4), ACT.Copy
                               ).then_inc(hg0_ready, 1)
                act.wait_ge(picks_used, i + 1)
                if not isinstance(i, int):
                    act.wait_ge(scattered, i * 2)
                act.activation(back, ps[:, UB + 1, T:2 * T].rearrange("p (g t) -> p g t", g=G), ACT.Copy
                               ).then_inc(back_ready, 1)

            evict_gather(0)
            act.wait_ge(plan_ready, 1)
            items = act.value_load(plan[0:1, 0:1], min_val=EXPERTS, max_val=ITEMS)
            with act.Fori(0, items) as i:
                with act.Fori(0, FC // 2) as q:
                    for c in range(2):
                        hidden_tanh(i * FC + q * 2 + (FC + c), c, P)
                act.wait_ge(stage_used, i * FC + (ST_MOE + FC))
                act.activation(y_sb.rearrange("p (b n) -> p b n", b=2), ps[:, YB:YB + 2, :], ACT.Copy
                               ).then_inc(y_ready, 1)
                evict_gather(i + 1)
            act.wait_ge(og_ready, ITS)
            act.dma_start(so[:, 0:4, :].rearrange("p a b -> p (a b)"), norm_out).then_inc(no_in, 16)
            square_sum(4)
            act.activation(xn[:, 0, :], x[:, 0, :], ACT.Copy, scale=rstd[:, 0:1]).then_inc(xn0_ready, 1)
            act.wait_ge(fin_ready, 1)
            act.dma_start(y_out[:, 1, :], xn[:, 1, :]).then_inc(y_stored, 16)
            act.wait_ge(fin_ready, 2)
            act.dma_start(y_out[:, 0, :], xn[:, 0, :]).then_inc(y_stored, 16)
            act.wait_ge(y_stored, 32)
            act.wait_ge(m_stored, 16)
            for i in range(2):
                act.wait_ge(c_stored[i], 16 * (HEADS // 2))

        @block.vector
        def _(dve):
            n_chain = [0]

            def link(ins):
                n_chain[0] = n_chain[0] + 1
                ins.then_inc(dve_chain, 1)
                dve.wait_ge(dve_chain, n_chain[0])

            STT, TT, TS = dve.scalar_tensor_tensor, dve.tensor_tensor, dve.tensor_scalar

            def rsqrt(out, total, n, width, last=None):
                v, y, t = (root[:, i, 0:width] for i in range(3))
                bits = mybir.dt.int32
                link(TS(v, total, 1.0 / n, EPS, ALU.mult, ALU.add))
                link(TS(t.bitcast(bits), v.bitcast(bits), 1, None, ALU.logical_shift_right))
                link(TS(y.bitcast(bits), t.bitcast(bits), -1.0, float(0x5F3759DF), ALU.mult, ALU.add))
                for step in range(3):
                    link(TT(t, y, y, ALU.mult))
                    link(STT(t, t, -0.5, v, ALU.mult, ALU.mult))
                    end = STT(out if step == 2 else y, t, 1.5, y, ALU.add, ALU.mult)
                    if step < 2:
                        link(end)
                return end

            dve.wait_ge(cond_exp, 1)
            link(TS(cd[:, :], ce[:, :], 1.0, None, ALU.add))
            link(dve.reciprocal(ce[:, :], cd[:, :]))
            TT(silu_c[:, :], vec[:, V_COND:V_COND + KD * G], ce[:, :], ALU.mult).then_inc(cond_ready, 1)
            dve.wait_ge(x_in_s, 16)
            dve.wait_ge(pos_in, 16)
            TT(x[:, 1, :], x[:, 1, :], gate[:, 1, :], ALU.add).then_inc(x_ready, 1)

            def modulation(hv):
                v, half = hv // 2, (hv % 2) * KD // 2
                ks = slice(half, half + KD // 2)

                def spread(at):
                    return vec[:, at + half:at + half + KD // 2].unsqueeze(2).to_broadcast([P, KD // 2, G])

                dve.wait_ge(stage_used, ada_stage(2 * hv + 1) + 1)
                bias = spread(V_ADA + v * KD)
                src = ps[:, MODB + hv % 2, :].rearrange("p (k g r) -> p k g r", k=KD // 2, g=G)[:, :, :, 0]
                if v % 3 == 1:
                    q = v // 3
                    link(TT(mod[:, v, ks, :], src, bias, ALU.add))
                    gain = V_NMIX + (q // 2) * KD if q % 2 == 0 else V_NFFN + (q // 2) * KD
                    STT(scl[:, q, ks, :], mod[:, v, ks, :], 1.0, spread(gain), ALU.add, ALU.mult
                        ).then_inc(mod_ready, 1)
                else:
                    TT(mod[:, v, ks, :], src, bias, ALU.add).then_inc(mod_ready, 1)

            def square_sum(q):
                link(dve.tensor_tensor_reduce(out=xn[:, 1, :], in0=x[:, 1, :], in1=x[:, 1, :], scale=1.0, scalar=0.0,
                                              op0=ALU.mult, op1=ALU.add, accum_out=ss[:, 1:2]))
                dve.wait_ge(ss_ready, q + 1)
                rsqrt(rstd[:, :], ss[:, :], D, G).then_inc(rstd_ready, 1)
                dve.wait_ge(rstd_ready, q + 1)

            for hv in range(ADA_FIRST // 2):
                modulation(hv)

            def norm_turn(q):
                if q == 0:
                    dve.wait_ge(x_ready, 1)
                else:
                    dve.wait_ge(x_ready, q + 1)
                square_sum(q)
                TS(xn[:, 1, :], x[:, 1, :], rstd[:, 1:2], None, ALU.mult).then_inc(xn1_ready, 1)
                for b in range(2):
                    dve.wait_ge(turned, 4 * q + b + 3)
                    if q == 0 and b == 0:
                        dve.wait_ge(mod_ready, 4)
                    for i in range(4):
                        k = 4 * b + i
                        TS(hT[:, k, P:T], ps[:, YB + 2 + b, i * P:(i + 1) * P], scl[:, q, k, 1:2], mod[:, 3 * q, k, 1:2],
                           ALU.mult, ALU.add).then_inc(hT1_ready, 1)

            norm_turn(0)

            dve.wait_ge(gate_raw, 2)
            for w in range(2):
                dve.tensor_copy(rt[0:32, 2 + w, :, :], rt[0:32, w, :, :])
                link(dve.tensor_copy(rt[32:ROWS, 2 + w, :, :], rt[32:ROWS, w, :, ::-1]))
            STT(rt[:, 4, :, :], rt[:, 3, :, :], -1.0, rt[:, 3, :, :], ALU.mult, ALU.min).then_inc(gate_abs, 1)
            dve.wait_ge(gate_ln, 1)
            link(STT(rt[:, 7, :, :], rt[:, 3, :, :], 0.0, rt[:, 6, :, :], ALU.min, ALU.subtract))
            one = cst[0:ROWS, C_ONE:C_ONE + P]
            for g in range(G):
                link(dve.tensor_tensor_scan(rt[:, 3, g, :], one, rt[:, 7, g, :], 0.0, ALU.mult, ALU.add))
            link(TT(row[:, 0:2, :], rt[:, 2, :, :], rt[:, 3, :, :], ALU.subtract))
            link(dve.tensor_tensor_scan(row[:, 6, :], one, row[:, 0, :], 0.0, ALU.mult, ALU.max))
            link(dve.tensor_tensor_scan(row[:, 7, :], one, row[:, 1, :], rc[:, 2:3], ALU.mult, ALU.max))
            link(TS(small[0:ROWS, 0:1], row[:, 6, P - 1:P], -1.0, None, ALU.mult))
            TT(rt[:, 4, :, :], rt[:, 3, :, :], row[:, 6:8, :], ALU.add).then_inc(gate_M, 1)
            dve.wait_ge(gate_M, 1)
            dve.tensor_copy(small[0:ROWS, 1:2], rt[:, 4, 0, P - 1:P]).then_inc(m_ready, 1)
            dve.wait_ge(gate_exps, 3)
            dve.tensor_copy(nat[0:32, :, :], row[0:32, :, :]).then_inc(nat_ready, 1)
            dve.tensor_copy(nat[32:ROWS, :, :], row[32:ROWS, :, ::-1]).then_inc(nat_ready, 1)

            def conv_qk(s):
                dve.wait_ge(proj_out, s + 1)
                if s >= 2:
                    dve.wait_ge(qk_done, s - 1)
                for t in range(A_TAPS):
                    for j in range(2):
                        w = vec[:, V_ACONV + t * 2 * KD + 2 * s + j:V_ACONV + t * 2 * KD + 2 * s + j + 1]
                        out = ca[:, s % 2, j, :].rearrange("p (g t) -> p g t", g=G)
                        src = pad[:, s % 2, j, :, t:t + P]
                        ins = (TS(out, src, w, None, ALU.mult) if t == 0 else STT(out, src, w, out, ALU.mult, ALU.add))
                    if t < A_TAPS - 1:
                        link(ins)
                ins.then_inc(conv_done, 1)

            def silu_qk(s):
                dve.wait_ge(qk_exp, s + 1)
                STT(qkT[:, 2 * s:2 * s + 2, :], eq[:, s % 2, :, :], 1.0, ca[:, s % 2, :, :], ALU.add, ALU.mult
                    ).then_inc(qk_done, 1)

            for s in range(HEADS):
                conv_qk(s)
                if s >= 1:
                    silu_qk(s - 1)
            silu_qk(HEADS - 1)
            dve.wait_ge(cols_psum, 1)
            gate_cols = ps[:, MISC, 0:6 * ROWS].rearrange("p (q r) -> p q r", q=6)
            dve.tensor_copy(col, gate_cols)
            link(TS(kscale, gate_cols[:, 4:6, :], 0.5, None, ALU.mult))
            TS(kscale[:, 0, :], kscale[:, 0, :], Q_SCALE, None, ALU.mult).then_inc(cols_ready, 1)
            for s in range(2 * HEADS, N_IN):
                i = 2 * (s - 2 * HEADS)
                dve.wait_ge(proj_out, s + 1)
                TS(so[:, i:i + 2, :], so[:, i:i + 2, :], 1.0, 0.5, ALU.add, ALU.mult).then_inc(so_ready, 1)

            def masked(it):
                dve.wait_ge(front, it + 1)
                TT(tmp[:, it % 2, :, :], ps[:, UB + it % 2, P:3 * P].rearrange("p (d t) -> p d t", d=DIR), mask,
                   ALU.add).then_inc(tmp_ready, 1)

            def out_gate(it):
                h, g = it // 2, it % 2
                dve.wait_ge(hT_back, it + 1)
                for c in range(2):
                    f = 2 * h + c
                    o = so[:, f, g * P:(g + 1) * P]
                    ins = STT(o, ps[:, UB + it % 2, c * P:(c + 1) * P], vec[:, V_GN + f:V_GN + f + 1], o,
                              ALU.mult, ALU.mult)
                ins.then_inc(og_ready, 1)

            dve.wait_ge(so_ready, HEADS)
            masked(0)
            made = ADA_FIRST // 2
            for it in range(ITS):
                h, g = it // 2, it % 2
                b = UB + it % 2
                dve.wait_ge(p_ready, it + 1)
                if it >= 2:
                    dve.wait_ge(num_done, it - 1)
                if it == 0:
                    dve.wait_ge(qk_done, HEADS)
                for d in range(DIR):
                    ins = STT(sT[:, it % 2, d, :], pe_[:, it % 2, d, :], 0.25 * Q_SCALE, ps[:, b, 0:P], ALU.mult,
                              ALU.mult)
                ins.then_inc(s_ready, 1)
                if g == 0:
                    if it >= 1:
                        dve.wait_ge(num_done, it)
                    for d in range(DIR):
                        r = 32 * d + h
                        ins = TS(kw[:, d, :], ps[:, b, 3 * P:4 * P], kscale[:, 1, r:r + 1], None, ALU.mult)
                    ins.then_inc(kw_ready, 1)
                if it >= 1:
                    out_gate(it - 1)
                    while 2 * (made + 1) <= ada_through(it - 1):
                        modulation(made)
                        made += 1
                if it + 1 < ITS:
                    masked(it + 1)
                dve.wait_ge(num_done, it + 1)
                if g == 0:
                    src = ps[:, YB:YB + 2, :]
                    link(dve.tensor_copy(small[:, 8:10].unsqueeze(2), src[:, :, DV:DVA]))
                    den = small[:, 8:10]
                else:
                    src = nm
                    dve.wait_ge(qc_used, it + 1)
                    link(TT(nm, ps[:, YB:YB + 2, 0:DVA], qcs, ALU.add))
                    link(dve.tensor_copy(small[:, 8:10].unsqueeze(2), nm[:, :, DV:DVA]))
                    den = small[:, 8:10]
                link(STT(small[:, 10:12], den, -1.0, den, ALU.mult, ALU.max))
                link(TT(small[:, 12:14], small[:, 10:12], col[:, 2 + g, h:h + 33:32], ALU.max))
                link(dve.reciprocal(small[:, 14:16], small[:, 12:14]))
                link(TS(h0, src[:, 0, 0:DV], small[:, 14:15], None, ALU.mult))
                if it >= 1:
                    dve.wait_ge(hn_ready, it)
                STT(hs, src[:, 1, 0:DV], small[:, 15:16], h0, ALU.mult, ALU.add).then_inc(num_used, 1)
                dve.wait_ge(hs_squared, it + 1)
                link(rsqrt(small[:, 6:7], small[:, 4:5], DV, 1))
                if it >= 1:
                    dve.wait_ge(hT_back, it)
                TS(hn, hs, small[:, 6:7], None, ALU.mult).then_inc(hn_ready, 1)
            out_gate(ITS - 1)
            while 2 * (made + 1) <= ADA_FIRST + ADA_MID:
                modulation(made)
                made += 1

            def residual(q, last_stage, scale=1.0):
                dve.wait_ge(stage_used, last_stage)
                dve.wait_ge(gateb_ready, 4 * q + 4)
                gv = gate_b[:, 0:G * D].rearrange("p (b n) -> p b n", b=4)
                for b in range(4):
                    ins = STT(gv[:, b, :], gv[:, b, :], scale, ps[:, YB + b, :], ALU.mult, ALU.mult)
                link(ins)
                TT(x[:, :, :], x[:, :, :], gate, ALU.add).then_inc(x_ready, 1)

            residual(0, ST_OUT + N_OUT)
            norm_turn(1)

            def hidden(fc, c, n):
                dve.wait_ge(e_done, fc + 1)
                link(STT(ft[:, c % 2, 0:n], fe[:, c % 2, 0:n], 1.0, ps[:, UB + c % 2, 0:n], ALU.add, ALU.mult))
                STT(fact[:, c % 2, 0:n], ft[:, c % 2, 0:n], 0.5, ps[:, UB + c % 2, n:2 * n], ALU.mult, ALU.mult
                    ).then_inc(act_done, 1)

            LINKS = 1
            start = n_chain[0]
            with dve.Fori(0, FC // 2) as i:
                for c in range(2):
                    n_chain[0] = i * (2 * LINKS) + (start + c * LINKS)
                    hidden(i * 2 + c, c, T)
            n_chain[0] = start + FC * LINKS
            residual(1, ST_FF + FC)
            norm_turn(2)

            dve.wait_ge(memsets, 4)
            for i in range(2):
                dve.wait_ge(c_stored[i], 16 * (HEADS // 2))
            for s in range(N_PW1):
                dve.wait_ge(glu_exp, s + 1)
                link(TS(fd, fe[:, s % 2, :], 1.0, 0.5, ALU.add, ALU.mult))
                TT(pad31[:, s, :, 15:15 + P], ps[:, UB + s % 2, 0:T].rearrange("p (g t) -> p g t", g=G),
                   fd.rearrange("p (g t) -> p g t", g=G), ALU.mult).then_inc(glu_done, 1)
                dve.wait_ge(glu_done, s + 1)
                out = cv[:, s, :].rearrange("p (g t) -> p g t", g=G)
                for t in range(B_TAPS):
                    w = vec[:, V_BCONV + t * KD + s:V_BCONV + t * KD + s + 1]
                    src = pad31[:, s, :, t:t + P]
                    if t == 0:
                        link(TS(out, src, w, vec[:, V_BDW + s:V_BDW + s + 1], ALU.mult, ALU.add))
                    elif t < B_TAPS - 1:
                        link(STT(out, src, w, out, ALU.mult, ALU.add))
                    else:
                        STT(out, src, w, out, ALU.mult, ALU.add).then_inc(cv_ready, 1)
                while 2 * (made + 1) <= ada_beside(s):
                    modulation(made)
                    made += 1
            dve.wait_ge(rb_ready, 1)
            for k in range(KD):
                ins = STT(z[:, k, :], cv[:, k, :], vec[:, V_BNORM + k:V_BNORM + k + 1], rb, ALU.mult, ALU.mult)
            ins.then_inc(z_ready, 1)
            dve.wait_ge(ez_ready, 1)
            STT(z, ez, 1.0, z, ALU.add, ALU.mult).then_inc(zs_ready, 1)
            residual(2, ST_PW2 + N_PW2, 0.5)
            norm_turn(3)

            def bc(a):
                return a.unsqueeze(2).to_broadcast([P, G, EXPERTS])

            dve.wait_ge(route_psum, 1)
            link(dve.tensor_copy(lg, ps[:, MISC, 0:G * EXPERTS].rearrange("p (g e) -> p g e", g=G)))
            cur = lg
            for j in range(2):
                link(dve.tensor_reduce(tk[:, j, :], cur, X, ALU.max))
                link(TT(key, cur, bc(tk[:, j, :]), ALU.is_equal))
                link(TT(key, key, desc, ALU.mult))
                link(dve.tensor_reduce(tk[:, 4 + j, :], key, X, ALU.max))
                link(TT(oh[:, j, :, :], desc, bc(tk[:, 4 + j, :]), ALU.is_equal))
                if j == 0:
                    link(STT(l2, oh[:, 0, :, :], -3e38, lg, ALU.mult, ALU.add))
                    cur = l2
            TT(sel, oh[:, 0, :, :], oh[:, 1, :, :], ALU.add).then_inc(sel_ready, 1)
            TT(tk[:, 2, :], tk[:, 1, :], tk[:, 0, :], ALU.subtract).then_inc(route_gap, 1)
            for b in range(2):
                dve.wait_ge(htok_psum, b + 3)
                dve.tensor_copy(htok[:, 1, b * 512:(b + 1) * 512], ps[:, YB + 2 + b, :]).then_inc(htok_ready1, 1)
            dve.wait_ge(route_exp, 1)
            link(TS(tk[:, 6, :], tk[:, 3, :], 1.0, None, ALU.add))
            link(dve.reciprocal(tk[:, 7, :], tk[:, 6, :]))
            link(TT(tk[:, 8, :], tk[:, 7, :], tk[:, 3, :], ALU.mult))
            link(TT(oh[:, 0, :, :], oh[:, 0, :, :], bc(tk[:, 7, :]), ALU.mult))
            link(TT(oh[:, 1, :, :], oh[:, 1, :, :], bc(tk[:, 8, :]), ALU.mult))
            own = item_comb[:, :, 0:EXPERTS]
            link(TT(own, oh[:, 0, :, :], oh[:, 1, :, :], ALU.add))
            dve.wait_ge(pos_psum, 1)
            slots = item_pos[:, :, 0:EXPERTS]
            link(TT(key, ps[:, MISC, 0:G * EXPERTS].rearrange("p (g e) -> p g e", g=G), sel, ALU.mult))
            link(STT(slots, sel, -1.0, key, ALU.add, ALU.add))

            def make_picks(i):
                for g in range(G):
                    p = item_pos[:, g, bass.ds(i, 1)] if not isinstance(i, int) else item_pos[:, g, i:i + 1]
                    w = item_comb[:, g, bass.ds(i, 1)] if not isinstance(i, int) else item_comb[:, g, i:i + 1]
                    TS(pick[:, g, :], iota, p, None, ALU.is_equal)
                    ins = TS(pick_w[:, g, :], iota, p, w, ALU.is_equal, ALU.mult)
                ins.then_inc(pick_ready, 1)

            make_picks(0)
            count, is_over, rank, order = (over[:, n, :] for n in range(4))
            link(dve.tensor_copy(count, ps[:, MISC, G * EXPERTS:(G + 1) * EXPERTS]))
            link(TS(is_over, count, float(P), None, ALU.is_gt))
            link(dve.tensor_tensor_scan(rank, cst[:, C_ONE:C_ONE + EXPERTS], is_over, 0.0, ALU.mult, ALU.add))
            link(TT(order, is_over, rank, ALU.mult))
            for k in range(OVER + 1):
                i = EXPERTS + k
                link(TS(hit, order, float(k + 1), None, ALU.is_equal))
                link(dve.tensor_reduce(rsum[:, 0, 0:1], hit, X, ALU.add))
                both = hit.unsqueeze(1).to_broadcast([P, G, EXPERTS])
                link(STT(prod, slots, -float(P), both, ALU.add, ALU.mult))
                link(dve.tensor_reduce(rsum[:, 1, :], prod, X, ALU.add))
                link(TS(item_pos[:, :, i], rsum[:, 1, :], rsum[:, 0, 0:1], -1.0, ALU.add, ALU.add))
                link(TT(prod, own, both, ALU.mult))
                link(dve.tensor_reduce(item_comb[:, :, i], prod, X, ALU.add))
                if k < OVER:
                    link(TT(hit, hit, desc[:, 0, :], ALU.mult))
                    link(dve.tensor_reduce(rsum[:, 2, 0:1], hit, X, ALU.add))
                    link(STT(plan_f[:, 2 + k:3 + k], rsum[:, 0, 0:1], float(EXPERTS), rsum[:, 2, 0:1], ALU.mult,
                             ALU.subtract))
            dve.memset(plan_f[:, 1:2], float(EXPERTS - 1))
            dve.memset(plan_f[:, 5:7], 0.0)
            link(TS(plan_f[:, 0:1], rank[:, EXPERTS - 1:EXPERTS], float(EXPERTS), None, ALU.add))
            link(TS(plan_f[:, 7:8], rank[:, EXPERTS - 1:EXPERTS], 1.0, None, ALU.add))
            dve.tensor_copy(plan[0:1, :], plan_f[0:1, :]).then_inc(plan_ready, 1)

            def evict_gather(i):
                dve.wait_ge(gathered, i + 1)
                dve.tensor_copy(hgT[:, 4:8, :], ps[:, 1, :].rearrange("p (k t) -> p k t", k=4)).then_inc(hg1_ready, 1)

            evict_gather(0)
            dve.wait_ge(plan_ready, 1)
            items = dve.value_load(plan[0:1, 0:1], min_val=EXPERTS, max_val=ITEMS)
            start = n_chain[0]
            with dve.Fori(0, items) as i:
                dve.wait_ge(picks_used, i + 1)
                make_picks(i + 1)
                with dve.Fori(0, FC // 2) as q:
                    for c in range(2):
                        n_chain[0] = i * (FC * LINKS) + q * (2 * LINKS) + (start + c * LINKS)
                        hidden(i * FC + q * 2 + (FC + c), c, P)
                evict_gather(i + 1)
                for g, free in ((0, acc0_free), (1, acc1_free)):
                    dve.wait_ge(scattered, i * 2 + (g + 1))
                    dve.wait_ge(free, i + 1)
                    a = acc[:, g, :].rearrange("p (b n) -> p b n", b=2)
                    TT(a, ps[:, QB - 2 * g:QB - 2 * g + 2, :], a, ALU.add).then_inc(free, 1)
            n_chain[0] = items * (FC * LINKS) + start
            dve.wait_ge(acc0_free, items + 1)
            dve.wait_ge(acc1_free, items + 1)
            dve.wait_ge(gateb_ready, 16)
            link(TT(acc, acc, gate, ALU.mult))
            TT(x[:, :, :], x[:, :, :], acc, ALU.add).then_inc(x_ready, 1)
            dve.wait_ge(no_in, 16)
            dve.wait_ge(x_ready, 5)
            square_sum(4)
            no = so[:, 0:4, :].rearrange("p a b -> p (a b)")
            STT(xn[:, 1, :], x[:, 1, :], rstd[:, 1:2], no, ALU.mult, ALU.mult).then_inc(fin_ready, 1)
            dve.wait_ge(xn0_ready, 5)
            TT(xn[:, 0, :], xn[:, 0, :], no, ALU.mult).then_inc(fin_ready, 1)

        @block.tensor
        def _(pe):
            def arrived(n, j=None):
                j = n if j is None else j
                sl = slot(j)
                turn = n // SLOTS if isinstance(n, int) else None
                assert turn is not None
                pe.wait_ge(loaded[sl], 16 * (turn + 1))
                return ring[:, sl, :]

            pe.wait_ge(cst_in, 16)

            def ada(a, n):
                w = arrived(n)
                hv = a // 2
                if a % 2 == 0 and hv >= 2:
                    pe.wait_ge(mod_ready, hv - 1)
                    if hv == ADA_FIRST // 2 + 1:
                        pe.wait_ge(cols_ready, 1)
                for j in range(2):
                    c = (2 * (a % 2) + j) * P
                    for k in range(KD):
                        ins = pe.matmul(ps[:, MODB + hv % 2, c:c + P], w[:, k * 256 + j * P:k * 256 + (j + 1) * P],
                                        silu_c[:, k * G:(k + 1) * G].unsqueeze(2).to_broadcast([P, G, P // G]), start=(k == 0), stop=(k == KD - 1))
                ins.then_inc(stage_used, 1)

            def norm_turn(q):
                for g in range(G):
                    pe.wait_ge([xn0_ready, xn1_ready][g], q + 1)
                    for b in range(2):
                        for i in range(4):
                            k = 4 * b + i
                            ins = pe.transpose(ps[:, YB + 2 * g + b, i * P:(i + 1) * P], xn[:, g, k * P:(k + 1) * P],
                                               ident)
                        ins.then_inc(turned, 1)
                pe.wait_ge(hT0_ready, 8 * q + 8)
                pe.wait_ge(hT1_ready, 8 * q + 8)

            def tokens(f, k, g):
                return f[:, k, g * P:(g + 1) * P]

            pe.wait_ge(cond_ready, 1)
            for a in range(ADA_FIRST):
                ada(a, ada_stage(a))
            norm_turn(0)
            pe.wait_ge(late_in, 48)
            for w in range(2):
                for k in range(KD):
                    ins = pe.matmul(ps[0:ROWS, MISC, w * T:(w + 1) * T], wg[:, k, w, :], hT[:, k, :],
                                    start=(k == 0), stop=(k == KD - 1))
            ins.then_inc(gates_psum, 1)

            for s in range(N_IN):
                n = ST_IN + s
                w = arrived(n)
                b = UB + s % 2
                if s >= 2:
                    pe.wait_ge(proj_out, s - 1)
                for j in range(2):
                    for k in range(KD):
                        if HEADS <= s < 2 * HEADS:
                            ins = pe.matmul(ps[:, b, j * T:(j + 1) * T], tokens(hT, k, j), w[:, k * 256:(k + 1) * 256],
                                            start=(k == 0), stop=(k == KD - 1))
                        else:
                            ins = pe.matmul(ps[:, b, j * T:(j + 1) * T], w[:, k * 256 + j * P:k * 256 + (j + 1) * P],
                                            hT[:, k, :], start=(k == 0), stop=(k == KD - 1))
                ins.then_inc(stage_used, 1)
                if s == 2 * HEADS:
                    pe.wait_ge(nat_ready, 2)
                    for q in range(6):
                        ins = pe.transpose(ps[:, MISC, q * ROWS:(q + 1) * ROWS], nat[:, q, :], ident[0:ROWS, 0:ROWS])
                    ins.then_inc(cols_psum, 1)

            def front_step(it):
                h, g = it // 2, it % 2
                b = UB + it % 2
                if it >= 2:
                    pe.wait_ge(s_ready, it - 1)
                    pe.wait_ge(kw_ready, it // 2)
                    pe.wait_ge(og_ready, it - 1)
                pe.matmul(ps[:, b, 0:P], tokens(qkT, HEADS + h, g), tokens(qkT, h, g), start=True, stop=True)
                for d in range(DIR):
                    r = 32 * d + h
                    ins = pe.matmul(ps[:, b, (1 + d) * P:(2 + d) * P], ident[0:ROWS, r:r + 1].to_broadcast([ROWS, P]),
                                    nat[:, 6 + g, :], start=True, stop=True)
                if g == 0:
                    ins = pe.transpose(ps[:, b, 3 * P:4 * P], tokens(qkT, HEADS + h, 0), ident)
                ins.then_inc(front, 1)

            def turn_head(it):
                pe.wait_ge(hn_ready, it + 1)
                for c in range(2):
                    ins = pe.transpose(ps[:, UB + it % 2, c * P:(c + 1) * P], hn[:, c * P:(c + 1) * P], ident)
                ins.then_inc(hT_back, 1)

            pe.wait_ge(qk_done, HEADS)
            pe.wait_ge(proj_out, N_IN)
            front_step(0)
            a = ADA_FIRST
            for it in range(ITS):
                h, g = it // 2, it % 2
                pe.wait_ge(s_ready, it + 1)
                if g == 0:
                    pe.wait_ge(kw_ready, h + 1)
                else:
                    pe.wait_ge(c0_in[h % 2], 16 * (h // 2 + 1))
                if it >= 1:
                    pe.wait_ge(qc_used, it)
                    pe.wait_ge(num_used, it)
                for d in range(DIR):
                    if g == 0:
                        pe.matmul(ps[:, QB + d, 0:DVA], kw[:, d, :], vaug[:, 0, h, :], start=True, stop=True)
                    else:
                        pe.matmul(ps[:, QB + d, 0:DVA], tokens(qkT, h, 1), c0b[:, h % 2, d, :], start=True, stop=True)
                for d in range(DIR):
                    ins = pe.matmul(ps[:, YB + d, 0:DVA], sT[:, it % 2, d, :], vaug[:, g, h, :], start=True, stop=True)
                ins.then_inc(num_done, 1)
                if it + 1 < ITS:
                    front_step(it + 1)
                while a < ada_through(it):
                    ada(a, ada_stage(a))
                    a += 1
                turn_head(it)

            def gate_rows(q):
                v = 3 * q + 2
                pe.wait_ge(mod_ready, 2 * (v + 1))
                if q == 0:
                    pe.wait_ge(mod_ready, (ADA_FIRST + ADA_MID) // 2)
                for i in range(4):
                    for c in range(4):
                        k = 4 * (i % 2) + c
                        ins = pe.matmul(ps[:, i, c * P:(c + 1) * P],
                                        mod[:, v, k, i // 2:i // 2 + 1].to_broadcast([P, P]), ident,
                                        start=True, stop=True)
                    ins.then_inc(gateb_psum, 1)

            def down(src, base, stages):
                for s in range(stages):
                    w = arrived(base + s)
                    for kk in range(2):
                        k = 2 * s + kk
                        for g in range(G):
                            for hf in range(2):
                                ins = pe.matmul(ps[:, YB + 2 * g + hf, :], tokens(src, k, g),
                                                w[:, kk * D + hf * 512:kk * D + (hf + 1) * 512],
                                                start=(k == 0), stop=(k == 2 * stages - 1))
                    ins.then_inc(stage_used, 1)

            pe.wait_ge(og_ready, ITS)
            gate_rows(0)
            pe.wait_ge(num_used, ITS)
            pe.wait_ge(qc_used, ITS)
            pe.wait_ge(gateb_ready, 4)
            down(so, ST_OUT, N_OUT)
            gate_rows(1)
            norm_turn(1)
            pe.wait_ge(gateb_ready, 8)

            def ffn(src, nt, first, turn0, fc0, item=None):
                def up_part(c):
                    sl = slot(first + c)
                    pe.wait_ge(loaded[sl], turn0 + 16 * ((first + c) // SLOTS - first // SLOTS))
                    w = ring[:, sl, :]
                    if item is not None or c >= 2:
                        pe.wait_ge(act_done, fc0 + (c - 1))
                    if item is not None and c == 1:
                        pe.wait_ge(back_ready, item + 1)
                    for j in range(2):
                        for k in range(KD):
                            ins = pe.matmul(ps[:, UB + c % 2, j * nt:(j + 1) * nt],
                                            w[:, (j * KD + k) * P:(j * KD + k + 1) * P], src[:, k, :],
                                            start=(k == 0), stop=(k == KD - 1))
                    ins.then_inc(u_done, 1)

                def down_part(c):
                    w = ring[:, slot(first + c), :]
                    pe.wait_ge(act_done, fc0 + (c + 1))
                    if c == 0 and item is not None:
                        pe.wait_ge(acc1_free, item + 1)
                    for g in range(nt // P):
                        for hf in range(2):
                            ins = pe.matmul(ps[:, YB + 2 * g + hf, :], fact[:, c % 2, g * P:(g + 1) * P],
                                            w[:, 2 * D + hf * 512:2 * D + (hf + 1) * 512],
                                            start=(c == 0), stop=(c == FC - 1))
                    ins.then_inc(stage_used, 1)

                up_part(0)
                for c in range(1, FC):
                    up_part(c)
                    down_part(c - 1)
                down_part(FC - 1)

            ffn(hT, T, ST_FF, 16 * (ST_FF // SLOTS + 1), 0)
            gate_rows(2)
            norm_turn(2)
            pe.wait_ge(gateb_ready, 12)

            def square_sum(s):
                pe.wait_ge(sq_ready, s + 1)
                pe.matmul(ps[:, YB, 0:T], ones, sqb[:, s % 2, :], start=(s == 0), stop=(s == N_PW1 - 1)
                          ).then_inc(ssq_done, 1)

            for s in range(N_PW1):
                w = arrived(pw1_stage(s))
                if s >= 2:
                    pe.wait_ge(glu_done, s - 1)
                for j in range(2):
                    for k in range(KD):
                        ins = pe.matmul(ps[:, UB + s % 2, j * T:(j + 1) * T], w[:, (j * KD + k) * P:(j * KD + k + 1) * P],
                                        hT[:, k, :], start=(k == 0), stop=(k == KD - 1))
                ins.then_inc(stage_used, 1)
                while a < ada_beside(s):
                    ada(a, ada_stage(a))
                    a += 1
                if s >= 2:
                    square_sum(s - 2)
            square_sum(N_PW1 - 2)
            square_sum(N_PW1 - 1)
            pe.wait_ge(zs_ready, 1)
            down(z, ST_PW2, N_PW2)
            gate_rows(3)
            norm_turn(3)
            pe.wait_ge(gateb_ready, 14)
            for g in range(G):
                for k in range(KD):
                    ins = pe.matmul(ps[:, MISC, g * EXPERTS:(g + 1) * EXPERTS], tokens(hT, k, g), wr[:, k, :],
                                    start=(k == 0), stop=(k == KD - 1))
            ins.then_inc(route_psum, 1)
            pe.wait_ge(gateb_ready, 16)
            for g in range(G):
                for b in range(2):
                    for i in range(4):
                        ins = pe.transpose(ps[:, YB + 2 * g + b, i * P:(i + 1) * P], tokens(hT, 4 * b + i, g), ident)
                    ins.then_inc(htok_psum, 1)
            pe.wait_ge(sel_ready, 1)
            for g in range(G):
                pe.matmul(ps[:, MISC, g * EXPERTS:(g + 1) * EXPERTS], tri, sel[:, g, :], start=True, stop=(g == 0))
                if g == 1:
                    pe.matmul(ps[:, MISC, g * EXPERTS:(g + 1) * EXPERTS], ones, sel[:, 0, :], start=False, stop=True)
            for g in range(G):
                ins = pe.matmul(ps[:, MISC, G * EXPERTS:(G + 1) * EXPERTS], ones, sel[:, g, :], start=(g == 0),
                                stop=(g == G - 1))
            ins.then_inc(pos_psum, 1)

            def gather(i):
                pe.wait_ge(pick_ready, i + 1)
                for k in range(KD):
                    for g in range(G):
                        ins = pe.matmul(ps[:, k // 4, (k % 4) * P:(k % 4 + 1) * P], htok[:, g, k * P:(k + 1) * P],
                                        pick[:, g, :], start=(g == 0), stop=(g == G - 1))
                ins.then_inc(gathered, 1)
                for g in range(G):
                    ins = pe.transpose(ps[:, UB + 1, T + g * P:T + (g + 1) * P], pick_w[:, g, :], ident)
                ins.then_inc(picks_used, 1)

            pe.wait_ge(htok_ready0, 2)
            pe.wait_ge(htok_ready1, 2)
            pe.wait_ge(plan_ready, 1)
            gather(0)
            items = pe.value_load(plan[0:1, 0:1], min_val=EXPERTS, max_val=ITEMS)
            with pe.Fori(0, items) as i:
                pe.wait_ge(hg0_ready, i + 1)
                pe.wait_ge(hg1_ready, i + 1)
                ffn(hgT, P, ST_MOE, i * (16 * FC // SLOTS) + 16 * (ST_MOE // SLOTS + 1), i * FC + FC, i)
                gather(i + 1)
                pe.wait_ge(y_ready, i + 1)
                pe.wait_ge(acc0_free, i + 1)
                for g in range(G):
                    for hf in range(2):
                        ins = pe.matmul(ps[:, QB - 2 * g + hf, :], back[:, g, :], y_sb[:, hf * 512:(hf + 1) * 512],
                                        start=True, stop=True)
                    ins.then_inc(scattered, 1)


_INPUTS = ("vecs", "consts", "rowc", "x_in", "pos", "w_gate", "w_router", "mix", "ff", "moe", "c0", "norm_out")
_OUTPUTS = (("y_out", (P, G, D)), ("c_out", (HEADS, P, DIR, DVA)), ("m_out", (ROWS, 1)))


def _constants():
    cst = np.zeros((P, C_ALL), np.float32)
    cst[:, C_ID:C_ID + P] = np.eye(P)
    cst[:, C_ONE:C_ONE + P] = 1.0
    j, t = np.arange(P)[:, None], np.arange(P)[None, :]
    cst[:, C_MASK:C_MASK + P] = np.where(j <= t, 0.0, BIG)
    cst[:, C_MASK + P:C_MASK + 2 * P] = np.where(j >= t, 0.0, BIG)
    cst[:, C_DESC:C_DESC + G * EXPERTS] = np.tile(np.arange(EXPERTS, 0, -1), G)
    cst[:, C_EPS] = EPS
    cst[:, C_TRI:C_TRI + P] = np.where(j < t, 1.0, 0.0)
    cst[:, C_IOTA:C_IOTA + P] = t
    grid_w = 64
    r = np.repeat(np.arange(P // grid_w, dtype=np.float32), grid_w)
    c = np.tile(np.arange(grid_w, dtype=np.float32), P // grid_w)
    quarter = D // 4
    freqs = (np.float32(10000.0) ** (-np.arange(quarter, dtype=np.float32) / quarter)).astype(np.float32)
    ar, ac = r[:, None] * freqs, c[:, None] * freqs
    pos = np.zeros((P, D), np.float32)
    pos[:, :] = np.concatenate([np.sin(ar), np.cos(ar), np.sin(ac), np.cos(ac)], axis=-1)
    return cst, pos


def kernel(**inputs):
    import concourse.bacc as bacc
    from concourse.bass_utils import run_bass_kernel_spmd

    a = {k: np.asarray(v) for k, v in inputs.items()}

    def chunks(v):
        return v.reshape(-1, P).T

    cond = np.stack([a["c_ctx"], a["c"][0]], axis=0).reshape(G, KD, P).transpose(2, 1, 0).reshape(P, KD * G)
    vecs = np.concatenate([chunks(a["b_ada"]), chunks(a["norm_mix"]), chunks(a["norm_ffn"]), chunks(a["a_gn"]),
                           chunks(a["b_b_dw"]), chunks(a["b_norm"]), chunks(a["a_w_conv"]), chunks(a["b_w_dw"]),
                           cond], axis=1)
    consts, pos = _constants()
    rowc = np.zeros((ROWS, 4), np.float32)
    w_gate = np.zeros((P, KD, 2, ROWS), np.float32)
    gw = a["a_w_in"][0][:, 6144:].reshape(KD, P, 4, HEADS).transpose(1, 0, 2, 3)
    for d in range(DIR):
        rowc[32 * d:32 * d + HEADS, 0] = a["a_b_gate"][0, 2 * d]
        rowc[32 * d:32 * d + HEADS, 1] = a["a_b_gate"][0, 2 * d + 1]
        rowc[32 * d:32 * d + HEADS, 2] = a["state_m"][0, 0, d]
        w_gate[:, :, 0, 32 * d:32 * d + HEADS] = gw[:, :, 2 * d]
        w_gate[:, :, 1, 32 * d:32 * d + HEADS] = gw[:, :, 2 * d + 1]

    def columns(w, width):
        n = w.shape[1] // width
        return w.reshape(KD, P, n, width).transpose(2, 1, 0, 3).reshape(n, P, KD * width)

    def rows_of(w, per):
        n = w.shape[0] // P // per
        return w.reshape(n, per, P, D).transpose(0, 2, 1, 3).reshape(n, P, per * D)

    ada = np.concatenate([columns(a["w_ada"][0], 256), columns(a["w_ada"][1], 256)])
    pw1 = a["b_w_pw1"][0]
    pw1 = np.concatenate([columns(pw1[:, :D], P), columns(pw1[:, D:], P)], axis=2)
    beside = [part for s in range(N_PW1) for part in (pw1[s:s + 1], ada[ada_beside(s - 1):ada_beside(s)])]
    mix = np.concatenate([ada[:ADA_FIRST], columns(a["a_w_in"][0][:, :6144], 256),
                          ada[ADA_FIRST:ADA_FIRST + ADA_MID], rows_of(a["a_w_out"][0], 2), *beside,
                          rows_of(a["b_w_pw2"][0], 2)])

    def swiglu(w1, w2):
        return np.concatenate([columns(w1[:, :FF], P), columns(w1[:, FF:], P), rows_of(w2, 1)], axis=2)

    ff = swiglu(a["ff_w1"][0], a["ff_w2"][0])
    moe = np.concatenate([swiglu(a["moe_w1"][0, e], a["moe_w2"][0, e]) for e in range(EXPERTS)])
    c0 = np.concatenate([a["state_C"][0, 0], a["state_n"][0, 0][..., None]], axis=-1).transpose(1, 2, 0, 3)
    arrays = dict(vecs=vecs, consts=consts, rowc=rowc,
                  x_in=np.stack([a["x_prompt"][0], a["x_sample"][0]], axis=1), pos=pos, w_gate=w_gate,
                  w_router=a["moe_router"][0].reshape(KD, P, EXPERTS).transpose(1, 0, 2), mix=mix, ff=ff, moe=moe,
                  c0=c0, norm_out=np.broadcast_to(a["norm_out"], (P, D)))
    arrays = {k: np.ascontiguousarray(v) for k, v in arrays.items()}

    nc = bacc.Bacc("TRN2", target_bir_lowering=False, num_devices=1)
    f32 = mybir.dt.float32
    args = [nc.dram_tensor(k, arrays[k].shape, f32, kind="ExternalInput").ap() for k in _INPUTS]
    args += [nc.dram_tensor(k, s, f32, kind="ExternalOutput").ap() for k, s in _OUTPUTS]
    mlstm_conformer_kernel(nc, *args)
    r = run_bass_kernel_spmd(nc, [arrays], core_ids=[0]).results[0]
    y, c, m = (np.asarray(r[k]) for k, _ in _OUTPUTS)
    state = c.transpose(2, 0, 1, 3)
    m2 = np.stack([m[32 * d:32 * d + HEADS, 0] for d in range(DIR)])
    return (np.ascontiguousarray(y[:, 0])[None], np.ascontiguousarray(y[:, 1])[None],
            np.ascontiguousarray(state[..., :DV])[None, None], np.ascontiguousarray(state[..., DV])[None, None],
            m2[None, None])
```

```python
import numpy as np
import concourse.bass as bass
from concourse import mybir
from contextlib import ExitStack

P = 128
D = 1024
KD = D // P
G = 2
T = G * P
HEADS = 8
DV = 256
DVA = DV + 1
DIR = 2
FF = 3584
FC = FF // P
EXPERTS = 8
A_TAPS, B_TAPS = 5, 31
EPS = 1e-6
WORK = 17040
Q_SCALE = float(P) ** -0.5
ROWS = 32 * (DIR - 1) + HEADS
BIG = 1e30

SLOTS = 7
STAGE = 3072
MIX = 2048
ADA_STAGES = 2 * 6 * D // 256
ADA_FIRST = 8
ST_IN = ADA_FIRST
N_IN = 24
ST_ADA = ST_IN + N_IN
ADA_LAST = 3 * 4
ADA_MID = ADA_STAGES - ADA_FIRST - ADA_LAST
ST_OUT = ST_ADA + ADA_MID
N_OUT = 8
ST_FF = ST_OUT + N_OUT
ST_PW1 = ST_FF + FC
N_PW1 = 8


def ada_beside(s):
    return ADA_FIRST + ADA_MID + ADA_LAST * (s + 1) // N_PW1


def pw1_stage(s):
    return ST_PW1 + s + (ada_beside(s - 1) - ADA_FIRST - ADA_MID)


ST_PW2 = ST_PW1 + N_PW1 + ADA_LAST
N_PW2 = 4
ST_MOE = ST_PW2 + N_PW2

ROW = 512
GROUPS = FF // ROW
GC = ROW // P
PER = STAGE // ROW
EXPERT_ROWS = []
for _q in range(GROUPS):
    EXPERT_ROWS += [("gate", _q, _k, 0) for _k in range(KD)] + [("up", _q, _k, 0) for _k in range(KD)]
    if _q:
        EXPERT_ROWS += [("down", _q - 1, _c, _h) for _c in range(GC) for _h in range(2)]
EXPERT_ROWS += [("down", GROUPS - 1, _c, _h) for _c in range(GC) for _h in range(2)]
assert len(EXPERT_ROWS) == FC * PER
UP_END = [EXPERT_ROWS.index(("up", _q, KD - 1, 0)) for _q in range(GROUPS)]
TURN_ROW = [UP_END[_q] + (8 if _q < GROUPS - 1 else 5) for _q in range(GROUPS)]
SCATTER_ROWS = [40, 46, 52, 58]
BACK_ROW = 66
GATHER_ROW = 156


CUT = 3
CUTS = len(EXPERT_ROWS) // CUT
W_BUFS = 4


def behind(row):
    return min(row // CUT + W_BUFS, CUTS)


ITS = G * HEADS

V_ADA = 0
V_NMIX = V_ADA + 2 * 6 * KD
V_NFFN = V_NMIX + 2 * KD
V_GN = V_NFFN + 2 * KD
V_BDW = V_GN + 2 * KD
V_BNORM = V_BDW + KD
V_ACONV = V_BNORM + KD
V_BCONV = V_ACONV + A_TAPS * 2 * KD
V_COND = V_BCONV + B_TAPS * KD
V_ALL = V_COND + KD * G
C_ID = 0
C_ONE = P
C_MASK = 2 * P
C_DESC = C_MASK + DIR * P
C_EPS = C_DESC + G * EXPERTS
C_TRI = C_EPS + 1
C_IOTA = C_TRI + P
C_ALL = C_IOTA + P

OVER = (2 * G * P - 1) // (P + 1)
ITEMS = EXPERTS + OVER
COLS = ITEMS + 1


def mlstm_conformer_kernel(nc, vecs, consts, rowc, x_in, pos, w_gate, w_router, mix, ff, moe, c0, norm_out,
                           y_out, c_out, m_out):
    f32 = mybir.dt.float32
    ALU = mybir.AluOpType
    ACT = mybir.ActivationFunctionType
    X = mybir.AxisListType.X

    ctx = ExitStack()
    with ctx:
        def sb(name, *shape):
            return ctx.enter_context(nc.sbuf_tensor(name, list(shape), f32))

        def sem(name):
            return ctx.enter_context(nc.semaphore(name))

        ring = sb("ring", P, SLOTS, STAGE)
        x = sb("x", P, G, D)
        xn = sb("xn", P, G, D)
        hT = sb("hT", P, KD, T)
        gate_b = sb("gate_b", P, G * D)
        so = sb("so", P, 2 * HEADS, T)
        vec = sb("vec", P, V_ALL)
        cst = sb("cst", P, C_ALL)
        rc = sb("rc", ROWS, 4)
        wg = sb("wg", P, KD, 2, ROWS)
        wr = sb("wr", P, KD, EXPERTS)
        silu_c = sb("silu_c", P, KD * G)
        ce = sb("ce", P, KD * G)
        cd = sb("cd", P, KD * G)
        mod = sb("mod", P, 12, KD, G)
        scl = sb("scl", P, 4, KD, G)
        ss = sb("ss", P, G)
        rstd = sb("rstd", P, G)
        lnv = sb("lnv", P, G)
        small = sb("small", P, 16)
        root = sb("root", P, 4, G)
        f32r = mybir.dt.float32r
        first = ExitStack()
        plan_f = sb("plan_f", P, 8)
        plan = ctx.enter_context(nc.sbuf_tensor("plan", [1, 8], mybir.dt.int32))
        work = first.enter_context(nc.sbuf_tensor("work", [P, WORK], f32))
        at = [0]

        def carve(*shape, rows=P):
            n = int(np.prod(shape))
            a = work[0:rows, at[0]:at[0] + n]
            at[0] += n
            assert at[0] <= WORK
            if len(shape) == 1:
                return a
            names = "abcd"[:len(shape)]
            return a.rearrange(f"p ({' '.join(names)}) -> p {' '.join(names)}",
                               **{k: v for k, v in zip(names, shape)})

        qkT = carve(2 * HEADS, T)
        vaug = carve(G, HEADS, DVA)
        c0b = carve(2, DIR, DVA)
        stc = carve(2, DIR, DVA)
        row = carve(8, P, rows=ROWS)
        nat = carve(8, P, rows=ROWS)
        col = carve(6, ROWS)
        kscale = carve(2, ROWS)
        kw = carve(DIR, P)
        qcs = carve(DIR, DVA)
        nm = carve(DIR, DVA)
        h0 = carve(DV)
        hs = carve(DV)
        hn = carve(DV)
        hsq = carve(DV)
        shared = at[0]
        tmp = carve(2, DIR, P)
        pe_ = carve(2, DIR, P)
        sT = carve(2, DIR, P)
        at[0] = shared
        ca = carve(2, 2, T)
        eq = carve(2, 2, T)
        rt = xn[0:ROWS, :, :].rearrange("p g d -> p (g d)").rearrange("p (n g t) -> p n g t", g=G, t=P)
        pad = gate_b[:, 0:2 * 2 * G * (P + A_TAPS - 1)].rearrange("p (b j g t) -> p b j g t", b=2, j=2, g=G)
        at[0] = 0
        fe = carve(2, T)
        fd = carve(T)
        ft = carve(2, T)
        fact = carve(2, T)
        pad31 = carve(KD, G, P + B_TAPS - 1)
        cv = carve(KD, T)
        z = carve(KD, T)
        ez = carve(KD, T)
        sqb = carve(2, T)
        rb = carve(T)
        assert at[0] <= WORK
        at[0] = 0
        work = so[:, :, :].rearrange("p c t -> p (c t)")
        acc = carve(G, D)
        y_sb = carve(D)
        pick = carve(G, P)
        pick_w = carve(G, P)
        back = carve(G, P)
        lg = carve(G, EXPERTS)
        l2 = carve(G, EXPERTS)
        oh = carve(2, G, EXPERTS)
        key = carve(G, EXPERTS)
        tk = carve(9, G)
        sel = carve(G, EXPERTS)
        item_pos = carve(G, COLS)
        item_comb = carve(G, COLS)
        over = carve(4, EXPERTS)
        hit = carve(EXPERTS)
        prod = carve(G, EXPERTS)
        rsum = carve(3, G)
        assert at[0] <= 2 * HEADS * T
        at[0] = 0
        work = hT[:, :, :].rearrange("p k t -> p (k t)")
        gain_out = work[:, 0:D]
        th = carve(ROW)
        sg = carve(ROW)
        hid = carve(ROW)
        gate = gate_b[:, 0:G * D].rearrange("p (g d) -> p g d", g=G)
        ident = cst[:, C_ID:C_ID + P]
        ones = cst[:, C_ONE:C_ONE + P]
        mask = cst[:, C_MASK:C_MASK + DIR * P].rearrange("p (d t) -> p d t", d=DIR)
        desc = cst[:, C_DESC:C_DESC + G * EXPERTS].rearrange("p (g e) -> p g e", g=G)
        eps = cst[:, C_EPS:C_EPS + 1]
        tri = cst[:, C_TRI:C_TRI + P]
        iota = cst[:, C_IOTA:C_IOTA + P]
        htok = xn
        first.close()

        def part(name, *shape):
            return ctx.enter_context(nc.sbuf_tensor(name, list(shape), f32r))

        w_hi, w_lo = part("w_hi", P, W_BUFS, CUT * ROW), part("w_lo", P, W_BUFS, CUT * ROW)
        hg_hi, hg_lo = part("hg_hi", P, KD, P), part("hg_lo", P, KD, P)
        hid_hi, hid_lo = part("hid_hi", P, 2, ROW), part("hid_lo", P, 2, ROW)

        ps = ctx.enter_context(nc.psum_tensor("ps", [P, 8, 512], f32))
        MODB, MISC, UB, YB, QB = 0, 1, 2, 4, 6

        vec_in, cst_in, x_in_s, pos_in, late_in = sem("vec_in"), sem("cst_in"), sem("x_in_s"), sem("pos_in"), sem("late_in")
        no_in = sem("no_in")
        loaded = [sem(f"loaded{i}") for i in range(SLOTS)]
        stage_used = sem("stage_used")
        cond_exp, cond_ready = sem("cond_exp"), sem("cond_ready")
        dve_chain, act_chain = sem("dve_chain"), sem("act_chain")
        x_ready, ss_ready, rstd_ready, hs_squared = sem("x_ready"), sem("ss_ready"), sem("rstd_ready"), sem("hs_squared")
        xn0_ready, xn1_ready, turned = sem("xn0_ready"), sem("xn1_ready"), sem("turned")
        hT0_ready, hT1_ready = sem("hT0_ready"), sem("hT1_ready")
        mod_ready = sem("mod_ready")
        gates_psum, gate_raw, gate_abs, gate_ln = sem("gates_psum"), sem("gate_raw"), sem("gate_abs"), sem("gate_ln")
        gate_M, gate_exps, nat_ready, cols_psum, cols_ready = (sem("gate_M"), sem("gate_exps"), sem("nat_ready"),
                                                               sem("cols_psum"), sem("cols_ready"))
        memsets = sem("memsets")
        proj_out, conv_done, qk_exp, qk_done, so_ready = (sem("proj_out"), sem("conv_done"), sem("qk_exp"),
                                                          sem("qk_done"), sem("so_ready"))
        front, tmp_ready, p_ready, s_ready, kw_ready = (sem("front"), sem("tmp_ready"), sem("p_ready"),
                                                        sem("s_ready"), sem("kw_ready"))
        num_done, qc_used, num_used, hn_ready = sem("num_done"), sem("qc_used"), sem("num_used"), sem("hn_ready")
        c0_in = [sem("c0_in0"), sem("c0_in1")]
        c_stored = [sem("c_stored0"), sem("c_stored1")]
        m_stored, m_ready, y_stored = sem("m_stored"), sem("m_ready"), sem("y_stored")
        hT_back, og_ready = sem("hT_back"), sem("og_ready")
        gateb_psum, gateb_ready = sem("gateb_psum"), sem("gateb_ready")
        u_done, e_done, act_done = sem("u_done"), sem("e_done"), sem("act_done")
        glu_exp, glu_done, cv_ready, sq_ready, ssq_done = (sem("glu_exp"), sem("glu_done"), sem("cv_ready"),
                                                           sem("sq_ready"), sem("ssq_done"))
        rb_ready, z_ready, ez_ready, zs_ready = sem("rb_ready"), sem("z_ready"), sem("ez_ready"), sem("zs_ready")
        route_psum, route_gap, route_exp = sem("route_psum"), sem("route_gap"), sem("route_exp")
        fin_ready = sem("fin_ready")
        sel_ready, pos_psum, plan_ready = sem("sel_ready"), sem("pos_psum"), sem("plan_ready")
        htok_psum, htok_ready0, htok_ready1 = sem("htok_psum"), sem("htok_ready0"), sem("htok_ready1")
        pick_ready, gathered, picks_used = sem("pick_ready"), sem("gathered"), sem("picks_used")
        hg_hi_ready, hg_ready, back_ready = sem("hg_hi_ready"), sem("hg_ready"), sem("back_ready")
        y_ready, scattered, acc_added = sem("y_ready"), sem("scattered"), sem("acc_added")
        hi_ready, split_ready = sem("hi_ready"), sem("split_ready")
        hid_turned, hid_hi_ready, hid_ready = sem("hid_turned"), sem("hid_hi_ready"), sem("hid_ready")

        block = ctx.enter_context(nc.Block())

        def slot(n):
            return n % SLOTS

        def ada_stage(a):
            if a < ADA_FIRST:
                return a
            if a < ADA_FIRST + ADA_MID:
                return ST_ADA + a - ADA_FIRST
            s = next(s for s in range(N_PW1) if a < ada_beside(s))
            return pw1_stage(s) + 1 + a - ada_beside(s - 1)

        def ada_through(it):
            return ADA_FIRST + ADA_MID * (it + 1) // ITS

        @block.sync
        def _(sp):
            def load(src, base, count, width, first=0):
                def one(n, row, j):
                    sp.wait_ge(stage_used, n - SLOTS + 1)
                    sp.dma_start(ring[:, slot(base + j), 0:width],
                                 src[bass.ds(row, 1), :, :].rearrange("o p n -> (o p) n")
                                 ).then_inc(loaded[slot(base + j)], 16)
                turns = count // SLOTS
                if turns > 1:
                    with sp.Fori(0, turns) as i:
                        for j in range(SLOTS):
                            one(i * SLOTS + (base + j), i * SLOTS + (first + j), j)
                else:
                    turns = 0
                for j in range(turns * SLOTS, count):
                    one(base + j, first + j, j)

            sp.dma_start(vec[:, :], vecs).then_inc(vec_in, 16)
            sp.dma_start(cst[:, :], consts).then_inc(cst_in, 16)
            sp.dma_start(x[:, :, :], x_in).then_inc(x_in_s, 16)
            sp.dma_start(gate[:, 1, :], pos).then_inc(pos_in, 16)
            for n in range(SLOTS):
                sp.dma_start(ring[:, n, 0:MIX], mix[n]).then_inc(loaded[n], 16)
            load(mix, SLOTS, ST_FF - SLOTS, MIX, SLOTS)
            load(ff, ST_FF, FC, STAGE)
            load(mix, ST_PW1, ST_MOE - ST_PW1, MIX, ST_FF)
            def expert_stage(m, row, j):
                sp.dma_start(ring[:, slot(ST_MOE + j), :], moe[bass.ds(row, 1), :, :].rearrange("o p n -> (o p) n")
                             ).then_inc(loaded[slot(ST_MOE + j)], 16)

            for m in range(SLOTS):
                sp.wait_ge(stage_used, ST_MOE + m - SLOTS + 1)
                expert_stage(m, m, m)
            with sp.Fori(1, (EXPERTS - 1) * FC // SLOTS) as i:
                for j in range(SLOTS):
                    sp.wait_ge(split_ready, i * (2 * SLOTS) + 2 * (j - SLOTS + 1))
                    expert_stage(i * SLOTS + j, i * SLOTS + j, j)
            sp.wait_ge(plan_ready, 1)
            items = sp.value_load(plan[0:1, 7:8], min_val=1, max_val=1 + OVER)
            with sp.Fori(0, items) as k:
                e = sp.value_load(plan[0:1, bass.ds(k + 1, 1)], min_val=0, max_val=EXPERTS - 1)
                with sp.Fori(0, FC // SLOTS) as i:
                    for j in range(SLOTS):
                        sp.wait_ge(split_ready, k * CUTS + i * (2 * SLOTS) + ((EXPERTS - 1) * CUTS + 2 * (j - SLOTS + 1)))
                        expert_stage(None, e * FC + i * SLOTS + j, j)

        @block.gpsimd
        def _(pool):
            pool.memset(vaug[:, :, :, DV:DVA], 1.0).then_inc(memsets, 1)
            pool.wait_ge(x_ready, 1)
            pool.memset(pad[:, :, :, :, 0:2], 0.0).then_inc(memsets, 1)
            pool.memset(pad[:, :, :, :, P + 2:P + 4], 0.0).then_inc(memsets, 1)
            for h in range(HEADS):
                if h >= 2:
                    pool.wait_ge(num_done, 2 * (h - 2) + 2)
                pool.dma_start(c0b[:, h % 2, :, :], c0[h]).then_inc(c0_in[h % 2], 16)
            pool.wait_ge(x_ready, 3)
            pool.memset(pad31, 0.0).then_inc(memsets, 1)
            pool.memset(acc, 0.0).then_inc(acc_added, 1)
            pool.memset(back, 0.0).then_inc(back_ready, 1)

        @block.scalar
        def _(act):
            n_chain = [0]

            def link(ins):
                n_chain[0] += 1
                ins.then_inc(act_chain, 1)
                act.wait_ge(act_chain, n_chain[0])

            act.wait_ge(pos_in, 16)
            act.dma_start(wg[:, :, :, :], w_gate).then_inc(late_in, 16)
            act.dma_start(rc[:, :], rowc).then_inc(late_in, 16)
            act.dma_start(wr[:, :, :], w_router).then_inc(late_in, 16)

            act.activation(ce[:, :], vec[:, V_COND:V_COND + KD * G], ACT.Exp, scale=-1.0).then_inc(cond_exp, 1)

            def square_sum(q):
                act.wait_ge(x_ready, q + 1)
                act.activation(xn[:, 0, :], x[:, 0, :], ACT.Square, accum_out=ss[:, 0:1]).then_inc(ss_ready, 1)
                act.wait_ge(rstd_ready, q + 1)

            def norm_turn(q):
                square_sum(q)
                act.activation(xn[:, 0, :], x[:, 0, :], ACT.Copy, scale=rstd[:, 0:1]).then_inc(xn0_ready, 1)
                for b in range(2):
                    act.wait_ge(turned, 4 * q + b + 1)
                    if b == 0:
                        act.wait_ge(mod_ready, 2 * (3 * q + 2))
                    for i in range(4):
                        k = 4 * b + i
                        act.activation(hT[:, k, 0:P], ps[:, YB + b, i * P:(i + 1) * P], ACT.Identity,
                                       scale=scl[:, q, k, 0:1], bias=mod[:, 3 * q, k, 0:1]).then_inc(hT0_ready, 1)

            def gate_copies(q):
                for i in range(4):
                    act.wait_ge(gateb_psum, 4 * q + i + 1)
                    if i == 0:
                        act.wait_ge(x_ready, q + 1)
                    act.activation(gate[:, i // 2, (i % 2) * 512:(i % 2 + 1) * 512], ps[:, i, :],
                                   ACT.Copy).then_inc(gateb_ready, 1)

            act.wait_ge(cst_in, 16)
            norm_turn(0)

            act.wait_ge(late_in, 48)
            act.wait_ge(gates_psum, 1)
            for w in range(2):
                act.activation(rt[:, w, :, :], ps[0:ROWS, MISC, w * T:(w + 1) * T], ACT.Identity,
                               bias=rc[:, w:w + 1]).then_inc(gate_raw, 1)
            act.wait_ge(gate_abs, 1)
            link(act.activation(rt[:, 5, :, :], rt[:, 4, :, :], ACT.Exp))
            act.activation(rt[:, 6, :, :], rt[:, 5, :, :], ACT.Ln, bias=cst[0:ROWS, C_ONE:C_ONE + 1]).then_inc(gate_ln, 1)
            act.wait_ge(gate_M, 1)
            act.activation(row[:, 2:4, :], rt[:, 4, :, :], ACT.Exp, scale=-1.0).then_inc(gate_exps, 1)
            act.activation(row[:, 4, :], row[:, 7, :], ACT.Exp, scale=-1.0, bias=rc[:, 2:3]).then_inc(gate_exps, 1)
            act.activation(row[:, 5, :], row[:, 0, :], ACT.Exp, bias=small[0:ROWS, 0:1]).then_inc(gate_exps, 1)

            def silu_exp(s):
                act.wait_ge(conv_done, s + 1)
                if s >= 2:
                    act.wait_ge(qk_done, s - 1)
                act.activation(eq[:, s % 2, :, :], ca[:, s % 2, :, :], ACT.Tanh, scale=0.5).then_inc(qk_exp, 1)

            for s in range(N_IN):
                b = UB + s % 2
                act.wait_ge(stage_used, ST_IN + s + 1)
                if s < HEADS:
                    if s == 0:
                        act.wait_ge(memsets, 3)
                    if s >= 2:
                        act.wait_ge(conv_done, s - 1)
                    act.activation(pad[:, s % 2, 0, :, 2:P + 2], ps[:, b, 0:T].rearrange("p (g t) -> p g t", g=G), ACT.Copy)
                    act.activation(pad[:, s % 2, 1, :, 2:P + 2], ps[:, b, T:2 * T].rearrange("p (g t) -> p g t", g=G),
                                   ACT.Copy).then_inc(proj_out, 1)
                elif s < 2 * HEADS:
                    act.activation(vaug[:, :, s - HEADS, 0:DV], ps[:, b, :].rearrange("p (g v) -> p g v", g=G),
                                   ACT.Copy).then_inc(proj_out, 1)
                else:
                    i = 2 * (s - 2 * HEADS)
                    act.activation(so[:, i:i + 2, :], ps[:, b, :].rearrange("p (c t) -> p c t", c=2), ACT.Tanh,
                                   scale=0.5).then_inc(proj_out, 1)
                if 1 <= s <= HEADS:
                    silu_exp(s - 1)

            def decay_scores(it):
                h, g = it // 2, it % 2
                act.wait_ge(tmp_ready, it + 1)
                if it == 0:
                    act.wait_ge(cols_ready, 1)
                for d in range(DIR):
                    r = 32 * d + h
                    ins = act.activation(pe_[:, it % 2, d, :], tmp[:, it % 2, d, :], ACT.Exp, scale=-1.0,
                                         bias=col[:, g, r:r + 1])
                ins.then_inc(p_ready, 1)

            decay_scores(0)
            for it in range(ITS):
                h, g = it // 2, it % 2
                if it + 1 < ITS:
                    decay_scores(it + 1)
                act.wait_ge(num_done, it + 1)
                if g == 0:
                    if h >= 2:
                        act.wait_ge(c_stored[h % 2], 16 * (h // 2))
                    act.activation(stc[:, h % 2, :, :], ps[:, QB:QB + 2, 0:DVA], ACT.Copy).then_inc(qc_used, 1)
                    act.wait_ge(qc_used, it + 1)
                    act.dma_start(c_out[h], stc[:, h % 2, :, :]).then_inc(c_stored[h % 2], 16)
                else:
                    if it >= 2:
                        act.wait_ge(num_used, it)
                    for d in range(DIR):
                        r = 32 * d + h
                        ins = act.activation(qcs[:, d, :], ps[:, QB + d, 0:DVA], ACT.Copy, scale=kscale[:, 0, r:r + 1])
                    ins.then_inc(qc_used, 1)
                act.wait_ge(num_used, it + 1)
                act.activation(hsq, hs, ACT.Square, accum_out=small[:, 4:5]).then_inc(hs_squared, 1)
                act.wait_ge(hs_squared, it + 1)
            act.wait_ge(m_ready, 1)
            act.dma_start(m_out, small[0:ROWS, 1:2]).then_inc(m_stored, 16)
            gate_copies(0)
            norm_turn(1)
            gate_copies(1)

            def hidden_tanh(fc, c, n):
                act.wait_ge(u_done, fc + 1)
                act.activation(fe[:, c % 2, 0:n], ps[:, UB + c % 2, 0:n], ACT.Tanh, scale=0.5).then_inc(e_done, 1)

            with act.Fori(0, FC // 2) as i:
                for c in range(2):
                    hidden_tanh(i * 2 + c, c, T)
            norm_turn(2)
            gate_copies(2)

            for s in range(N_PW1):
                act.wait_ge(stage_used, pw1_stage(s) + 1)
                act.activation(fe[:, s % 2, :], ps[:, UB + s % 2, T:2 * T], ACT.Tanh, scale=0.5).then_inc(glu_exp, 1)
                if s >= 1:
                    act.wait_ge(cv_ready, s)
                    if s >= 3:
                        act.wait_ge(ssq_done, s - 2)
                    act.activation(sqb[:, (s - 1) % 2, :], cv[:, s - 1, :], ACT.Square).then_inc(sq_ready, 1)
            act.wait_ge(cv_ready, N_PW1)
            act.wait_ge(ssq_done, N_PW1 - 2)
            act.activation(sqb[:, (N_PW1 - 1) % 2, :], cv[:, N_PW1 - 1, :], ACT.Square).then_inc(sq_ready, 1)
            act.wait_ge(ssq_done, N_PW1)
            link(act.activation(rb, ps[:, YB, 0:T], ACT.Ln, scale=1.0 / D, bias=eps))
            act.activation(rb, rb, ACT.Exp, scale=-0.5).then_inc(rb_ready, 1)
            act.wait_ge(z_ready, 1)
            for k in range(KD):
                ins = act.activation(ez[:, k, :], z[:, k, :], ACT.Tanh, scale=0.5)
            ins.then_inc(ez_ready, 1)
            norm_turn(3)
            gate_copies(3)
            act.wait_ge(route_gap, 1)
            act.activation(tk[:, 3, :], tk[:, 2, :], ACT.Exp).then_inc(route_exp, 1)
            for b in range(2):
                act.wait_ge(htok_psum, b + 1)
                act.activation(htok[:, 0, b * 512:(b + 1) * 512], ps[:, YB + b, :], ACT.Copy).then_inc(htok_ready0, 1)

            def hg_high(i):
                act.wait_ge(gathered, i + 1)
                act.activation(hg_hi[:, :, :], ps[:, UB:UB + 2, :].rearrange("p b (k t) -> p (b k) t", k=4), ACT.Copy
                               ).then_inc(hg_hi_ready, 1)

            def last_output(i):
                act.wait_ge(stage_used, i * CUTS + ST_MOE)
                act.activation(y_sb.rearrange("p (b n) -> p b n", b=2), ps[:, YB:YB + 2, :], ACT.Copy
                               ).then_inc(y_ready, 1)

            hg_high(0)
            act.wait_ge(plan_ready, 1)
            items = act.value_load(plan[0:1, 0:1], min_val=EXPERTS, max_val=ITEMS)
            with act.Fori(0, items) as i:
                for s in range(CUTS + 1):
                    if s == W_BUFS:
                        last_output(i)
                    if s == behind(BACK_ROW):
                        act.wait_ge(picks_used, i + 1)
                        act.activation(back, ps[:, 7, 0:T].rearrange("p (g t) -> p g t", g=G), ACT.Copy
                                       ).then_inc(back_ready, 1)
                    for q in range(GROUPS):
                        if s == behind(UP_END[q]):
                            act.wait_ge(u_done, i * GROUPS + (FC + q + 1))
                            act.activation(th, ps[:, 2 * (q % 2), :], ACT.Tanh, scale=0.5).then_inc(e_done, 1)
                        if s == behind(TURN_ROW[q]):
                            act.wait_ge(hid_turned, i * GROUPS + (q + 1))
                            act.activation(hid_hi[:, q % 2, :], ps[:, 6, :], ACT.Copy).then_inc(hid_hi_ready, 1)
                    if s == behind(GATHER_ROW):
                        hg_high(i + 1)
                    if s < CUTS:
                        sl = slot(ST_MOE + s // 2)
                        if s % 2 == 0:
                            act.wait_ge(loaded[sl], i * (16 * FC // SLOTS) + 16 * ((ST_MOE + s // 2) // SLOTS + 1))
                        act.wait_ge(stage_used, i * CUTS + (ST_MOE + s - W_BUFS + 1))
                        act.activation(w_hi[:, s % W_BUFS, :], ring[:, sl, s % 2 * CUT * ROW:(s % 2 + 1) * CUT * ROW],
                                       ACT.Copy).then_inc(hi_ready, 1)
            last_output(items)
            act.wait_ge(act_done, items * GROUPS + FC)
            act.dma_start(gain_out, norm_out).then_inc(no_in, 16)
            square_sum(4)
            act.activation(xn[:, 0, :], x[:, 0, :], ACT.Copy, scale=rstd[:, 0:1]).then_inc(xn0_ready, 1)
            act.wait_ge(fin_ready, 1)
            act.dma_start(y_out[:, 1, :], xn[:, 1, :]).then_inc(y_stored, 16)
            act.wait_ge(fin_ready, 2)
            act.dma_start(y_out[:, 0, :], xn[:, 0, :]).then_inc(y_stored, 16)
            act.wait_ge(y_stored, 32)
            act.wait_ge(m_stored, 16)
            for i in range(2):
                act.wait_ge(c_stored[i], 16 * (HEADS // 2))

        @block.vector
        def _(dve):
            n_chain = [0]

            def link(ins):
                n_chain[0] = n_chain[0] + 1
                ins.then_inc(dve_chain, 1)
                dve.wait_ge(dve_chain, n_chain[0])

            STT, TT, TS = dve.scalar_tensor_tensor, dve.tensor_tensor, dve.tensor_scalar

            def rsqrt(out, total, n, width, last=None):
                v, y, t = (root[:, i, 0:width] for i in range(3))
                bits = mybir.dt.int32
                link(TS(v, total, 1.0 / n, EPS, ALU.mult, ALU.add))
                link(TS(t.bitcast(bits), v.bitcast(bits), 1, None, ALU.logical_shift_right))
                link(TS(y.bitcast(bits), t.bitcast(bits), -1.0, float(0x5F3759DF), ALU.mult, ALU.add))
                for step in range(3):
                    link(TT(t, y, y, ALU.mult))
                    link(STT(t, t, -0.5, v, ALU.mult, ALU.mult))
                    end = STT(out if step == 2 else y, t, 1.5, y, ALU.add, ALU.mult)
                    if step < 2:
                        link(end)
                return end

            dve.wait_ge(cond_exp, 1)
            link(TS(cd[:, :], ce[:, :], 1.0, None, ALU.add))
            link(dve.reciprocal(ce[:, :], cd[:, :]))
            TT(silu_c[:, :], vec[:, V_COND:V_COND + KD * G], ce[:, :], ALU.mult).then_inc(cond_ready, 1)
            dve.wait_ge(x_in_s, 16)
            dve.wait_ge(pos_in, 16)
            TT(x[:, 1, :], x[:, 1, :], gate[:, 1, :], ALU.add).then_inc(x_ready, 1)

            def modulation(hv):
                v, half = hv // 2, (hv % 2) * KD // 2
                ks = slice(half, half + KD // 2)

                def spread(at):
                    return vec[:, at + half:at + half + KD // 2].unsqueeze(2).to_broadcast([P, KD // 2, G])

                dve.wait_ge(stage_used, ada_stage(2 * hv + 1) + 1)
                bias = spread(V_ADA + v * KD)
                src = ps[:, MODB + hv % 2, :].rearrange("p (k g r) -> p k g r", k=KD // 2, g=G)[:, :, :, 0]
                if v % 3 == 1:
                    q = v // 3
                    link(TT(mod[:, v, ks, :], src, bias, ALU.add))
                    gain = V_NMIX + (q // 2) * KD if q % 2 == 0 else V_NFFN + (q // 2) * KD
                    STT(scl[:, q, ks, :], mod[:, v, ks, :], 1.0, spread(gain), ALU.add, ALU.mult
                        ).then_inc(mod_ready, 1)
                else:
                    TT(mod[:, v, ks, :], src, bias, ALU.add).then_inc(mod_ready, 1)

            def square_sum(q):
                link(dve.tensor_tensor_reduce(out=xn[:, 1, :], in0=x[:, 1, :], in1=x[:, 1, :], scale=1.0, scalar=0.0,
                                              op0=ALU.mult, op1=ALU.add, accum_out=ss[:, 1:2]))
                dve.wait_ge(ss_ready, q + 1)
                rsqrt(rstd[:, :], ss[:, :], D, G).then_inc(rstd_ready, 1)
                dve.wait_ge(rstd_ready, q + 1)

            for hv in range(ADA_FIRST // 2):
                modulation(hv)

            def norm_turn(q):
                if q == 0:
                    dve.wait_ge(x_ready, 1)
                else:
                    dve.wait_ge(x_ready, q + 1)
                square_sum(q)
                TS(xn[:, 1, :], x[:, 1, :], rstd[:, 1:2], None, ALU.mult).then_inc(xn1_ready, 1)
                for b in range(2):
                    dve.wait_ge(turned, 4 * q + b + 3)
                    if q == 0 and b == 0:
                        dve.wait_ge(mod_ready, 4)
                    for i in range(4):
                        k = 4 * b + i
                        TS(hT[:, k, P:T], ps[:, YB + 2 + b, i * P:(i + 1) * P], scl[:, q, k, 1:2], mod[:, 3 * q, k, 1:2],
                           ALU.mult, ALU.add).then_inc(hT1_ready, 1)

            norm_turn(0)

            dve.wait_ge(gate_raw, 2)
            for w in range(2):
                dve.tensor_copy(rt[0:32, 2 + w, :, :], rt[0:32, w, :, :])
                link(dve.tensor_copy(rt[32:ROWS, 2 + w, :, :], rt[32:ROWS, w, :, ::-1]))
            STT(rt[:, 4, :, :], rt[:, 3, :, :], -1.0, rt[:, 3, :, :], ALU.mult, ALU.min).then_inc(gate_abs, 1)
            dve.wait_ge(gate_ln, 1)
            link(STT(rt[:, 7, :, :], rt[:, 3, :, :], 0.0, rt[:, 6, :, :], ALU.min, ALU.subtract))
            one = cst[0:ROWS, C_ONE:C_ONE + P]
            for g in range(G):
                link(dve.tensor_tensor_scan(rt[:, 3, g, :], one, rt[:, 7, g, :], 0.0, ALU.mult, ALU.add))
            link(TT(row[:, 0:2, :], rt[:, 2, :, :], rt[:, 3, :, :], ALU.subtract))
            link(dve.tensor_tensor_scan(row[:, 6, :], one, row[:, 0, :], 0.0, ALU.mult, ALU.max))
            link(dve.tensor_tensor_scan(row[:, 7, :], one, row[:, 1, :], rc[:, 2:3], ALU.mult, ALU.max))
            link(TS(small[0:ROWS, 0:1], row[:, 6, P - 1:P], -1.0, None, ALU.mult))
            TT(rt[:, 4, :, :], rt[:, 3, :, :], row[:, 6:8, :], ALU.add).then_inc(gate_M, 1)
            dve.wait_ge(gate_M, 1)
            dve.tensor_copy(small[0:ROWS, 1:2], rt[:, 4, 0, P - 1:P]).then_inc(m_ready, 1)
            dve.wait_ge(gate_exps, 3)
            dve.tensor_copy(nat[0:32, :, :], row[0:32, :, :]).then_inc(nat_ready, 1)
            dve.tensor_copy(nat[32:ROWS, :, :], row[32:ROWS, :, ::-1]).then_inc(nat_ready, 1)

            def conv_qk(s):
                dve.wait_ge(proj_out, s + 1)
                if s >= 2:
                    dve.wait_ge(qk_done, s - 1)
                for t in range(A_TAPS):
                    for j in range(2):
                        w = vec[:, V_ACONV + t * 2 * KD + 2 * s + j:V_ACONV + t * 2 * KD + 2 * s + j + 1]
                        out = ca[:, s % 2, j, :].rearrange("p (g t) -> p g t", g=G)
                        src = pad[:, s % 2, j, :, t:t + P]
                        ins = (TS(out, src, w, None, ALU.mult) if t == 0 else STT(out, src, w, out, ALU.mult, ALU.add))
                    if t < A_TAPS - 1:
                        link(ins)
                ins.then_inc(conv_done, 1)

            def silu_qk(s):
                dve.wait_ge(qk_exp, s + 1)
                STT(qkT[:, 2 * s:2 * s + 2, :], eq[:, s % 2, :, :], 1.0, ca[:, s % 2, :, :], ALU.add, ALU.mult
                    ).then_inc(qk_done, 1)

            for s in range(HEADS):
                conv_qk(s)
                if s >= 1:
                    silu_qk(s - 1)
            silu_qk(HEADS - 1)
            dve.wait_ge(cols_psum, 1)
            gate_cols = ps[:, MISC, 0:6 * ROWS].rearrange("p (q r) -> p q r", q=6)
            dve.tensor_copy(col, gate_cols)
            link(TS(kscale, gate_cols[:, 4:6, :], 0.5, None, ALU.mult))
            TS(kscale[:, 0, :], kscale[:, 0, :], Q_SCALE, None, ALU.mult).then_inc(cols_ready, 1)
            for s in range(2 * HEADS, N_IN):
                i = 2 * (s - 2 * HEADS)
                dve.wait_ge(proj_out, s + 1)
                TS(so[:, i:i + 2, :], so[:, i:i + 2, :], 1.0, 0.5, ALU.add, ALU.mult).then_inc(so_ready, 1)

            def masked(it):
                dve.wait_ge(front, it + 1)
                TT(tmp[:, it % 2, :, :], ps[:, UB + it % 2, P:3 * P].rearrange("p (d t) -> p d t", d=DIR), mask,
                   ALU.add).then_inc(tmp_ready, 1)

            def out_gate(it):
                h, g = it // 2, it % 2
                dve.wait_ge(hT_back, it + 1)
                for c in range(2):
                    f = 2 * h + c
                    o = so[:, f, g * P:(g + 1) * P]
                    ins = STT(o, ps[:, UB + it % 2, c * P:(c + 1) * P], vec[:, V_GN + f:V_GN + f + 1], o,
                              ALU.mult, ALU.mult)
                ins.then_inc(og_ready, 1)

            dve.wait_ge(so_ready, HEADS)
            masked(0)
            made = ADA_FIRST // 2
            for it in range(ITS):
                h, g = it // 2, it % 2
                b = UB + it % 2
                dve.wait_ge(p_ready, it + 1)
                if it >= 2:
                    dve.wait_ge(num_done, it - 1)
                if it == 0:
                    dve.wait_ge(qk_done, HEADS)
                for d in range(DIR):
                    ins = STT(sT[:, it % 2, d, :], pe_[:, it % 2, d, :], 0.25 * Q_SCALE, ps[:, b, 0:P], ALU.mult,
                              ALU.mult)
                ins.then_inc(s_ready, 1)
                if g == 0:
                    if it >= 1:
                        dve.wait_ge(num_done, it)
                    for d in range(DIR):
                        r = 32 * d + h
                        ins = TS(kw[:, d, :], ps[:, b, 3 * P:4 * P], kscale[:, 1, r:r + 1], None, ALU.mult)
                    ins.then_inc(kw_ready, 1)
                if it >= 1:
                    out_gate(it - 1)
                    while 2 * (made + 1) <= ada_through(it - 1):
                        modulation(made)
                        made += 1
                if it + 1 < ITS:
                    masked(it + 1)
                dve.wait_ge(num_done, it + 1)
                if g == 0:
                    src = ps[:, YB:YB + 2, :]
                    link(dve.tensor_copy(small[:, 8:10].unsqueeze(2), src[:, :, DV:DVA]))
                    den = small[:, 8:10]
                else:
                    src = nm
                    dve.wait_ge(qc_used, it + 1)
                    link(TT(nm, ps[:, YB:YB + 2, 0:DVA], qcs, ALU.add))
                    link(dve.tensor_copy(small[:, 8:10].unsqueeze(2), nm[:, :, DV:DVA]))
                    den = small[:, 8:10]
                link(STT(small[:, 10:12], den, -1.0, den, ALU.mult, ALU.max))
                link(TT(small[:, 12:14], small[:, 10:12], col[:, 2 + g, h:h + 33:32], ALU.max))
                link(dve.reciprocal(small[:, 14:16], small[:, 12:14]))
                link(TS(h0, src[:, 0, 0:DV], small[:, 14:15], None, ALU.mult))
                if it >= 1:
                    dve.wait_ge(hn_ready, it)
                STT(hs, src[:, 1, 0:DV], small[:, 15:16], h0, ALU.mult, ALU.add).then_inc(num_used, 1)
                dve.wait_ge(hs_squared, it + 1)
                link(rsqrt(small[:, 6:7], small[:, 4:5], DV, 1))
                if it >= 1:
                    dve.wait_ge(hT_back, it)
                TS(hn, hs, small[:, 6:7], None, ALU.mult).then_inc(hn_ready, 1)
            out_gate(ITS - 1)
            while 2 * (made + 1) <= ADA_FIRST + ADA_MID:
                modulation(made)
                made += 1

            def residual(q, last_stage, scale=1.0):
                dve.wait_ge(stage_used, last_stage)
                dve.wait_ge(gateb_ready, 4 * q + 4)
                gv = gate_b[:, 0:G * D].rearrange("p (b n) -> p b n", b=4)
                for b in range(4):
                    ins = STT(gv[:, b, :], gv[:, b, :], scale, ps[:, YB + b, :], ALU.mult, ALU.mult)
                link(ins)
                TT(x[:, :, :], x[:, :, :], gate, ALU.add).then_inc(x_ready, 1)

            residual(0, ST_OUT + N_OUT)
            norm_turn(1)

            def hidden(fc, c, n):
                dve.wait_ge(e_done, fc + 1)
                link(STT(ft[:, c % 2, 0:n], fe[:, c % 2, 0:n], 1.0, ps[:, UB + c % 2, 0:n], ALU.add, ALU.mult))
                STT(fact[:, c % 2, 0:n], ft[:, c % 2, 0:n], 0.5, ps[:, UB + c % 2, n:2 * n], ALU.mult, ALU.mult
                    ).then_inc(act_done, 1)

            LINKS = 1
            start = n_chain[0]
            with dve.Fori(0, FC // 2) as i:
                for c in range(2):
                    n_chain[0] = i * (2 * LINKS) + (start + c * LINKS)
                    hidden(i * 2 + c, c, T)
            n_chain[0] = start + FC * LINKS
            residual(1, ST_FF + FC)
            norm_turn(2)

            dve.wait_ge(memsets, 4)
            for i in range(2):
                dve.wait_ge(c_stored[i], 16 * (HEADS // 2))
            for s in range(N_PW1):
                dve.wait_ge(glu_exp, s + 1)
                link(TS(fd, fe[:, s % 2, :], 1.0, 0.5, ALU.add, ALU.mult))
                TT(pad31[:, s, :, 15:15 + P], ps[:, UB + s % 2, 0:T].rearrange("p (g t) -> p g t", g=G),
                   fd.rearrange("p (g t) -> p g t", g=G), ALU.mult).then_inc(glu_done, 1)
                dve.wait_ge(glu_done, s + 1)
                out = cv[:, s, :].rearrange("p (g t) -> p g t", g=G)
                for t in range(B_TAPS):
                    w = vec[:, V_BCONV + t * KD + s:V_BCONV + t * KD + s + 1]
                    src = pad31[:, s, :, t:t + P]
                    if t == 0:
                        link(TS(out, src, w, vec[:, V_BDW + s:V_BDW + s + 1], ALU.mult, ALU.add))
                    elif t < B_TAPS - 1:
                        link(STT(out, src, w, out, ALU.mult, ALU.add))
                    else:
                        STT(out, src, w, out, ALU.mult, ALU.add).then_inc(cv_ready, 1)
                while 2 * (made + 1) <= ada_beside(s):
                    modulation(made)
                    made += 1
            dve.wait_ge(rb_ready, 1)
            for k in range(KD):
                ins = STT(z[:, k, :], cv[:, k, :], vec[:, V_BNORM + k:V_BNORM + k + 1], rb, ALU.mult, ALU.mult)
            ins.then_inc(z_ready, 1)
            dve.wait_ge(ez_ready, 1)
            STT(z, ez, 1.0, z, ALU.add, ALU.mult).then_inc(zs_ready, 1)
            residual(2, ST_PW2 + N_PW2, 0.5)
            norm_turn(3)

            def bc(a):
                return a.unsqueeze(2).to_broadcast([P, G, EXPERTS])

            dve.wait_ge(route_psum, 1)
            link(dve.tensor_copy(lg, ps[:, MISC, 0:G * EXPERTS].rearrange("p (g e) -> p g e", g=G)))
            cur = lg
            for j in range(2):
                link(dve.tensor_reduce(tk[:, j, :], cur, X, ALU.max))
                link(TT(key, cur, bc(tk[:, j, :]), ALU.is_equal))
                link(TT(key, key, desc, ALU.mult))
                link(dve.tensor_reduce(tk[:, 4 + j, :], key, X, ALU.max))
                link(TT(oh[:, j, :, :], desc, bc(tk[:, 4 + j, :]), ALU.is_equal))
                if j == 0:
                    link(STT(l2, oh[:, 0, :, :], -3e38, lg, ALU.mult, ALU.add))
                    cur = l2
            TT(sel, oh[:, 0, :, :], oh[:, 1, :, :], ALU.add).then_inc(sel_ready, 1)
            TT(tk[:, 2, :], tk[:, 1, :], tk[:, 0, :], ALU.subtract).then_inc(route_gap, 1)
            for b in range(2):
                dve.wait_ge(htok_psum, b + 3)
                dve.tensor_copy(htok[:, 1, b * 512:(b + 1) * 512], ps[:, YB + 2 + b, :]).then_inc(htok_ready1, 1)
            dve.wait_ge(route_exp, 1)
            link(TS(tk[:, 6, :], tk[:, 3, :], 1.0, None, ALU.add))
            link(dve.reciprocal(tk[:, 7, :], tk[:, 6, :]))
            link(TT(tk[:, 8, :], tk[:, 7, :], tk[:, 3, :], ALU.mult))
            link(TT(oh[:, 0, :, :], oh[:, 0, :, :], bc(tk[:, 7, :]), ALU.mult))
            link(TT(oh[:, 1, :, :], oh[:, 1, :, :], bc(tk[:, 8, :]), ALU.mult))
            own = item_comb[:, :, 0:EXPERTS]
            link(TT(own, oh[:, 0, :, :], oh[:, 1, :, :], ALU.add))
            dve.wait_ge(pos_psum, 1)
            slots = item_pos[:, :, 0:EXPERTS]
            link(TT(key, ps[:, MISC, 0:G * EXPERTS].rearrange("p (g e) -> p g e", g=G), sel, ALU.mult))
            link(STT(slots, sel, -1.0, key, ALU.add, ALU.add))

            def make_picks(i):
                for g in range(G):
                    p = item_pos[:, g, bass.ds(i, 1)] if not isinstance(i, int) else item_pos[:, g, i:i + 1]
                    w = item_comb[:, g, bass.ds(i, 1)] if not isinstance(i, int) else item_comb[:, g, i:i + 1]
                    TS(pick[:, g, :], iota, p, None, ALU.is_equal)
                    ins = TS(pick_w[:, g, :], iota, p, w, ALU.is_equal, ALU.mult)
                ins.then_inc(pick_ready, 1)

            make_picks(0)
            count, is_over, rank, order = (over[:, n, :] for n in range(4))
            link(dve.tensor_copy(count, ps[:, MISC, G * EXPERTS:(G + 1) * EXPERTS]))
            link(TS(is_over, count, float(P), None, ALU.is_gt))
            link(dve.tensor_tensor_scan(rank, cst[:, C_ONE:C_ONE + EXPERTS], is_over, 0.0, ALU.mult, ALU.add))
            link(TT(order, is_over, rank, ALU.mult))
            for k in range(OVER + 1):
                i = EXPERTS + k
                link(TS(hit, order, float(k + 1), None, ALU.is_equal))
                link(dve.tensor_reduce(rsum[:, 0, 0:1], hit, X, ALU.add))
                both = hit.unsqueeze(1).to_broadcast([P, G, EXPERTS])
                link(STT(prod, slots, -float(P), both, ALU.add, ALU.mult))
                link(dve.tensor_reduce(rsum[:, 1, :], prod, X, ALU.add))
                link(TS(item_pos[:, :, i], rsum[:, 1, :], rsum[:, 0, 0:1], -1.0, ALU.add, ALU.add))
                link(TT(prod, own, both, ALU.mult))
                link(dve.tensor_reduce(item_comb[:, :, i], prod, X, ALU.add))
                if k < OVER:
                    link(TT(hit, hit, desc[:, 0, :], ALU.mult))
                    link(dve.tensor_reduce(rsum[:, 2, 0:1], hit, X, ALU.add))
                    link(STT(plan_f[:, 2 + k:3 + k], rsum[:, 0, 0:1], float(EXPERTS), rsum[:, 2, 0:1], ALU.mult,
                             ALU.subtract))
            dve.memset(plan_f[:, 1:2], float(EXPERTS - 1))
            dve.memset(plan_f[:, 5:7], 0.0)
            link(TS(plan_f[:, 0:1], rank[:, EXPERTS - 1:EXPERTS], float(EXPERTS), None, ALU.add))
            link(TS(plan_f[:, 7:8], rank[:, EXPERTS - 1:EXPERTS], 1.0, None, ALU.add))
            dve.tensor_copy(plan[0:1, :], plan_f[0:1, :]).then_inc(plan_ready, 1)

            def hg_low(i):
                dve.wait_ge(hg_hi_ready, i + 1)
                TT(hg_lo[:, :, :], ps[:, UB:UB + 2, :].rearrange("p b (k t) -> p (b k) t", k=4),
                   hg_hi[:, :, :].bitcast(f32), ALU.subtract).then_inc(hg_ready, 1)

            def add_output(i, n):
                dve.wait_ge(scattered, i * 4 + (n + 1))
                dve.wait_ge(acc_added, i * 4 + (n + 1))
                a = acc[:, n // 2, (n % 2) * 512:(n % 2 + 1) * 512]
                TT(a, ps[:, 7, :], a, ALU.add).then_inc(acc_added, 1)

            hg_low(0)
            dve.wait_ge(plan_ready, 1)
            items = dve.value_load(plan[0:1, 0:1], min_val=EXPERTS, max_val=ITEMS)
            start = n_chain[0]
            with dve.Fori(0, items) as i:
                for s in range(CUTS + 1):
                    for n in range(4):
                        if s == behind(SCATTER_ROWS[n]):
                            add_output(i, n)
                    if s == behind(BACK_ROW) + 1:
                        dve.wait_ge(picks_used, i + 1)
                        dve.wait_ge(gathered, i + 1)
                        make_picks(i + 1)
                    for q in range(GROUPS):
                        b = 2 * (q % 2)
                        if s == behind(UP_END[q]):
                            dve.wait_ge(e_done, i * GROUPS + (FC + q + 1))
                            n_chain[0] = i * GROUPS + (start + q)
                            link(STT(sg, th, 1.0, ps[:, b, :], ALU.add, ALU.mult))
                            STT(hid, sg, 0.5, ps[:, b + 1, :], ALU.mult, ALU.mult).then_inc(act_done, 1)
                        if s == behind(TURN_ROW[q]):
                            dve.wait_ge(hid_hi_ready, i * GROUPS + (q + 1))
                            TT(hid_lo[:, q % 2, :], ps[:, 6, :], hid_hi[:, q % 2, :].bitcast(f32), ALU.subtract
                               ).then_inc(hid_ready, 1)
                    if s == behind(GATHER_ROW):
                        hg_low(i + 1)
                    if s < CUTS:
                        dve.wait_ge(hi_ready, i * CUTS + (s + 1))
                        TT(w_lo[:, s % W_BUFS, :], ring[:, slot(ST_MOE + s // 2), s % 2 * CUT * ROW:(s % 2 + 1) * CUT * ROW],
                           w_hi[:, s % W_BUFS, :].bitcast(f32), ALU.subtract).then_inc(split_ready, 1)
            for n in range(4):
                add_output(items, n)
            n_chain[0] = items * GROUPS + start
            dve.wait_ge(acc_added, items * 4 + 5)
            dve.wait_ge(gateb_ready, 16)
            link(TT(acc, acc, gate, ALU.mult))
            TT(x[:, :, :], x[:, :, :], acc, ALU.add).then_inc(x_ready, 1)
            dve.wait_ge(no_in, 16)
            dve.wait_ge(x_ready, 5)
            square_sum(4)
            no = gain_out
            STT(xn[:, 1, :], x[:, 1, :], rstd[:, 1:2], no, ALU.mult, ALU.mult).then_inc(fin_ready, 1)
            dve.wait_ge(xn0_ready, 5)
            TT(xn[:, 0, :], xn[:, 0, :], no, ALU.mult).then_inc(fin_ready, 1)

        @block.tensor
        def _(pe):
            def arrived(n, j=None):
                j = n if j is None else j
                sl = slot(j)
                turn = n // SLOTS if isinstance(n, int) else None
                assert turn is not None
                pe.wait_ge(loaded[sl], 16 * (turn + 1))
                return ring[:, sl, :]

            pe.wait_ge(cst_in, 16)

            def ada(a, n):
                w = arrived(n)
                hv = a // 2
                if a % 2 == 0 and hv >= 2:
                    pe.wait_ge(mod_ready, hv - 1)
                    if hv == ADA_FIRST // 2 + 1:
                        pe.wait_ge(cols_ready, 1)
                for j in range(2):
                    c = (2 * (a % 2) + j) * P
                    for k in range(KD):
                        ins = pe.matmul(ps[:, MODB + hv % 2, c:c + P], w[:, k * 256 + j * P:k * 256 + (j + 1) * P],
                                        silu_c[:, k * G:(k + 1) * G].unsqueeze(2).to_broadcast([P, G, P // G]), start=(k == 0), stop=(k == KD - 1))
                ins.then_inc(stage_used, 1)

            def norm_turn(q):
                for g in range(G):
                    pe.wait_ge([xn0_ready, xn1_ready][g], q + 1)
                    for b in range(2):
                        for i in range(4):
                            k = 4 * b + i
                            ins = pe.transpose(ps[:, YB + 2 * g + b, i * P:(i + 1) * P], xn[:, g, k * P:(k + 1) * P],
                                               ident)
                        ins.then_inc(turned, 1)
                pe.wait_ge(hT0_ready, 8 * q + 8)
                pe.wait_ge(hT1_ready, 8 * q + 8)

            def tokens(f, k, g):
                return f[:, k, g * P:(g + 1) * P]

            pe.wait_ge(cond_ready, 1)
            for a in range(ADA_FIRST):
                ada(a, ada_stage(a))
            norm_turn(0)
            pe.wait_ge(late_in, 48)
            for w in range(2):
                for k in range(KD):
                    ins = pe.matmul(ps[0:ROWS, MISC, w * T:(w + 1) * T], wg[:, k, w, :], hT[:, k, :],
                                    start=(k == 0), stop=(k == KD - 1))
            ins.then_inc(gates_psum, 1)

            for s in range(N_IN):
                n = ST_IN + s
                w = arrived(n)
                b = UB + s % 2
                if s >= 2:
                    pe.wait_ge(proj_out, s - 1)
                for j in range(2):
                    for k in range(KD):
                        if HEADS <= s < 2 * HEADS:
                            ins = pe.matmul(ps[:, b, j * T:(j + 1) * T], tokens(hT, k, j), w[:, k * 256:(k + 1) * 256],
                                            start=(k == 0), stop=(k == KD - 1))
                        else:
                            ins = pe.matmul(ps[:, b, j * T:(j + 1) * T], w[:, k * 256 + j * P:k * 256 + (j + 1) * P],
                                            hT[:, k, :], start=(k == 0), stop=(k == KD - 1))
                ins.then_inc(stage_used, 1)
                if s == 2 * HEADS:
                    pe.wait_ge(nat_ready, 2)
                    for q in range(6):
                        ins = pe.transpose(ps[:, MISC, q * ROWS:(q + 1) * ROWS], nat[:, q, :], ident[0:ROWS, 0:ROWS])
                    ins.then_inc(cols_psum, 1)

            def front_step(it):
                h, g = it // 2, it % 2
                b = UB + it % 2
                if it >= 2:
                    pe.wait_ge(s_ready, it - 1)
                    pe.wait_ge(kw_ready, it // 2)
                    pe.wait_ge(og_ready, it - 1)
                pe.matmul(ps[:, b, 0:P], tokens(qkT, HEADS + h, g), tokens(qkT, h, g), start=True, stop=True)
                for d in range(DIR):
                    r = 32 * d + h
                    ins = pe.matmul(ps[:, b, (1 + d) * P:(2 + d) * P], ident[0:ROWS, r:r + 1].to_broadcast([ROWS, P]),
                                    nat[:, 6 + g, :], start=True, stop=True)
                if g == 0:
                    ins = pe.transpose(ps[:, b, 3 * P:4 * P], tokens(qkT, HEADS + h, 0), ident)
                ins.then_inc(front, 1)

            def turn_head(it):
                pe.wait_ge(hn_ready, it + 1)
                for c in range(2):
                    ins = pe.transpose(ps[:, UB + it % 2, c * P:(c + 1) * P], hn[:, c * P:(c + 1) * P], ident)
                ins.then_inc(hT_back, 1)

            pe.wait_ge(qk_done, HEADS)
            pe.wait_ge(proj_out, N_IN)
            front_step(0)
            a = ADA_FIRST
            for it in range(ITS):
                h, g = it // 2, it % 2
                pe.wait_ge(s_ready, it + 1)
                if g == 0:
                    pe.wait_ge(kw_ready, h + 1)
                else:
                    pe.wait_ge(c0_in[h % 2], 16 * (h // 2 + 1))
                if it >= 1:
                    pe.wait_ge(qc_used, it)
                    pe.wait_ge(num_used, it)
                for d in range(DIR):
                    if g == 0:
                        pe.matmul(ps[:, QB + d, 0:DVA], kw[:, d, :], vaug[:, 0, h, :], start=True, stop=True)
                    else:
                        pe.matmul(ps[:, QB + d, 0:DVA], tokens(qkT, h, 1), c0b[:, h % 2, d, :], start=True, stop=True)
                for d in range(DIR):
                    ins = pe.matmul(ps[:, YB + d, 0:DVA], sT[:, it % 2, d, :], vaug[:, g, h, :], start=True, stop=True)
                ins.then_inc(num_done, 1)
                if it + 1 < ITS:
                    front_step(it + 1)
                while a < ada_through(it):
                    ada(a, ada_stage(a))
                    a += 1
                turn_head(it)

            def gate_rows(q):
                v = 3 * q + 2
                pe.wait_ge(mod_ready, 2 * (v + 1))
                if q == 0:
                    pe.wait_ge(mod_ready, (ADA_FIRST + ADA_MID) // 2)
                for i in range(4):
                    for c in range(4):
                        k = 4 * (i % 2) + c
                        ins = pe.matmul(ps[:, i, c * P:(c + 1) * P],
                                        mod[:, v, k, i // 2:i // 2 + 1].to_broadcast([P, P]), ident,
                                        start=True, stop=True)
                    ins.then_inc(gateb_psum, 1)

            def down(src, base, stages):
                for s in range(stages):
                    w = arrived(base + s)
                    for kk in range(2):
                        k = 2 * s + kk
                        for g in range(G):
                            for hf in range(2):
                                ins = pe.matmul(ps[:, YB + 2 * g + hf, :], tokens(src, k, g),
                                                w[:, kk * D + hf * 512:kk * D + (hf + 1) * 512],
                                                start=(k == 0), stop=(k == 2 * stages - 1))
                    ins.then_inc(stage_used, 1)

            pe.wait_ge(og_ready, ITS)
            gate_rows(0)
            pe.wait_ge(num_used, ITS)
            pe.wait_ge(qc_used, ITS)
            pe.wait_ge(gateb_ready, 4)
            down(so, ST_OUT, N_OUT)
            gate_rows(1)
            norm_turn(1)
            pe.wait_ge(gateb_ready, 8)

            def ffn(src, nt, first, turn0, fc0):
                def up_part(c):
                    sl = slot(first + c)
                    pe.wait_ge(loaded[sl], turn0 + 16 * ((first + c) // SLOTS - first // SLOTS))
                    w = ring[:, sl, :]
                    if c >= 2:
                        pe.wait_ge(act_done, fc0 + (c - 1))
                    for j in range(2):
                        for k in range(KD):
                            ins = pe.matmul(ps[:, UB + c % 2, j * nt:(j + 1) * nt],
                                            w[:, (j * KD + k) * P:(j * KD + k + 1) * P], src[:, k, :],
                                            start=(k == 0), stop=(k == KD - 1))
                    ins.then_inc(u_done, 1)

                def down_part(c):
                    w = ring[:, slot(first + c), :]
                    pe.wait_ge(act_done, fc0 + (c + 1))
                    for g in range(nt // P):
                        for hf in range(2):
                            ins = pe.matmul(ps[:, YB + 2 * g + hf, :], fact[:, c % 2, g * P:(g + 1) * P],
                                            w[:, 2 * D + hf * 512:2 * D + (hf + 1) * 512],
                                            start=(c == 0), stop=(c == FC - 1))
                    ins.then_inc(stage_used, 1)

                up_part(0)
                for c in range(1, FC):
                    up_part(c)
                    down_part(c - 1)
                down_part(FC - 1)

            ffn(hT, T, ST_FF, 16 * (ST_FF // SLOTS + 1), 0)
            gate_rows(2)
            norm_turn(2)
            pe.wait_ge(gateb_ready, 12)

            def square_sum(s):
                pe.wait_ge(sq_ready, s + 1)
                pe.matmul(ps[:, YB, 0:T], ones, sqb[:, s % 2, :], start=(s == 0), stop=(s == N_PW1 - 1)
                          ).then_inc(ssq_done, 1)

            for s in range(N_PW1):
                w = arrived(pw1_stage(s))
                if s >= 2:
                    pe.wait_ge(glu_done, s - 1)
                for j in range(2):
                    for k in range(KD):
                        ins = pe.matmul(ps[:, UB + s % 2, j * T:(j + 1) * T], w[:, (j * KD + k) * P:(j * KD + k + 1) * P],
                                        hT[:, k, :], start=(k == 0), stop=(k == KD - 1))
                ins.then_inc(stage_used, 1)
                while a < ada_beside(s):
                    ada(a, ada_stage(a))
                    a += 1
                if s >= 2:
                    square_sum(s - 2)
            square_sum(N_PW1 - 2)
            square_sum(N_PW1 - 1)
            pe.wait_ge(zs_ready, 1)
            down(z, ST_PW2, N_PW2)
            gate_rows(3)
            norm_turn(3)
            pe.wait_ge(gateb_ready, 14)
            for g in range(G):
                for k in range(KD):
                    ins = pe.matmul(ps[:, MISC, g * EXPERTS:(g + 1) * EXPERTS], tokens(hT, k, g), wr[:, k, :],
                                    start=(k == 0), stop=(k == KD - 1))
            ins.then_inc(route_psum, 1)
            pe.wait_ge(gateb_ready, 16)
            for g in range(G):
                for b in range(2):
                    for i in range(4):
                        ins = pe.transpose(ps[:, YB + 2 * g + b, i * P:(i + 1) * P], tokens(hT, 4 * b + i, g), ident)
                    ins.then_inc(htok_psum, 1)
            pe.wait_ge(sel_ready, 1)
            for g in range(G):
                pe.matmul(ps[:, MISC, g * EXPERTS:(g + 1) * EXPERTS], tri, sel[:, g, :], start=True, stop=(g == 0))
                if g == 1:
                    pe.matmul(ps[:, MISC, g * EXPERTS:(g + 1) * EXPERTS], ones, sel[:, 0, :], start=False, stop=True)
            for g in range(G):
                ins = pe.matmul(ps[:, MISC, G * EXPERTS:(G + 1) * EXPERTS], ones, sel[:, g, :], start=(g == 0),
                                stop=(g == G - 1))
            ins.then_inc(pos_psum, 1)

            def gather(i):
                pe.wait_ge(pick_ready, i + 1)
                for k in range(KD):
                    for g in range(G):
                        ins = pe.matmul(ps[:, UB + k // 4, (k % 4) * P:(k % 4 + 1) * P], htok[:, g, k * P:(k + 1) * P],
                                        pick[:, g, :], start=(g == 0), stop=(g == G - 1))
                ins.then_inc(gathered, 1)

            def scatter(i, n):
                if n == 0:
                    pe.wait_ge(y_ready, i + 1)
                    pe.wait_ge(back_ready, i + 1)
                pe.wait_ge(acc_added, i * 4 + (n + 1))
                pe.matmul(ps[:, 7, :], back[:, n // 2, :], y_sb[:, (n % 2) * 512:(n % 2 + 1) * 512],
                          start=True, stop=True).then_inc(scattered, 1)

            def product(out, hi, lo, w, start, stop):
                pe.matmul(out, hi, w_hi[:, w[0], w[1]:w[1] + ROW], start=start, stop=False)
                pe.matmul(out, hi, w_lo[:, w[0], w[1]:w[1] + ROW], start=False, stop=False)
                return pe.matmul(out, lo, w_hi[:, w[0], w[1]:w[1] + ROW], start=False, stop=stop)

            pe.wait_ge(htok_ready0, 2)
            pe.wait_ge(htok_ready1, 2)
            gather(0)
            pe.wait_ge(plan_ready, 1)
            items = pe.value_load(plan[0:1, 0:1], min_val=EXPERTS, max_val=ITEMS)
            with pe.Fori(0, items) as i:
                pe.wait_ge(hg_ready, i + 1)
                for r, (kind, q, k, half) in enumerate(EXPERT_ROWS):
                    s = r // CUT
                    if r % CUT == 0:
                        pe.wait_ge(split_ready, i * CUTS + (s + 1))
                    w = (s % W_BUFS, (r % CUT) * ROW)
                    if kind == "down":
                        if (k, half) == (0, 0):
                            pe.wait_ge(hid_ready, i * GROUPS + (q + 1))
                            if q == 0:
                                pe.wait_ge(y_ready, i + 1)
                        c = slice(k * P, (k + 1) * P)
                        ins = product(ps[:, YB + half, :], hid_hi[:, q % 2, c], hid_lo[:, q % 2, c], w,
                                      (q, k) == (0, 0), (q, k) == (GROUPS - 1, GC - 1))
                    else:
                        ins = product(ps[:, 2 * (q % 2) + (kind == "up"), :], hg_hi[:, k, :], hg_lo[:, k, :], w,
                                      k == 0, k == KD - 1)
                    if r % CUT == CUT - 1:
                        ins.then_inc(stage_used, 1)
                    if r in UP_END:
                        ins.then_inc(u_done, 1)
                    if r in TURN_ROW:
                        t = TURN_ROW.index(r)
                        pe.wait_ge(act_done, i * GROUPS + (FC + t + 1))
                        for c in range(GC):
                            ins = pe.transpose(ps[:, 6, c * P:(c + 1) * P], hid[:, c * P:(c + 1) * P], ident)
                        ins.then_inc(hid_turned, 1)
                    if r in SCATTER_ROWS:
                        scatter(i, SCATTER_ROWS.index(r))
                    if r == BACK_ROW:
                        pe.wait_ge(acc_added, i * 4 + 5)
                        for g in range(G):
                            ins = pe.transpose(ps[:, 7, g * P:(g + 1) * P], pick_w[:, g, :], ident)
                        ins.then_inc(picks_used, 1)
                    if r == GATHER_ROW:
                        gather(i + 1)
            for n in range(4):
                scatter(items, n)


_INPUTS = ("vecs", "consts", "rowc", "x_in", "pos", "w_gate", "w_router", "mix", "ff", "moe", "c0", "norm_out")
_OUTPUTS = (("y_out", (P, G, D)), ("c_out", (HEADS, P, DIR, DVA)), ("m_out", (ROWS, 1)))


def _constants():
    cst = np.zeros((P, C_ALL), np.float32)
    cst[:, C_ID:C_ID + P] = np.eye(P)
    cst[:, C_ONE:C_ONE + P] = 1.0
    j, t = np.arange(P)[:, None], np.arange(P)[None, :]
    cst[:, C_MASK:C_MASK + P] = np.where(j <= t, 0.0, BIG)
    cst[:, C_MASK + P:C_MASK + 2 * P] = np.where(j >= t, 0.0, BIG)
    cst[:, C_DESC:C_DESC + G * EXPERTS] = np.tile(np.arange(EXPERTS, 0, -1), G)
    cst[:, C_EPS] = EPS
    cst[:, C_TRI:C_TRI + P] = np.where(j < t, 1.0, 0.0)
    cst[:, C_IOTA:C_IOTA + P] = t
    grid_w = 64
    r = np.repeat(np.arange(P // grid_w, dtype=np.float32), grid_w)
    c = np.tile(np.arange(grid_w, dtype=np.float32), P // grid_w)
    quarter = D // 4
    freqs = (np.float32(10000.0) ** (-np.arange(quarter, dtype=np.float32) / quarter)).astype(np.float32)
    ar, ac = r[:, None] * freqs, c[:, None] * freqs
    pos = np.zeros((P, D), np.float32)
    pos[:, :] = np.concatenate([np.sin(ar), np.cos(ar), np.sin(ac), np.cos(ac)], axis=-1)
    return cst, pos


def kernel(**inputs):
    import concourse.bacc as bacc
    from concourse.bass_utils import run_bass_kernel_spmd

    a = {k: np.asarray(v) for k, v in inputs.items()}

    def chunks(v):
        return v.reshape(-1, P).T

    cond = np.stack([a["c_ctx"], a["c"][0]], axis=0).reshape(G, KD, P).transpose(2, 1, 0).reshape(P, KD * G)
    vecs = np.concatenate([chunks(a["b_ada"]), chunks(a["norm_mix"]), chunks(a["norm_ffn"]), chunks(a["a_gn"]),
                           chunks(a["b_b_dw"]), chunks(a["b_norm"]), chunks(a["a_w_conv"]), chunks(a["b_w_dw"]),
                           cond], axis=1)
    consts, pos = _constants()
    rowc = np.zeros((ROWS, 4), np.float32)
    w_gate = np.zeros((P, KD, 2, ROWS), np.float32)
    gw = a["a_w_in"][0][:, 6144:].reshape(KD, P, 4, HEADS).transpose(1, 0, 2, 3)
    for d in range(DIR):
        rowc[32 * d:32 * d + HEADS, 0] = a["a_b_gate"][0, 2 * d]
        rowc[32 * d:32 * d + HEADS, 1] = a["a_b_gate"][0, 2 * d + 1]
        rowc[32 * d:32 * d + HEADS, 2] = a["state_m"][0, 0, d]
        w_gate[:, :, 0, 32 * d:32 * d + HEADS] = gw[:, :, 2 * d]
        w_gate[:, :, 1, 32 * d:32 * d + HEADS] = gw[:, :, 2 * d + 1]

    def columns(w, width):
        n = w.shape[1] // width
        return w.reshape(KD, P, n, width).transpose(2, 1, 0, 3).reshape(n, P, KD * width)

    def rows_of(w, per):
        n = w.shape[0] // P // per
        return w.reshape(n, per, P, D).transpose(0, 2, 1, 3).reshape(n, P, per * D)

    ada = np.concatenate([columns(a["w_ada"][0], 256), columns(a["w_ada"][1], 256)])
    pw1 = a["b_w_pw1"][0]
    pw1 = np.concatenate([columns(pw1[:, :D], P), columns(pw1[:, D:], P)], axis=2)
    beside = [part for s in range(N_PW1) for part in (pw1[s:s + 1], ada[ada_beside(s - 1):ada_beside(s)])]
    mix = np.concatenate([ada[:ADA_FIRST], columns(a["a_w_in"][0][:, :6144], 256),
                          ada[ADA_FIRST:ADA_FIRST + ADA_MID], rows_of(a["a_w_out"][0], 2), *beside,
                          rows_of(a["b_w_pw2"][0], 2)])

    def swiglu(w1, w2):
        return np.concatenate([columns(w1[:, :FF], P), columns(w1[:, FF:], P), rows_of(w2, 1)], axis=2)

    ff = swiglu(a["ff_w1"][0], a["ff_w2"][0])
    moe = np.empty((EXPERTS, FC, P, PER, ROW), np.float32)
    for e in range(EXPERTS):
        w1 = a["moe_w1"][0, e].reshape(KD, P, 2, GROUPS, ROW)
        w2 = a["moe_w2"][0, e].reshape(GROUPS, GC, P, 2, ROW)
        for r, (kind, q, k, half) in enumerate(EXPERT_ROWS):
            moe[e, r // PER, :, r % PER] = w2[q, k, :, half] if kind == "down" else w1[k, :, int(kind == "up"), q]
    moe = moe.reshape(EXPERTS * FC, P, STAGE)
    c0 = np.concatenate([a["state_C"][0, 0], a["state_n"][0, 0][..., None]], axis=-1).transpose(1, 2, 0, 3)
    arrays = dict(vecs=vecs, consts=consts, rowc=rowc,
                  x_in=np.stack([a["x_prompt"][0], a["x_sample"][0]], axis=1), pos=pos, w_gate=w_gate,
                  w_router=a["moe_router"][0].reshape(KD, P, EXPERTS).transpose(1, 0, 2), mix=mix, ff=ff, moe=moe,
                  c0=c0, norm_out=np.broadcast_to(a["norm_out"], (P, D)))
    arrays = {k: np.ascontiguousarray(v) for k, v in arrays.items()}

    nc = bacc.Bacc("TRN2", target_bir_lowering=False, num_devices=1)
    f32 = mybir.dt.float32
    args = [nc.dram_tensor(k, arrays[k].shape, f32, kind="ExternalInput").ap() for k in _INPUTS]
    args += [nc.dram_tensor(k, s, f32, kind="ExternalOutput").ap() for k, s in _OUTPUTS]
    mlstm_conformer_kernel(nc, *args)
    r = run_bass_kernel_spmd(nc, [arrays], core_ids=[0]).results[0]
    y, c, m = (np.asarray(r[k]) for k, _ in _OUTPUTS)
    state = c.transpose(2, 0, 1, 3)
    m2 = np.stack([m[32 * d:32 * d + HEADS, 0] for d in range(DIR)])
    return (np.ascontiguousarray(y[:, 0])[None], np.ascontiguousarray(y[:, 1])[None],
            np.ascontiguousarray(state[..., :DV])[None, None], np.ascontiguousarray(state[..., DV])[None, None],
            m2[None, None])
```

```python
import numpy as np
import concourse.bass as bass
from concourse import mybir
from contextlib import ExitStack

P = 128
D = 1024
KD = D // P
G = 2
T = G * P
HEADS = 8
DV = 256
DVA = DV + 1
DIR = 2
FF = 3584
FC = FF // P
EXPERTS = 8
A_TAPS, B_TAPS = 5, 31
EPS = 1e-6
WORK = 17040
Q_SCALE = float(P) ** -0.5
ROWS = 32 * (DIR - 1) + HEADS
BIG = 1e30

SLOTS = 7
STAGE = 3072
MIX = 2048
ADA_STAGES = 2 * 6 * D // 256
ADA_FIRST = 8
ST_IN = ADA_FIRST
N_IN = 24
ST_ADA = ST_IN + N_IN
ADA_LAST = 3 * 4
ADA_MID = ADA_STAGES - ADA_FIRST - ADA_LAST
ST_OUT = ST_ADA + ADA_MID
N_OUT = 8
ST_FF = ST_OUT + N_OUT
ST_PW1 = ST_FF + FC
N_PW1 = 8


def ada_beside(s):
    return ADA_FIRST + ADA_MID + ADA_LAST * (s + 1) // N_PW1


def pw1_stage(s):
    return ST_PW1 + s + (ada_beside(s - 1) - ADA_FIRST - ADA_MID)


ST_PW2 = ST_PW1 + N_PW1 + ADA_LAST
N_PW2 = 4
ST_MOE = ST_PW2 + N_PW2

ROW = 512
GROUPS = FF // ROW
GC = ROW // P
PER = STAGE // ROW
EXPERT_ROWS = []
for _q in range(GROUPS):
    EXPERT_ROWS += [("gate", _q, _k, 0) for _k in range(KD)] + [("up", _q, _k, 0) for _k in range(KD)]
    if _q:
        EXPERT_ROWS += [("down", _q - 1, _c, _h) for _c in range(GC) for _h in range(2)]
EXPERT_ROWS += [("down", GROUPS - 1, _c, _h) for _c in range(GC) for _h in range(2)]
assert len(EXPERT_ROWS) == FC * PER
UP_END = [EXPERT_ROWS.index(("up", _q, KD - 1, 0)) for _q in range(GROUPS)]
TURN_ROW = [UP_END[_q] + (8 if _q < GROUPS - 1 else 5) for _q in range(GROUPS)]
SCATTER_ROWS = [40, 46, 52, 58]
BACK_ROW = 66
GATHER_ROW = 156


CUT = 3
CUTS = len(EXPERT_ROWS) // CUT
W_BUFS = 4
FF_CUTS = 2 * FC
FRONT = CUT * ROW // P


def behind(row):
    return min(row // CUT + W_BUFS, CUTS)


ITS = G * HEADS

V_ADA = 0
V_NMIX = V_ADA + 2 * 6 * KD
V_NFFN = V_NMIX + 2 * KD
V_GN = V_NFFN + 2 * KD
V_BDW = V_GN + 2 * KD
V_BNORM = V_BDW + KD
V_ACONV = V_BNORM + KD
V_BCONV = V_ACONV + A_TAPS * 2 * KD
V_COND = V_BCONV + B_TAPS * KD
V_ALL = V_COND + KD * G
C_ID = 0
C_ONE = P
C_MASK = 2 * P
C_DESC = C_MASK + DIR * P
C_EPS = C_DESC + G * EXPERTS
C_TRI = C_EPS + 1
C_IOTA = C_TRI + P
C_ALL = C_IOTA + P

OVER = (2 * G * P - 1) // (P + 1)
ITEMS = EXPERTS + OVER
COLS = ITEMS + 1


def mlstm_conformer_kernel(nc, vecs, consts, rowc, x_in, pos, w_gate, w_router, mix, ff, moe, c0, norm_out,
                           y_out, c_out, m_out):
    f32 = mybir.dt.float32
    ALU = mybir.AluOpType
    ACT = mybir.ActivationFunctionType
    X = mybir.AxisListType.X

    ctx = ExitStack()
    with ctx:
        def sb(name, *shape):
            return ctx.enter_context(nc.sbuf_tensor(name, list(shape), f32))

        def sem(name):
            return ctx.enter_context(nc.semaphore(name))

        ring = sb("ring", P, SLOTS, STAGE)
        x = sb("x", P, G, D)
        xn = sb("xn", P, G, D)
        hT = sb("hT", P, KD, T)
        gate_b = sb("gate_b", P, G * D)
        so = sb("so", P, 2 * HEADS, T)
        vec = sb("vec", P, V_ALL)
        cst = sb("cst", P, C_ALL)
        rc = sb("rc", ROWS, 4)
        wg = so[:, :, :].rearrange("p c t -> p (c t)")[:, 0:KD * 2 * ROWS].rearrange("p (k w r) -> p k w r", k=KD, w=2)
        wr = sb("wr", P, KD, EXPERTS)
        silu_c = sb("silu_c", P, KD * G)
        ce = sb("ce", P, KD * G)
        cd = sb("cd", P, KD * G)
        mod = sb("mod", P, 12, KD, G)
        scl = sb("scl", P, 4, KD, G)
        ss = sb("ss", P, G)
        rstd = sb("rstd", P, G)
        lnv = sb("lnv", P, G)
        small = sb("small", P, 16)
        root = sb("root", P, 4, G)
        f32r = mybir.dt.float32r
        first = ExitStack()
        plan_f = sb("plan_f", P, 8)
        plan = ctx.enter_context(nc.sbuf_tensor("plan", [1, 8], mybir.dt.int32))
        work = first.enter_context(nc.sbuf_tensor("work", [P, WORK], f32))
        at = [0]

        def carve(*shape, rows=P):
            n = int(np.prod(shape))
            a = work[0:rows, at[0]:at[0] + n]
            at[0] += n
            assert at[0] <= WORK
            if len(shape) == 1:
                return a
            names = "abcd"[:len(shape)]
            return a.rearrange(f"p ({' '.join(names)}) -> p {' '.join(names)}",
                               **{k: v for k, v in zip(names, shape)})

        qkT = carve(2 * HEADS, T)
        vaug = carve(G, HEADS, DVA)
        c0b = carve(2, DIR, DVA)
        stc = carve(2, DIR, DVA)
        row = carve(8, P, rows=ROWS)
        nat = carve(8, P, rows=ROWS)
        col = carve(6, ROWS)
        kscale = carve(2, ROWS)
        kw = carve(DIR, P)
        qcs = carve(DIR, DVA)
        nm = carve(DIR, DVA)
        h0 = carve(DV)
        hs = carve(DV)
        hn = carve(DV)
        hsq = carve(DV)
        shared = at[0]
        tmp = carve(2, DIR, P)
        pe_ = carve(2, DIR, P)
        sT = carve(2, DIR, P)
        at[0] = shared
        ca = carve(2, 2, T)
        eq = carve(2, 2, T)
        rt = xn[0:ROWS, :, :].rearrange("p g d -> p (g d)").rearrange("p (n g t) -> p n g t", g=G, t=P)
        pad = gate_b[:, 0:2 * 2 * G * (P + A_TAPS - 1)].rearrange("p (b j g t) -> p b j g t", b=2, j=2, g=G)
        at[0] = 0
        fe = carve(2, T)
        fd = carve(T)
        pad31 = carve(KD, G, P + B_TAPS - 1)
        cv = carve(KD, T)
        odd = carve(T)
        z = carve(KD, T)
        ez = carve(KD, T)
        sqb = carve(2, T)
        rb = carve(T)
        assert at[0] <= WORK
        at[0] = 0
        work = so[:, :, :].rearrange("p c t -> p (c t)")
        ff_th = carve(2, T)
        ff_sg = carve(2, T)
        fact = carve(2, T)
        at[0] = 0
        acc = carve(G, D)
        y_sb = carve(D)
        pick = carve(G, P)
        pick_w = carve(G, P)
        back = carve(G, P)
        lg = carve(G, EXPERTS)
        l2 = carve(G, EXPERTS)
        oh = carve(2, G, EXPERTS)
        key = carve(G, EXPERTS)
        tk = carve(9, G)
        sel = carve(G, EXPERTS)
        item_pos = carve(G, COLS)
        item_comb = carve(G, COLS)
        over = carve(4, EXPERTS)
        assert at[0] <= 2 * HEADS * T
        at[0] = 0
        work = hT[:, :, :].rearrange("p k t -> p (k t)")
        gain_out = work[:, 0:D]
        th = carve(ROW)
        sg = carve(ROW)
        hid_tok = carve(ROW)
        more = OVER + 1
        hit = carve(more, EXPERTS)
        hit_desc = carve(more, EXPERTS)
        prod = carve(G, more, EXPERTS)
        prod_comb = carve(G, more, EXPERTS)
        has, who, first_slots = carve(more), carve(more), carve(G, more)
        gate = gate_b[:, 0:G * D].rearrange("p (g d) -> p g d", g=G)
        ident = cst[:, C_ID:C_ID + P]
        ones = cst[:, C_ONE:C_ONE + P]
        mask = cst[:, C_MASK:C_MASK + DIR * P].rearrange("p (d t) -> p d t", d=DIR)
        desc = cst[:, C_DESC:C_DESC + G * EXPERTS].rearrange("p (g e) -> p g e", g=G)
        eps = cst[:, C_EPS:C_EPS + 1]
        tri = cst[:, C_TRI:C_TRI + P]
        iota = cst[:, C_IOTA:C_IOTA + P]
        htok = xn
        first.close()

        def part(name, *shape):
            return ctx.enter_context(nc.sbuf_tensor(name, list(shape), f32r))

        w_hi, w_lo = part("w_hi", P, W_BUFS, CUT * ROW), part("w_lo", P, W_BUFS, CUT * ROW)
        hg = part("hg", P, 2, KD, P)
        hg_hi, hg_lo = hg[:, 0, :, :], hg[:, 1, :, :]
        hid = part("hid", P, 4, ROW)
        hid_hi, hid_lo = hid[:, 0:2, :], hid[:, 2:4, :]
        hT_hi = hg[:, :, :, :].rearrange("p a k t -> p (a k t)").rearrange("p (k t) -> p k t", t=T)
        hT_lo = [hid[:, 2:4, :].rearrange("p a (k t) -> p (a k) t", t=T), part("hT_lo", P, KD // 2, T)[:, :, :]]
        ff_hi, ff_lo = (hid[:, _n, :].rearrange("p (c t) -> p c t", t=T) for _n in range(2))

        ps = ctx.enter_context(nc.psum_tensor("ps", [P, 8, 512], f32))
        MODB, MISC, UB, YB, QB = 0, 1, 2, 4, 6
        LAST_BANKS = 0, 1, 7, 6

        vec_in, cst_in, x_in_s, pos_in, late_in = sem("vec_in"), sem("cst_in"), sem("x_in_s"), sem("pos_in"), sem("late_in")
        no_in = sem("no_in")
        loaded = [sem(f"loaded{i}") for i in range(SLOTS)]
        stage_used = sem("stage_used")
        cond_exp, cond_ready = sem("cond_exp"), sem("cond_ready")
        dve_chain, act_chain = sem("dve_chain"), sem("act_chain")
        x_ready, ss_ready, rstd_ready, hs_squared = sem("x_ready"), sem("ss_ready"), sem("rstd_ready"), sem("hs_squared")
        xn0_ready, xn1_ready, turned = sem("xn0_ready"), sem("xn1_ready"), sem("turned")
        hT0_ready, hT1_ready = sem("hT0_ready"), sem("hT1_ready")
        mod_ready = sem("mod_ready")
        gates_psum, gate_raw, gate_abs, gate_ln = sem("gates_psum"), sem("gate_raw"), sem("gate_abs"), sem("gate_ln")
        gate_M, gate_exps, nat_ready, cols_psum, cols_ready = (sem("gate_M"), sem("gate_exps"), sem("nat_ready"),
                                                               sem("cols_psum"), sem("cols_ready"))
        memsets = sem("memsets")
        proj_out, conv_done, qk_exp, qk_done, so_ready = (sem("proj_out"), sem("conv_done"), sem("qk_exp"),
                                                          sem("qk_done"), sem("so_ready"))
        front, tmp_ready, p_ready, s_ready, kw_ready = (sem("front"), sem("tmp_ready"), sem("p_ready"),
                                                        sem("s_ready"), sem("kw_ready"))
        num_done, qc_used, num_used, hn_ready = sem("num_done"), sem("qc_used"), sem("num_used"), sem("hn_ready")
        c0_in = [sem("c0_in0"), sem("c0_in1")]
        c_stored = [sem("c_stored0"), sem("c_stored1")]
        m_stored, m_ready, y_stored = sem("m_stored"), sem("m_ready"), sem("y_stored")
        hT_back, og_ready = sem("hT_back"), sem("og_ready")
        gateb_psum, gateb_ready = sem("gateb_psum"), sem("gateb_ready")
        u_done, e_done, act_done = sem("u_done"), sem("e_done"), sem("act_done")
        glu_exp, glu_done, cv_ready, sq_ready, ssq_done = (sem("glu_exp"), sem("glu_done"), sem("cv_ready"),
                                                           sem("sq_ready"), sem("ssq_done"))
        rb_ready, z_ready, ez_ready, zs_ready = sem("rb_ready"), sem("z_ready"), sem("ez_ready"), sem("zs_ready")
        route_psum, route_gap, route_exp = sem("route_psum"), sem("route_gap"), sem("route_exp")
        fin_ready = sem("fin_ready")
        sel_ready, pos_psum, plan_ready = sem("sel_ready"), sem("pos_psum"), sem("plan_ready")
        htok_psum, htok_ready0, htok_ready1 = sem("htok_psum"), sem("htok_ready0"), sem("htok_ready1")
        pick_ready, gathered, picks_used = sem("pick_ready"), sem("gathered"), sem("picks_used")
        hg_hi_ready, hg_ready, back_ready = sem("hg_hi_ready"), sem("hg_ready"), sem("back_ready")
        y_ready, scattered, acc_added = sem("y_ready"), sem("scattered"), sem("acc_added")
        hi_ready, split_ready, front_used = sem("hi_ready"), sem("split_ready"), sem("front_used")
        hT_hi_ready, hT_lo_ready = sem("hT_hi_ready"), sem("hT_lo_ready")
        hid_turned, hid_hi_ready, hid_ready = sem("hid_turned"), sem("hid_hi_ready"), sem("hid_ready")

        block = ctx.enter_context(nc.Block())

        def slot(n):
            return n % SLOTS

        def ada_stage(a):
            if a < ADA_FIRST:
                return a
            if a < ADA_FIRST + ADA_MID:
                return ST_ADA + a - ADA_FIRST
            s = next(s for s in range(N_PW1) if a < ada_beside(s))
            return pw1_stage(s) + 1 + a - ada_beside(s - 1)

        def ada_through(it):
            return ADA_FIRST + ADA_MID * (it + 1) // ITS

        @block.sync
        def _(sp):
            def load(src, base, count, width, first=0):
                def one(n, row, j):
                    sp.wait_ge(stage_used, n - SLOTS + 1)
                    sp.dma_start(ring[:, slot(base + j), 0:width],
                                 src[bass.ds(row, 1), :, :].rearrange("o p n -> (o p) n")
                                 ).then_inc(loaded[slot(base + j)], 16)
                turns = count // SLOTS
                if turns > 1:
                    with sp.Fori(0, turns) as i:
                        for j in range(SLOTS):
                            one(i * SLOTS + (base + j), i * SLOTS + (first + j), j)
                else:
                    turns = 0
                for j in range(turns * SLOTS, count):
                    one(base + j, first + j, j)

            sp.dma_start(vec[:, :], vecs).then_inc(vec_in, 16)
            for n in range(SLOTS):
                if n == 2:
                    sp.dma_start(x[:, :, :], x_in).then_inc(x_in_s, 16)
                    sp.dma_start(gate[:, 1, :], pos).then_inc(pos_in, 16)
                    sp.dma_start(cst[:, :], consts).then_inc(cst_in, 16)
                sp.dma_start(ring[:, n, 0:MIX], mix[n]).then_inc(loaded[n], 16)
            load(mix, SLOTS, ST_FF - SLOTS, MIX, SLOTS)
            load(ff, ST_FF, FC, STAGE)
            load(mix, ST_PW1, ST_MOE - ST_PW1, MIX, ST_FF)
            def expert_stage(m, row, j):
                sp.dma_start(ring[:, slot(ST_MOE + j), :], moe[bass.ds(row, 1), :, :].rearrange("o p n -> (o p) n")
                             ).then_inc(loaded[slot(ST_MOE + j)], 16)

            for m in range(SLOTS):
                sp.wait_ge(stage_used, ST_MOE + m - SLOTS + 1)
                expert_stage(m, m, m)
            with sp.Fori(1, (EXPERTS - 1) * FC // SLOTS) as i:
                for j in range(SLOTS):
                    sp.wait_ge(split_ready, i * (2 * SLOTS) + (FF_CUTS + 2 * (j - SLOTS + 1)))
                    expert_stage(i * SLOTS + j, i * SLOTS + j, j)
            sp.wait_ge(plan_ready, 1)
            items = sp.value_load(plan[0:1, 7:8], min_val=1, max_val=1 + OVER)
            with sp.Fori(0, items) as k:
                e = sp.value_load(plan[0:1, bass.ds(k + 1, 1)], min_val=0, max_val=EXPERTS - 1)
                with sp.Fori(0, FC // SLOTS) as i:
                    for j in range(SLOTS):
                        sp.wait_ge(split_ready, k * CUTS + i * (2 * SLOTS)
                                   + (FF_CUTS + (EXPERTS - 1) * CUTS + 2 * (j - SLOTS + 1)))
                        expert_stage(None, e * FC + i * SLOTS + j, j)

        @block.gpsimd
        def _(pool):
            pool.memset(vaug[:, :, :, DV:DVA], 1.0).then_inc(memsets, 1)
            pool.wait_ge(x_ready, 1)
            pool.memset(pad[:, :, :, :, 0:2], 0.0).then_inc(memsets, 1)
            pool.memset(pad[:, :, :, :, P + 2:P + 4], 0.0).then_inc(memsets, 1)
            for h in range(HEADS):
                if h >= 2:
                    pool.wait_ge(num_done, 2 * (h - 2) + 2)
                pool.dma_start(c0b[:, h % 2, :, :], c0[h]).then_inc(c0_in[h % 2], 16)
            pool.wait_ge(x_ready, 3)
            pool.memset(pad31, 0.0).then_inc(memsets, 1)
            pool.memset(acc, 0.0).then_inc(acc_added, 1)
            pool.memset(back, 0.0).then_inc(back_ready, 1)

        @block.scalar
        def _(act):
            n_chain = [0]

            def link(ins):
                n_chain[0] += 1
                ins.then_inc(act_chain, 1)
                act.wait_ge(act_chain, n_chain[0])

            act.wait_ge(vec_in, 16)
            act.activation(ce[:, :], vec[:, V_COND:V_COND + KD * G], ACT.Exp, scale=-1.0).then_inc(cond_exp, 1)
            act.wait_ge(pos_in, 16)
            act.dma_start(wg, w_gate).then_inc(late_in, 16)
            act.dma_start(rc[:, :], rowc).then_inc(late_in, 16)
            act.dma_start(wr[:, :, :], w_router).then_inc(late_in, 16)

            def square_sum(q):
                act.wait_ge(x_ready, q + 1)
                act.activation(xn[:, 0, :], x[:, 0, :], ACT.Square, accum_out=ss[:, 0:1]).then_inc(ss_ready, 1)
                act.wait_ge(rstd_ready, q + 1)

            def norm_turn(q):
                square_sum(q)
                act.activation(xn[:, 0, :], x[:, 0, :], ACT.Copy, scale=rstd[:, 0:1]).then_inc(xn0_ready, 1)
                for b in range(2):
                    act.wait_ge(turned, 4 * q + b + 1)
                    if b == 0:
                        act.wait_ge(mod_ready, 2 * (3 * q + 2))
                    for i in range(4):
                        k = 4 * b + i
                        act.activation(hT[:, k, 0:P], ps[:, YB + b, i * P:(i + 1) * P], ACT.Identity,
                                       scale=scl[:, q, k, 0:1], bias=mod[:, 3 * q, k, 0:1]).then_inc(hT0_ready, 1)

            def gate_copies(q):
                for i in range(4):
                    act.wait_ge(gateb_psum, 4 * q + i + 1)
                    if i == 0:
                        act.wait_ge(x_ready, q + 1)
                    act.activation(gate[:, i // 2, (i % 2) * 512:(i % 2 + 1) * 512], ps[:, i, :],
                                   ACT.Copy).then_inc(gateb_ready, 1)

            act.wait_ge(cst_in, 16)
            norm_turn(0)

            act.wait_ge(late_in, 48)
            act.wait_ge(gates_psum, 1)
            for w in range(2):
                act.activation(rt[:, w, :, :], ps[0:ROWS, MISC, w * T:(w + 1) * T], ACT.Identity,
                               bias=rc[:, w:w + 1]).then_inc(gate_raw, 1)
            act.wait_ge(gate_abs, 1)
            link(act.activation(rt[:, 5, :, :], rt[:, 4, :, :], ACT.Exp))
            act.activation(rt[:, 6, :, :], rt[:, 5, :, :], ACT.Ln, bias=cst[0:ROWS, C_ONE:C_ONE + 1]).then_inc(gate_ln, 1)
            act.wait_ge(gate_M, 1)
            act.activation(row[:, 2:4, :], rt[:, 4, :, :], ACT.Exp, scale=-1.0).then_inc(gate_exps, 1)
            act.activation(row[:, 4, :], row[:, 7, :], ACT.Exp, scale=-1.0, bias=rc[:, 2:3]).then_inc(gate_exps, 1)
            act.activation(row[:, 5, :], row[:, 0, :], ACT.Exp, bias=small[0:ROWS, 0:1]).then_inc(gate_exps, 1)

            def silu_exp(s):
                act.wait_ge(conv_done, s + 1)
                if s >= 2:
                    act.wait_ge(qk_done, s - 1)
                act.activation(eq[:, s % 2, :, :], ca[:, s % 2, :, :], ACT.Tanh, scale=0.5).then_inc(qk_exp, 1)

            for s in range(N_IN):
                b = UB + s % 2
                act.wait_ge(stage_used, ST_IN + s + 1)
                if s < HEADS:
                    if s == 0:
                        act.wait_ge(memsets, 3)
                    if s >= 2:
                        act.wait_ge(conv_done, s - 1)
                    act.activation(pad[:, s % 2, 0, :, 2:P + 2], ps[:, b, 0:T].rearrange("p (g t) -> p g t", g=G), ACT.Copy)
                    act.activation(pad[:, s % 2, 1, :, 2:P + 2], ps[:, b, T:2 * T].rearrange("p (g t) -> p g t", g=G),
                                   ACT.Copy).then_inc(proj_out, 1)
                elif s < 2 * HEADS:
                    act.activation(vaug[:, :, s - HEADS, 0:DV], ps[:, b, :].rearrange("p (g v) -> p g v", g=G),
                                   ACT.Copy).then_inc(proj_out, 1)
                else:
                    i = 2 * (s - 2 * HEADS)
                    act.activation(so[:, i:i + 2, :], ps[:, b, :].rearrange("p (c t) -> p c t", c=2), ACT.Tanh,
                                   scale=0.5).then_inc(proj_out, 1)
                if 1 <= s <= HEADS:
                    silu_exp(s - 1)

            def decay_scores(it):
                h, g = it // 2, it % 2
                act.wait_ge(tmp_ready, it + 1)
                if it == 0:
                    act.wait_ge(cols_ready, 1)
                for d in range(DIR):
                    r = 32 * d + h
                    ins = act.activation(pe_[:, it % 2, d, :], tmp[:, it % 2, d, :], ACT.Exp, scale=-1.0,
                                         bias=col[:, g, r:r + 1])
                ins.then_inc(p_ready, 1)

            decay_scores(0)
            for it in range(ITS):
                h, g = it // 2, it % 2
                if it + 1 < ITS:
                    decay_scores(it + 1)
                act.wait_ge(num_done, it + 1)
                if g == 0:
                    if h >= 2:
                        act.wait_ge(c_stored[h % 2], 16 * (h // 2))
                    act.activation(stc[:, h % 2, :, :], ps[:, QB:QB + 2, 0:DVA], ACT.Copy).then_inc(qc_used, 1)
                    act.wait_ge(qc_used, it + 1)
                    act.dma_start(c_out[h], stc[:, h % 2, :, :]).then_inc(c_stored[h % 2], 16)
                else:
                    if it >= 2:
                        act.wait_ge(num_used, it)
                    for d in range(DIR):
                        r = 32 * d + h
                        ins = act.activation(qcs[:, d, :], ps[:, QB + d, 0:DVA], ACT.Copy, scale=kscale[:, 0, r:r + 1])
                    ins.then_inc(qc_used, 1)
                act.wait_ge(num_used, it + 1)
                act.activation(hsq, hs, ACT.Square, accum_out=small[:, 4:5]).then_inc(hs_squared, 1)
                act.wait_ge(hs_squared, it + 1)
            act.wait_ge(m_ready, 1)
            act.dma_start(m_out, small[0:ROWS, 1:2]).then_inc(m_stored, 16)
            gate_copies(0)

            def ff_high(c, j):
                n = ST_FF + c
                act.wait_ge(loaded[slot(n)], 16 * (n // SLOTS + 1))
                if c >= 2:
                    if j == 0:
                        act.wait_ge(front_used, c - 1)
                    else:
                        act.wait_ge(stage_used, ST_FF + c - 1)
                act.activation(w_hi[:, (2 * c + j) % W_BUFS, :], ring[:, slot(n), j * CUT * ROW:(j + 1) * CUT * ROW],
                               ACT.Copy).then_inc(hi_ready, 1)

            act.wait_ge(stage_used, ST_OUT + 1)
            for i in range(2):
                act.wait_ge(c_stored[i], 16 * (HEADS // 2))
            for j in range(2):
                ff_high(0, j)
            norm_turn(1)
            for b in range(2):
                ks = slice(4 * b, 4 * b + 4)
                act.wait_ge(hT0_ready, 8 + 4 * b + 4)
                act.wait_ge(hT1_ready, 8 + 4 * b + 4)
                act.activation(hT_hi[:, ks, :], hT[:, ks, :], ACT.Copy).then_inc(hT_hi_ready, 1)
            gate_copies(1)
            for c in range(FC):
                for j in range(2):
                    if c + 1 < FC:
                        ff_high(c + 1, j)
                    if j == 0:
                        act.wait_ge(u_done, c + 1)
                        act.activation(ff_th[:, c % 2, :], ps[:, UB + c % 2, 0:T], ACT.Tanh, scale=0.5
                                       ).then_inc(e_done, 1)
            norm_turn(2)
            gate_copies(2)

            for s in range(N_PW1):
                act.wait_ge(stage_used, pw1_stage(s) + 1)
                act.activation(fe[:, s % 2, :], ps[:, UB + s % 2, T:2 * T], ACT.Tanh, scale=0.5).then_inc(glu_exp, 1)
                if s >= 1:
                    act.wait_ge(cv_ready, s)
                    if s >= 3:
                        act.wait_ge(ssq_done, s - 2)
                    act.activation(sqb[:, (s - 1) % 2, :], cv[:, s - 1, :], ACT.Square).then_inc(sq_ready, 1)
            act.wait_ge(cv_ready, N_PW1)
            act.wait_ge(ssq_done, N_PW1 - 2)
            act.activation(sqb[:, (N_PW1 - 1) % 2, :], cv[:, N_PW1 - 1, :], ACT.Square).then_inc(sq_ready, 1)
            act.wait_ge(ssq_done, N_PW1)
            link(act.activation(rb, ps[:, YB, 0:T], ACT.Ln, scale=1.0 / D, bias=eps))
            act.activation(rb, rb, ACT.Exp, scale=-0.5).then_inc(rb_ready, 1)
            for k in range(KD):
                act.wait_ge(z_ready, k + 1)
                act.activation(ez[:, k, :], z[:, k, :], ACT.Tanh, scale=0.5).then_inc(ez_ready, 1)
            norm_turn(3)
            gate_copies(3)
            act.wait_ge(route_gap, 1)
            act.activation(tk[:, 3, :], tk[:, 2, :], ACT.Exp).then_inc(route_exp, 1)
            for b in range(2):
                act.wait_ge(htok_psum, b + 1)
                act.activation(htok[:, 0, b * 512:(b + 1) * 512], ps[:, YB + b, :], ACT.Copy).then_inc(htok_ready0, 1)

            def hg_high(i):
                act.wait_ge(gathered, i + 1)
                act.activation(hg_hi, ps[:, UB:UB + 2, :].rearrange("p b (k t) -> p (b k) t", k=4), ACT.Copy
                               ).then_inc(hg_hi_ready, 1)

            def last_output(i):
                act.wait_ge(stage_used, i * CUTS + ST_MOE)
                act.activation(y_sb.rearrange("p (b n) -> p b n", b=2), ps[:, YB:YB + 2, :], ACT.Copy
                               ).then_inc(y_ready, 1)

            hg_high(0)
            act.wait_ge(plan_ready, 1)
            items = act.value_load(plan[0:1, 0:1], min_val=EXPERTS, max_val=ITEMS)
            with act.Fori(0, items) as i:
                for s in range(CUTS + 1):
                    if s == W_BUFS:
                        last_output(i)
                    if s == behind(BACK_ROW):
                        act.wait_ge(picks_used, i + 1)
                        act.activation(back, ps[:, 7, 0:T].rearrange("p (g t) -> p g t", g=G), ACT.Copy
                                       ).then_inc(back_ready, 1)
                    for q in range(GROUPS):
                        if s == behind(UP_END[q]):
                            act.wait_ge(u_done, i * GROUPS + (FC + q + 1))
                            act.activation(th, ps[:, 2 * (q % 2), :], ACT.Tanh, scale=0.5).then_inc(e_done, 1)
                        if s == behind(TURN_ROW[q]):
                            act.wait_ge(hid_turned, i * GROUPS + (q + 1))
                            act.activation(hid_hi[:, q % 2, :], ps[:, 6, :], ACT.Copy).then_inc(hid_hi_ready, 1)
                    if s == behind(GATHER_ROW):
                        hg_high(i + 1)
                    if s < CUTS:
                        sl = slot(ST_MOE + s // 2)
                        if s % 2 == 0:
                            act.wait_ge(loaded[sl], i * (16 * FC // SLOTS) + 16 * ((ST_MOE + s // 2) // SLOTS + 1))
                        act.wait_ge(stage_used, i * CUTS + (ST_MOE + s - W_BUFS + 1))
                        act.activation(w_hi[:, s % W_BUFS, :], ring[:, sl, s % 2 * CUT * ROW:(s % 2 + 1) * CUT * ROW],
                                       ACT.Copy).then_inc(hi_ready, 1)
            last_output(items)
            act.wait_ge(act_done, items * GROUPS + FC)
            act.dma_start(gain_out, norm_out).then_inc(no_in, 16)
            square_sum(4)
            act.activation(xn[:, 0, :], x[:, 0, :], ACT.Copy, scale=rstd[:, 0:1]).then_inc(xn0_ready, 1)
            act.wait_ge(fin_ready, 1)
            act.dma_start(y_out[:, 1, :], xn[:, 1, :]).then_inc(y_stored, 16)
            act.wait_ge(fin_ready, 2)
            act.dma_start(y_out[:, 0, :], xn[:, 0, :]).then_inc(y_stored, 16)
            act.wait_ge(y_stored, 32)
            act.wait_ge(m_stored, 16)
            for i in range(2):
                act.wait_ge(c_stored[i], 16 * (HEADS // 2))

        @block.vector
        def _(dve):
            n_chain = [0]

            def link(ins):
                n_chain[0] = n_chain[0] + 1
                ins.then_inc(dve_chain, 1)
                dve.wait_ge(dve_chain, n_chain[0])

            STT, TT, TS = dve.scalar_tensor_tensor, dve.tensor_tensor, dve.tensor_scalar

            def rsqrt(out, total, n, width, last=None):
                v, y, t = (root[:, i, 0:width] for i in range(3))
                bits = mybir.dt.int32
                link(TS(v, total, 1.0 / n, EPS, ALU.mult, ALU.add))
                link(TS(t.bitcast(bits), v.bitcast(bits), 1, None, ALU.logical_shift_right))
                link(TS(y.bitcast(bits), t.bitcast(bits), -1.0, float(0x5F3759DF), ALU.mult, ALU.add))
                for step in range(3):
                    link(TT(t, y, y, ALU.mult))
                    link(STT(t, t, -0.5, v, ALU.mult, ALU.mult))
                    end = STT(out if step == 2 else y, t, 1.5, y, ALU.add, ALU.mult)
                    if step < 2:
                        link(end)
                return end

            dve.wait_ge(cond_exp, 1)
            link(TS(cd[:, :], ce[:, :], 1.0, None, ALU.add))
            link(dve.reciprocal(ce[:, :], cd[:, :]))
            TT(silu_c[:, :], vec[:, V_COND:V_COND + KD * G], ce[:, :], ALU.mult).then_inc(cond_ready, 1)
            dve.wait_ge(x_in_s, 16)
            dve.wait_ge(pos_in, 16)
            TT(x[:, 1, :], x[:, 1, :], gate[:, 1, :], ALU.add).then_inc(x_ready, 1)

            def modulation(hv):
                v, half = hv // 2, (hv % 2) * KD // 2
                ks = slice(half, half + KD // 2)

                def spread(at):
                    return vec[:, at + half:at + half + KD // 2].unsqueeze(2).to_broadcast([P, KD // 2, G])

                dve.wait_ge(stage_used, ada_stage(2 * hv + 1) + 1)
                bias = spread(V_ADA + v * KD)
                src = ps[:, MODB + hv % 2, :].rearrange("p (k g r) -> p k g r", k=KD // 2, g=G)[:, :, :, 0]
                if v % 3 == 1:
                    q = v // 3
                    link(TT(mod[:, v, ks, :], src, bias, ALU.add))
                    gain = V_NMIX + (q // 2) * KD if q % 2 == 0 else V_NFFN + (q // 2) * KD
                    STT(scl[:, q, ks, :], mod[:, v, ks, :], 1.0, spread(gain), ALU.add, ALU.mult
                        ).then_inc(mod_ready, 1)
                else:
                    TT(mod[:, v, ks, :], src, bias, ALU.add).then_inc(mod_ready, 1)

            def square_sum(q):
                link(dve.tensor_tensor_reduce(out=xn[:, 1, :], in0=x[:, 1, :], in1=x[:, 1, :], scale=1.0, scalar=0.0,
                                              op0=ALU.mult, op1=ALU.add, accum_out=ss[:, 1:2]))
                dve.wait_ge(ss_ready, q + 1)
                rsqrt(rstd[:, :], ss[:, :], D, G).then_inc(rstd_ready, 1)
                dve.wait_ge(rstd_ready, q + 1)

            def norm(q):
                dve.wait_ge(x_ready, q + 1)
                square_sum(q)
                TS(xn[:, 1, :], x[:, 1, :], rstd[:, 1:2], None, ALU.mult).then_inc(xn1_ready, 1)

            def norm_turn(q):
                if q > 0:
                    norm(q)
                for b in range(2):
                    dve.wait_ge(turned, 4 * q + b + 3)
                    if q == 0 and b == 0:
                        dve.wait_ge(mod_ready, 4)
                    for i in range(4):
                        k = 4 * b + i
                        TS(hT[:, k, P:T], ps[:, YB + 2 + b, i * P:(i + 1) * P], scl[:, q, k, 1:2], mod[:, 3 * q, k, 1:2],
                           ALU.mult, ALU.add).then_inc(hT1_ready, 1)

            norm(0)
            for hv in range(ADA_FIRST // 2):
                modulation(hv)
            norm_turn(0)

            dve.wait_ge(gate_raw, 2)
            for w in range(2):
                dve.tensor_copy(rt[0:32, 2 + w, :, :], rt[0:32, w, :, :])
                link(dve.tensor_copy(rt[32:ROWS, 2 + w, :, :], rt[32:ROWS, w, :, ::-1]))
            STT(rt[:, 4, :, :], rt[:, 3, :, :], -1.0, rt[:, 3, :, :], ALU.mult, ALU.min).then_inc(gate_abs, 1)
            dve.wait_ge(gate_ln, 1)
            link(STT(rt[:, 7, :, :], rt[:, 3, :, :], 0.0, rt[:, 6, :, :], ALU.min, ALU.subtract))
            one = cst[0:ROWS, C_ONE:C_ONE + P]
            for g in range(G):
                link(dve.tensor_tensor_scan(rt[:, 3, g, :], one, rt[:, 7, g, :], 0.0, ALU.mult, ALU.add))
            link(TT(row[:, 0:2, :], rt[:, 2, :, :], rt[:, 3, :, :], ALU.subtract))
            link(dve.tensor_tensor_scan(row[:, 6, :], one, row[:, 0, :], 0.0, ALU.mult, ALU.max))
            link(dve.tensor_tensor_scan(row[:, 7, :], one, row[:, 1, :], rc[:, 2:3], ALU.mult, ALU.max))
            link(TS(small[0:ROWS, 0:1], row[:, 6, P - 1:P], -1.0, None, ALU.mult))
            TT(rt[:, 4, :, :], rt[:, 3, :, :], row[:, 6:8, :], ALU.add).then_inc(gate_M, 1)
            dve.wait_ge(gate_M, 1)
            dve.tensor_copy(small[0:ROWS, 1:2], rt[:, 4, 0, P - 1:P]).then_inc(m_ready, 1)
            dve.wait_ge(gate_exps, 3)
            dve.tensor_copy(nat[0:32, :, :], row[0:32, :, :]).then_inc(nat_ready, 1)
            dve.tensor_copy(nat[32:ROWS, :, :], row[32:ROWS, :, ::-1]).then_inc(nat_ready, 1)

            def conv_qk(s):
                dve.wait_ge(proj_out, s + 1)
                if s >= 2:
                    dve.wait_ge(qk_done, s - 1)
                for t in range(A_TAPS):
                    for j in range(2):
                        w = vec[:, V_ACONV + t * 2 * KD + 2 * s + j:V_ACONV + t * 2 * KD + 2 * s + j + 1]
                        out = ca[:, s % 2, j, :].rearrange("p (g t) -> p g t", g=G)
                        src = pad[:, s % 2, j, :, t:t + P]
                        ins = (TS(out, src, w, None, ALU.mult) if t == 0 else STT(out, src, w, out, ALU.mult, ALU.add))
                    if t < A_TAPS - 1:
                        link(ins)
                ins.then_inc(conv_done, 1)

            def silu_qk(s):
                dve.wait_ge(qk_exp, s + 1)
                STT(qkT[:, 2 * s:2 * s + 2, :], eq[:, s % 2, :, :], 1.0, ca[:, s % 2, :, :], ALU.add, ALU.mult
                    ).then_inc(qk_done, 1)

            for s in range(HEADS):
                conv_qk(s)
                if s >= 1:
                    silu_qk(s - 1)
            silu_qk(HEADS - 1)
            dve.wait_ge(cols_psum, 1)
            gate_cols = ps[:, MISC, 0:6 * ROWS].rearrange("p (q r) -> p q r", q=6)
            dve.tensor_copy(col, gate_cols)
            link(TS(kscale, gate_cols[:, 4:6, :], 0.5, None, ALU.mult))
            TS(kscale[:, 0, :], kscale[:, 0, :], Q_SCALE, None, ALU.mult).then_inc(cols_ready, 1)
            for s in range(2 * HEADS, N_IN):
                i = 2 * (s - 2 * HEADS)
                dve.wait_ge(proj_out, s + 1)
                TS(so[:, i:i + 2, :], so[:, i:i + 2, :], 1.0, 0.5, ALU.add, ALU.mult).then_inc(so_ready, 1)

            def masked(it):
                dve.wait_ge(front, it + 1)
                TT(tmp[:, it % 2, :, :], ps[:, UB + it % 2, P:3 * P].rearrange("p (d t) -> p d t", d=DIR), mask,
                   ALU.add).then_inc(tmp_ready, 1)

            def out_gate(it):
                h, g = it // 2, it % 2
                dve.wait_ge(hT_back, it + 1)
                for c in range(2):
                    f = 2 * h + c
                    o = so[:, f, g * P:(g + 1) * P]
                    ins = STT(o, ps[:, UB + it % 2, c * P:(c + 1) * P], vec[:, V_GN + f:V_GN + f + 1], o,
                              ALU.mult, ALU.mult)
                ins.then_inc(og_ready, 1)

            dve.wait_ge(so_ready, HEADS)
            masked(0)
            made = ADA_FIRST // 2
            for it in range(ITS):
                h, g = it // 2, it % 2
                b = UB + it % 2
                dve.wait_ge(p_ready, it + 1)
                if it >= 2:
                    dve.wait_ge(num_done, it - 1)
                if it == 0:
                    dve.wait_ge(qk_done, HEADS)
                for d in range(DIR):
                    ins = STT(sT[:, it % 2, d, :], pe_[:, it % 2, d, :], 0.25 * Q_SCALE, ps[:, b, 0:P], ALU.mult,
                              ALU.mult)
                ins.then_inc(s_ready, 1)
                if g == 0:
                    if it >= 1:
                        dve.wait_ge(num_done, it)
                    for d in range(DIR):
                        r = 32 * d + h
                        ins = TS(kw[:, d, :], ps[:, b, 3 * P:4 * P], kscale[:, 1, r:r + 1], None, ALU.mult)
                    ins.then_inc(kw_ready, 1)
                if it >= 1:
                    out_gate(it - 1)
                    while 2 * (made + 1) <= ada_through(it - 1):
                        modulation(made)
                        made += 1
                if it + 1 < ITS:
                    masked(it + 1)
                dve.wait_ge(num_done, it + 1)
                if g == 0:
                    src = ps[:, YB:YB + 2, :]
                    link(dve.tensor_copy(small[:, 8:10].unsqueeze(2), src[:, :, DV:DVA]))
                    den = small[:, 8:10]
                else:
                    src = nm
                    dve.wait_ge(qc_used, it + 1)
                    link(TT(nm, ps[:, YB:YB + 2, 0:DVA], qcs, ALU.add))
                    link(dve.tensor_copy(small[:, 8:10].unsqueeze(2), nm[:, :, DV:DVA]))
                    den = small[:, 8:10]
                link(STT(small[:, 10:12], den, -1.0, den, ALU.mult, ALU.max))
                link(TT(small[:, 12:14], small[:, 10:12], col[:, 2 + g, h:h + 33:32], ALU.max))
                link(dve.reciprocal(small[:, 14:16], small[:, 12:14]))
                link(TS(h0, src[:, 0, 0:DV], small[:, 14:15], None, ALU.mult))
                if it >= 1:
                    dve.wait_ge(hn_ready, it)
                STT(hs, src[:, 1, 0:DV], small[:, 15:16], h0, ALU.mult, ALU.add).then_inc(num_used, 1)
                dve.wait_ge(hs_squared, it + 1)
                link(rsqrt(small[:, 6:7], small[:, 4:5], DV, 1))
                if it >= 1:
                    dve.wait_ge(hT_back, it)
                TS(hn, hs, small[:, 6:7], None, ALU.mult).then_inc(hn_ready, 1)
            out_gate(ITS - 1)
            while 2 * (made + 1) <= ADA_FIRST + ADA_MID:
                modulation(made)
                made += 1

            def residual(q, last_stage, scale=1.0):
                dve.wait_ge(stage_used, last_stage)
                dve.wait_ge(gateb_ready, 4 * q + 4)
                gv = gate_b[:, 0:G * D].rearrange("p (b n) -> p b n", b=4)
                for b in range(4):
                    ins = STT(gv[:, b, :], gv[:, b, :], scale, ps[:, YB + b, :], ALU.mult, ALU.mult)
                link(ins)
                TT(x[:, :, :], x[:, :, :], gate, ALU.add).then_inc(x_ready, 1)

            def ff_low(c, j):
                n = 2 * c + j
                dve.wait_ge(hi_ready, n + 1)
                TT(w_lo[:, n % W_BUFS, :], ring[:, slot(ST_FF + c), j * CUT * ROW:(j + 1) * CUT * ROW],
                   w_hi[:, n % W_BUFS, :].bitcast(f32), ALU.subtract).then_inc(split_ready, 1)

            for j in range(2):
                ff_low(0, j)
            residual(0, ST_OUT + N_OUT)
            norm_turn(1)
            for b in range(2):
                ks = slice(4 * b, 4 * b + 4)
                dve.wait_ge(hT_hi_ready, b + 1)
                TT(hT_lo[b], hT[:, ks, :], hT_hi[:, ks, :].bitcast(f32), ALU.subtract).then_inc(hT_lo_ready, 1)

            for c in range(FC):
                for j in range(2):
                    if c + 1 < FC:
                        ff_low(c + 1, j)
                    if j == 0:
                        dve.wait_ge(e_done, c + 1)
                        up = ps[:, UB + c % 2, T:2 * T]
                        link(STT(ff_sg[:, c % 2, :], ff_th[:, c % 2, :], 1.0, ps[:, UB + c % 2, 0:T], ALU.add, ALU.mult))
                        STT(fact[:, c % 2, :], ff_sg[:, c % 2, :], 0.5, up, ALU.mult, ALU.mult)
                        link(STT(ff_hi[:, c % 2, :], ff_sg[:, c % 2, :], 0.5, up, ALU.mult, ALU.mult))
                        TT(ff_lo[:, c % 2, :], fact[:, c % 2, :], ff_hi[:, c % 2, :].bitcast(f32), ALU.subtract
                           ).then_inc(act_done, 1)
            residual(1, ST_FF + FC)
            norm_turn(2)

            dve.wait_ge(memsets, 4)
            for s in range(N_PW1):
                dve.wait_ge(glu_exp, s + 1)
                link(TS(fd, fe[:, s % 2, :], 1.0, 0.5, ALU.add, ALU.mult))
                TT(pad31[:, s, :, 15:15 + P], ps[:, UB + s % 2, 0:T].rearrange("p (g t) -> p g t", g=G),
                   fd.rearrange("p (g t) -> p g t", g=G), ALU.mult).then_inc(glu_done, 1)
                dve.wait_ge(glu_done, s + 1)
                out = cv[:, s, :].rearrange("p (g t) -> p g t", g=G)
                even_odd = out, odd.rearrange("p (g t) -> p g t", g=G)
                begun = n_chain[0]
                for t in range(B_TAPS):
                    w = vec[:, V_BCONV + t * KD + s:V_BCONV + t * KD + s + 1]
                    src, to = pad31[:, s, :, t:t + P], even_odd[t % 2]
                    if t == 0:
                        ins = TS(to, src, w, vec[:, V_BDW + s:V_BDW + s + 1], ALU.mult, ALU.add)
                    elif t == 1:
                        ins = TS(to, src, w, None, ALU.mult)
                    else:
                        dve.wait_ge(dve_chain, begun + t - 1)
                        ins = STT(to, src, w, to, ALU.mult, ALU.add)
                    ins.then_inc(dve_chain, 1)
                n_chain[0] = begun + B_TAPS
                dve.wait_ge(dve_chain, n_chain[0])
                TT(out, out, even_odd[1], ALU.add).then_inc(cv_ready, 1)
                while 2 * (made + 1) <= ada_beside(s):
                    modulation(made)
                    made += 1
            dve.wait_ge(rb_ready, 1)
            for k in range(KD + 2):
                if k < KD:
                    STT(z[:, k, :], cv[:, k, :], vec[:, V_BNORM + k:V_BNORM + k + 1], rb, ALU.mult, ALU.mult
                        ).then_inc(z_ready, 1)
                if k >= 2:
                    dve.wait_ge(ez_ready, k - 1)
                    STT(z[:, k - 2, :], ez[:, k - 2, :], 1.0, z[:, k - 2, :], ALU.add, ALU.mult
                        ).then_inc(zs_ready, 1)
            residual(2, ST_PW2 + N_PW2, 0.5)
            norm_turn(3)

            def bc(a):
                return a.unsqueeze(2).to_broadcast([P, G, EXPERTS])

            dve.wait_ge(route_psum, 1)
            link(dve.tensor_copy(lg, ps[:, MISC, 0:G * EXPERTS].rearrange("p (g e) -> p g e", g=G)))
            cur = lg
            for j in range(2):
                link(dve.tensor_reduce(tk[:, j, :], cur, X, ALU.max))
                link(TT(key, cur, bc(tk[:, j, :]), ALU.is_equal))
                link(TT(key, key, desc, ALU.mult))
                link(dve.tensor_reduce(tk[:, 4 + j, :], key, X, ALU.max))
                link(TT(oh[:, j, :, :], desc, bc(tk[:, 4 + j, :]), ALU.is_equal))
                if j == 0:
                    link(STT(l2, oh[:, 0, :, :], -3e38, lg, ALU.mult, ALU.add))
                    cur = l2
            TT(sel, oh[:, 0, :, :], oh[:, 1, :, :], ALU.add).then_inc(sel_ready, 1)
            TT(tk[:, 2, :], tk[:, 1, :], tk[:, 0, :], ALU.subtract).then_inc(route_gap, 1)
            for b in range(2):
                dve.wait_ge(htok_psum, b + 3)
                dve.tensor_copy(htok[:, 1, b * 512:(b + 1) * 512], ps[:, YB + 2 + b, :]).then_inc(htok_ready1, 1)
            dve.wait_ge(route_exp, 1)
            link(TS(tk[:, 6, :], tk[:, 3, :], 1.0, None, ALU.add))
            link(dve.reciprocal(tk[:, 7, :], tk[:, 6, :]))
            link(TT(tk[:, 8, :], tk[:, 7, :], tk[:, 3, :], ALU.mult))
            link(TT(oh[:, 0, :, :], oh[:, 0, :, :], bc(tk[:, 7, :]), ALU.mult))
            link(TT(oh[:, 1, :, :], oh[:, 1, :, :], bc(tk[:, 8, :]), ALU.mult))
            own = item_comb[:, :, 0:EXPERTS]
            link(TT(own, oh[:, 0, :, :], oh[:, 1, :, :], ALU.add))
            dve.wait_ge(pos_psum, 1)
            slots = item_pos[:, :, 0:EXPERTS]
            link(TT(key, ps[:, MISC, 0:G * EXPERTS].rearrange("p (g e) -> p g e", g=G), sel, ALU.mult))
            link(STT(slots, sel, -1.0, key, ALU.add, ALU.add))

            def make_picks(i):
                for g in range(G):
                    p = item_pos[:, g, bass.ds(i, 1)] if not isinstance(i, int) else item_pos[:, g, i:i + 1]
                    w = item_comb[:, g, bass.ds(i, 1)] if not isinstance(i, int) else item_comb[:, g, i:i + 1]
                    TS(pick[:, g, :], iota, p, None, ALU.is_equal)
                    ins = TS(pick_w[:, g, :], iota, p, w, ALU.is_equal, ALU.mult)
                ins.then_inc(pick_ready, 1)

            make_picks(0)
            count, is_over, rank, order = (over[:, n, :] for n in range(4))
            link(dve.tensor_copy(count, ps[:, MISC, G * EXPERTS:(G + 1) * EXPERTS]))
            link(TS(is_over, count, float(P), None, ALU.is_gt))
            link(dve.tensor_tensor_scan(rank, cst[:, C_ONE:C_ONE + EXPERTS], is_over, 0.0, ALU.mult, ALU.add))
            link(TT(order, is_over, rank, ALU.mult))
            over_items = slice(EXPERTS, COLS)

            def each(a):
                return a.unsqueeze(1).to_broadcast([P, G] + list(a.shape[1:]))

            link(TT(hit, order.unsqueeze(1).to_broadcast([P, more, EXPERTS]),
                    iota[:, 1:1 + more].unsqueeze(2).to_broadcast([P, more, EXPERTS]), ALU.is_equal))
            TT(hit_desc, hit, desc[:, 0, :].unsqueeze(1).to_broadcast([P, more, EXPERTS]), ALU.mult)
            for g in range(G):
                of_group = [a[:, g, :].unsqueeze(1).to_broadcast([P, more, EXPERTS]) for a in (slots, own)]
                STT(prod[:, g, :, :], of_group[0], -float(P), hit, ALU.add, ALU.mult)
                ins = TT(prod_comb[:, g, :, :], of_group[1], hit, ALU.mult)
            link(ins)
            dve.tensor_reduce(has, hit, X, ALU.add)
            dve.tensor_reduce(who, hit_desc, X, ALU.add)
            dve.tensor_reduce(first_slots, prod, X, ALU.add)
            link(dve.tensor_reduce(item_comb[:, :, over_items], prod_comb, X, ALU.add))
            STT(item_pos[:, :, over_items], first_slots, -1.0, each(has), ALU.add, ALU.add)
            STT(plan_f[:, 2:2 + OVER], has[:, 0:OVER], float(EXPERTS), who[:, 0:OVER], ALU.mult, ALU.subtract)
            dve.memset(plan_f[:, 1:2], float(EXPERTS - 1))
            dve.memset(plan_f[:, 5:7], 0.0)
            link(TS(plan_f[:, 0:1], rank[:, EXPERTS - 1:EXPERTS], float(EXPERTS), None, ALU.add))
            link(TS(plan_f[:, 7:8], rank[:, EXPERTS - 1:EXPERTS], 1.0, None, ALU.add))
            dve.tensor_copy(plan[0:1, :], plan_f[0:1, :]).then_inc(plan_ready, 1)

            def hg_low(i):
                dve.wait_ge(hg_hi_ready, i + 1)
                TT(hg_lo, ps[:, UB:UB + 2, :].rearrange("p b (k t) -> p (b k) t", k=4),
                   hg_hi.bitcast(f32), ALU.subtract).then_inc(hg_ready, 1)

            def add_output(i, n):
                dve.wait_ge(scattered, i * 4 + (n + 1))
                dve.wait_ge(acc_added, i * 4 + (n + 1))
                a = acc[:, n // 2, (n % 2) * 512:(n % 2 + 1) * 512]
                TT(a, ps[:, 7, :], a, ALU.add).then_inc(acc_added, 1)

            hg_low(0)
            dve.wait_ge(plan_ready, 1)
            items = dve.value_load(plan[0:1, 0:1], min_val=EXPERTS, max_val=ITEMS)
            start = n_chain[0]
            with dve.Fori(0, items) as i:
                for s in range(CUTS + 1):
                    for n in range(4):
                        if s == behind(SCATTER_ROWS[n]):
                            add_output(i, n)
                    if s == behind(BACK_ROW) + 1:
                        dve.wait_ge(picks_used, i + 1)
                        dve.wait_ge(gathered, i + 1)
                        make_picks(i + 1)
                    for q in range(GROUPS):
                        b = 2 * (q % 2)
                        if s == behind(UP_END[q]):
                            dve.wait_ge(e_done, i * GROUPS + (FC + q + 1))
                            n_chain[0] = i * GROUPS + (start + q)
                            link(STT(sg, th, 1.0, ps[:, b, :], ALU.add, ALU.mult))
                            STT(hid_tok, sg, 0.5, ps[:, b + 1, :], ALU.mult, ALU.mult).then_inc(act_done, 1)
                        if s == behind(TURN_ROW[q]):
                            dve.wait_ge(hid_hi_ready, i * GROUPS + (q + 1))
                            TT(hid_lo[:, q % 2, :], ps[:, 6, :], hid_hi[:, q % 2, :].bitcast(f32), ALU.subtract
                               ).then_inc(hid_ready, 1)
                    if s == behind(GATHER_ROW):
                        hg_low(i + 1)
                    if s < CUTS:
                        dve.wait_ge(hi_ready, i * CUTS + (FF_CUTS + s + 1))
                        TT(w_lo[:, s % W_BUFS, :], ring[:, slot(ST_MOE + s // 2), s % 2 * CUT * ROW:(s % 2 + 1) * CUT * ROW],
                           w_hi[:, s % W_BUFS, :].bitcast(f32), ALU.subtract).then_inc(split_ready, 1)
            n_chain[0] = items * GROUPS + start
            dve.wait_ge(acc_added, items * 4 + 1)
            dve.wait_ge(gateb_ready, 16)
            link(TT(acc, acc, gate, ALU.mult))
            link(TT(x[:, :, :], x[:, :, :], acc, ALU.add))
            for n in range(5):
                if n < 4:
                    part_n = n // 2, slice((n % 2) * 512, (n % 2 + 1) * 512)
                    dve.wait_ge(scattered, items * 4 + (n + 1))
                    TT(acc[:, part_n[0], part_n[1]], ps[:, LAST_BANKS[n], :], gate[:, part_n[0], part_n[1]], ALU.mult
                       ).then_inc(dve_chain, 1)
                if n > 0:
                    dve.wait_ge(dve_chain, n_chain[0] + n)
                    ins = TT(x[:, before[0], before[1]], x[:, before[0], before[1]], acc[:, before[0], before[1]],
                             ALU.add)
                before = part_n
            ins.then_inc(x_ready, 1)
            n_chain[0] = n_chain[0] + 4
            dve.wait_ge(no_in, 16)
            dve.wait_ge(x_ready, 5)
            square_sum(4)
            no = gain_out
            STT(xn[:, 1, :], x[:, 1, :], rstd[:, 1:2], no, ALU.mult, ALU.mult).then_inc(fin_ready, 1)
            dve.wait_ge(xn0_ready, 5)
            TT(xn[:, 0, :], xn[:, 0, :], no, ALU.mult).then_inc(fin_ready, 1)

        @block.tensor
        def _(pe):
            def arrived(n, j=None):
                j = n if j is None else j
                sl = slot(j)
                turn = n // SLOTS if isinstance(n, int) else None
                assert turn is not None
                pe.wait_ge(loaded[sl], 16 * (turn + 1))
                return ring[:, sl, :]

            def ada(a, n):
                w = arrived(n)
                hv = a // 2
                if a % 2 == 0 and hv >= 2:
                    pe.wait_ge(mod_ready, hv - 1)
                    if hv == ADA_FIRST // 2 + 1:
                        pe.wait_ge(cols_ready, 1)
                for j in range(2):
                    c = (2 * (a % 2) + j) * P
                    for k in range(KD):
                        ins = pe.matmul(ps[:, MODB + hv % 2, c:c + P], w[:, k * 256 + j * P:k * 256 + (j + 1) * P],
                                        silu_c[:, k * G:(k + 1) * G].unsqueeze(2).to_broadcast([P, G, P // G]), start=(k == 0), stop=(k == KD - 1))
                ins.then_inc(stage_used, 1)

            def norm_turn(q):
                for g in range(G):
                    pe.wait_ge([xn0_ready, xn1_ready][g], q + 1)
                    for b in range(2):
                        for i in range(4):
                            k = 4 * b + i
                            ins = pe.transpose(ps[:, YB + 2 * g + b, i * P:(i + 1) * P], xn[:, g, k * P:(k + 1) * P],
                                               ident)
                        ins.then_inc(turned, 1)
                pe.wait_ge(hT0_ready, 8 * q + 8)
                pe.wait_ge(hT1_ready, 8 * q + 8)

            def tokens(f, k, g):
                return f[:, k, g * P:(g + 1) * P]

            pe.wait_ge(cond_ready, 1)
            for a in range(ADA_FIRST):
                ada(a, ada_stage(a))
            pe.wait_ge(cst_in, 16)
            norm_turn(0)
            pe.wait_ge(late_in, 48)
            for w in range(2):
                for k in range(KD):
                    ins = pe.matmul(ps[0:ROWS, MISC, w * T:(w + 1) * T], wg[:, k, w, :], hT[:, k, :],
                                    start=(k == 0), stop=(k == KD - 1))
            ins.then_inc(gates_psum, 1)

            for s in range(N_IN):
                n = ST_IN + s
                w = arrived(n)
                b = UB + s % 2
                if s >= 2:
                    pe.wait_ge(proj_out, s - 1)
                for j in range(2):
                    for k in range(KD):
                        if HEADS <= s < 2 * HEADS:
                            ins = pe.matmul(ps[:, b, j * T:(j + 1) * T], tokens(hT, k, j), w[:, k * 256:(k + 1) * 256],
                                            start=(k == 0), stop=(k == KD - 1))
                        else:
                            ins = pe.matmul(ps[:, b, j * T:(j + 1) * T], w[:, k * 256 + j * P:k * 256 + (j + 1) * P],
                                            hT[:, k, :], start=(k == 0), stop=(k == KD - 1))
                ins.then_inc(stage_used, 1)
                if s == 2 * HEADS:
                    pe.wait_ge(nat_ready, 2)
                    for q in range(6):
                        ins = pe.transpose(ps[:, MISC, q * ROWS:(q + 1) * ROWS], nat[:, q, :], ident[0:ROWS, 0:ROWS])
                    ins.then_inc(cols_psum, 1)

            def front_step(it):
                h, g = it // 2, it % 2
                b = UB + it % 2
                if it >= 2:
                    pe.wait_ge(s_ready, it - 1)
                    pe.wait_ge(kw_ready, it // 2)
                    pe.wait_ge(og_ready, it - 1)
                pe.matmul(ps[:, b, 0:P], tokens(qkT, HEADS + h, g), tokens(qkT, h, g), start=True, stop=True)
                for d in range(DIR):
                    r = 32 * d + h
                    ins = pe.matmul(ps[:, b, (1 + d) * P:(2 + d) * P], ident[0:ROWS, r:r + 1].to_broadcast([ROWS, P]),
                                    nat[:, 6 + g, :], start=True, stop=True)
                if g == 0:
                    ins = pe.transpose(ps[:, b, 3 * P:4 * P], tokens(qkT, HEADS + h, 0), ident)
                ins.then_inc(front, 1)

            def turn_head(it):
                pe.wait_ge(hn_ready, it + 1)
                for c in range(2):
                    ins = pe.transpose(ps[:, UB + it % 2, c * P:(c + 1) * P], hn[:, c * P:(c + 1) * P], ident)
                ins.then_inc(hT_back, 1)

            pe.wait_ge(qk_done, HEADS)
            pe.wait_ge(proj_out, N_IN)
            front_step(0)
            a = ADA_FIRST
            for it in range(ITS):
                h, g = it // 2, it % 2
                pe.wait_ge(s_ready, it + 1)
                if g == 0:
                    pe.wait_ge(kw_ready, h + 1)
                else:
                    pe.wait_ge(c0_in[h % 2], 16 * (h // 2 + 1))
                if it >= 1:
                    pe.wait_ge(qc_used, it)
                    pe.wait_ge(num_used, it)
                for d in range(DIR):
                    if g == 0:
                        pe.matmul(ps[:, QB + d, 0:DVA], kw[:, d, :], vaug[:, 0, h, :], start=True, stop=True)
                    else:
                        pe.matmul(ps[:, QB + d, 0:DVA], tokens(qkT, h, 1), c0b[:, h % 2, d, :], start=True, stop=True)
                for d in range(DIR):
                    ins = pe.matmul(ps[:, YB + d, 0:DVA], sT[:, it % 2, d, :], vaug[:, g, h, :], start=True, stop=True)
                ins.then_inc(num_done, 1)
                if it + 1 < ITS:
                    front_step(it + 1)
                while a < ada_through(it):
                    ada(a, ada_stage(a))
                    a += 1
                turn_head(it)

            def gate_rows(q):
                v = 3 * q + 2
                pe.wait_ge(mod_ready, 2 * (v + 1))
                if q == 0:
                    pe.wait_ge(mod_ready, (ADA_FIRST + ADA_MID) // 2)
                for i in range(4):
                    for c in range(4):
                        k = 4 * (i % 2) + c
                        ins = pe.matmul(ps[:, i, c * P:(c + 1) * P],
                                        mod[:, v, k, i // 2:i // 2 + 1].to_broadcast([P, P]), ident,
                                        start=True, stop=True)
                    ins.then_inc(gateb_psum, 1)

            def down(src, base, stages, src_ready=None):
                for s in range(stages):
                    w = arrived(base + s)
                    for kk in range(2):
                        k = 2 * s + kk
                        if src_ready is not None:
                            pe.wait_ge(src_ready, k + 1)
                        for g in range(G):
                            for hf in range(2):
                                ins = pe.matmul(ps[:, YB + 2 * g + hf, :], tokens(src, k, g),
                                                w[:, kk * D + hf * 512:kk * D + (hf + 1) * 512],
                                                start=(k == 0), stop=(k == 2 * stages - 1))
                    ins.then_inc(stage_used, 1)

            pe.wait_ge(og_ready, ITS)
            gate_rows(0)
            pe.wait_ge(num_used, ITS)
            pe.wait_ge(qc_used, ITS)
            pe.wait_ge(gateb_ready, 4)
            down(so, ST_OUT, N_OUT)
            gate_rows(1)
            norm_turn(1)
            pe.wait_ge(gateb_ready, 8)

            def three(out, a_hi, a_lo, b_hi, b_lo, start, stop):
                pe.matmul(out, a_hi, b_hi, start=start, stop=False)
                pe.matmul(out, a_hi, b_lo, start=False, stop=False)
                return pe.matmul(out, a_lo, b_hi, start=False, stop=stop)

            def up_part(c):
                if c >= 2:
                    pe.wait_ge(act_done, c - 1)
                for j in range(2):
                    for k in range(KD):
                        i, n = divmod(j * KD + k, FRONT)
                        if n == 0:
                            pe.wait_ge(split_ready, 2 * c + i + 1)
                        w = slice(n * P, (n + 1) * P)
                        b = (2 * c + i) % W_BUFS
                        ins = three(ps[:, UB + c % 2, j * T:(j + 1) * T], w_hi[:, b, w], w_lo[:, b, w], hT_hi[:, k, :],
                                    hT_lo[k // 4][:, k % 4, :], k == 0, k == KD - 1)
                        if j * KD + k == FRONT - 1:
                            ins.then_inc(front_used, 1)
                ins.then_inc(u_done, 1)

            def down_part(c):
                b = (2 * c + 1) % W_BUFS
                pe.wait_ge(act_done, c + 1)
                for g in range(G):
                    for hf in range(2):
                        w = slice(ROW + hf * 512, ROW + (hf + 1) * 512)
                        t = slice(g * P, (g + 1) * P)
                        ins = three(ps[:, YB + 2 * g + hf, :], ff_hi[:, c % 2, t], ff_lo[:, c % 2, t], w_hi[:, b, w],
                                    w_lo[:, b, w], c == 0, c == FC - 1)
                ins.then_inc(stage_used, 1)

            pe.wait_ge(hT_lo_ready, 2)
            up_part(0)
            for c in range(1, FC):
                up_part(c)
                down_part(c - 1)
            down_part(FC - 1)
            gate_rows(2)
            norm_turn(2)
            pe.wait_ge(gateb_ready, 12)

            def square_sum(s):
                pe.wait_ge(sq_ready, s + 1)
                pe.matmul(ps[:, YB, 0:T], ones, sqb[:, s % 2, :], start=(s == 0), stop=(s == N_PW1 - 1)
                          ).then_inc(ssq_done, 1)

            for s in range(N_PW1):
                w = arrived(pw1_stage(s))
                if s >= 2:
                    pe.wait_ge(glu_done, s - 1)
                for j in range(2):
                    for k in range(KD):
                        ins = pe.matmul(ps[:, UB + s % 2, j * T:(j + 1) * T], w[:, (j * KD + k) * P:(j * KD + k + 1) * P],
                                        hT[:, k, :], start=(k == 0), stop=(k == KD - 1))
                ins.then_inc(stage_used, 1)
                while a < ada_beside(s):
                    ada(a, ada_stage(a))
                    a += 1
                if s >= 2:
                    square_sum(s - 2)
            square_sum(N_PW1 - 2)
            square_sum(N_PW1 - 1)
            down(z, ST_PW2, N_PW2, zs_ready)
            gate_rows(3)
            norm_turn(3)
            pe.wait_ge(gateb_ready, 14)
            for g in range(G):
                for k in range(KD):
                    ins = pe.matmul(ps[:, MISC, g * EXPERTS:(g + 1) * EXPERTS], tokens(hT, k, g), wr[:, k, :],
                                    start=(k == 0), stop=(k == KD - 1))
            ins.then_inc(route_psum, 1)
            pe.wait_ge(gateb_ready, 16)
            for g in range(G):
                for b in range(2):
                    for i in range(4):
                        ins = pe.transpose(ps[:, YB + 2 * g + b, i * P:(i + 1) * P], tokens(hT, 4 * b + i, g), ident)
                    ins.then_inc(htok_psum, 1)
            pe.wait_ge(sel_ready, 1)
            for g in range(G):
                pe.matmul(ps[:, MISC, g * EXPERTS:(g + 1) * EXPERTS], tri, sel[:, g, :], start=True, stop=(g == 0))
                if g == 1:
                    pe.matmul(ps[:, MISC, g * EXPERTS:(g + 1) * EXPERTS], ones, sel[:, 0, :], start=False, stop=True)
            for g in range(G):
                ins = pe.matmul(ps[:, MISC, G * EXPERTS:(G + 1) * EXPERTS], ones, sel[:, g, :], start=(g == 0),
                                stop=(g == G - 1))
            ins.then_inc(pos_psum, 1)

            def gather(i):
                pe.wait_ge(pick_ready, i + 1)
                for k in range(KD):
                    for g in range(G):
                        ins = pe.matmul(ps[:, UB + k // 4, (k % 4) * P:(k % 4 + 1) * P], htok[:, g, k * P:(k + 1) * P],
                                        pick[:, g, :], start=(g == 0), stop=(g == G - 1))
                ins.then_inc(gathered, 1)

            def scatter(i, n):
                if n == 0:
                    pe.wait_ge(y_ready, i + 1)
                    pe.wait_ge(back_ready, i + 1)
                pe.wait_ge(acc_added, i * 4 + (n + 1))
                pe.matmul(ps[:, 7, :], back[:, n // 2, :], y_sb[:, (n % 2) * 512:(n % 2 + 1) * 512],
                          start=True, stop=True).then_inc(scattered, 1)

            def product(out, hi, lo, w, start, stop):
                w = (slice(None), w[0], slice(w[1], w[1] + ROW))
                return three(out, hi, lo, w_hi[w], w_lo[w], start, stop)

            pe.wait_ge(htok_ready0, 2)
            pe.wait_ge(htok_ready1, 2)
            gather(0)
            pe.wait_ge(plan_ready, 1)
            items = pe.value_load(plan[0:1, 0:1], min_val=EXPERTS, max_val=ITEMS)
            with pe.Fori(0, items) as i:
                pe.wait_ge(hg_ready, i + 1)
                for r, (kind, q, k, half) in enumerate(EXPERT_ROWS):
                    s = r // CUT
                    if r % CUT == 0:
                        pe.wait_ge(split_ready, i * CUTS + (FF_CUTS + s + 1))
                    w = (s % W_BUFS, (r % CUT) * ROW)
                    if kind == "down":
                        if (k, half) == (0, 0):
                            pe.wait_ge(hid_ready, i * GROUPS + (q + 1))
                            if q == 0:
                                pe.wait_ge(y_ready, i + 1)
                        c = slice(k * P, (k + 1) * P)
                        ins = product(ps[:, YB + half, :], hid_hi[:, q % 2, c], hid_lo[:, q % 2, c], w,
                                      (q, k) == (0, 0), (q, k) == (GROUPS - 1, GC - 1))
                    else:
                        ins = product(ps[:, 2 * (q % 2) + (kind == "up"), :], hg_hi[:, k, :], hg_lo[:, k, :], w,
                                      k == 0, k == KD - 1)
                    if r % CUT == CUT - 1:
                        ins.then_inc(stage_used, 1)
                    if r in UP_END:
                        ins.then_inc(u_done, 1)
                    if r in TURN_ROW:
                        t = TURN_ROW.index(r)
                        pe.wait_ge(act_done, i * GROUPS + (FC + t + 1))
                        for c in range(GC):
                            ins = pe.transpose(ps[:, 6, c * P:(c + 1) * P], hid_tok[:, c * P:(c + 1) * P], ident)
                        ins.then_inc(hid_turned, 1)
                    if r in SCATTER_ROWS:
                        scatter(i, SCATTER_ROWS.index(r))
                    if r == BACK_ROW:
                        pe.wait_ge(acc_added, i * 4 + 5)
                        for g in range(G):
                            ins = pe.transpose(ps[:, 7, g * P:(g + 1) * P], pick_w[:, g, :], ident)
                        ins.then_inc(picks_used, 1)
                    if r == GATHER_ROW:
                        gather(i + 1)
            pe.wait_ge(acc_added, items * 4 + 1)
            pe.wait_ge(y_ready, items + 1)
            pe.wait_ge(back_ready, items + 1)
            for n in range(4):
                pe.matmul(ps[:, LAST_BANKS[n], :], back[:, n // 2, :], y_sb[:, (n % 2) * 512:(n % 2 + 1) * 512],
                          start=True, stop=True).then_inc(scattered, 1)


_INPUTS = ("vecs", "consts", "rowc", "x_in", "pos", "w_gate", "w_router", "mix", "ff", "moe", "c0", "norm_out")
_OUTPUTS = (("y_out", (P, G, D)), ("c_out", (HEADS, P, DIR, DVA)), ("m_out", (ROWS, 1)))


def _constants():
    cst = np.zeros((P, C_ALL), np.float32)
    cst[:, C_ID:C_ID + P] = np.eye(P)
    cst[:, C_ONE:C_ONE + P] = 1.0
    j, t = np.arange(P)[:, None], np.arange(P)[None, :]
    cst[:, C_MASK:C_MASK + P] = np.where(j <= t, 0.0, BIG)
    cst[:, C_MASK + P:C_MASK + 2 * P] = np.where(j >= t, 0.0, BIG)
    cst[:, C_DESC:C_DESC + G * EXPERTS] = np.tile(np.arange(EXPERTS, 0, -1), G)
    cst[:, C_EPS] = EPS
    cst[:, C_TRI:C_TRI + P] = np.where(j < t, 1.0, 0.0)
    cst[:, C_IOTA:C_IOTA + P] = t
    grid_w = 64
    r = np.repeat(np.arange(P // grid_w, dtype=np.float32), grid_w)
    c = np.tile(np.arange(grid_w, dtype=np.float32), P // grid_w)
    quarter = D // 4
    freqs = (np.float32(10000.0) ** (-np.arange(quarter, dtype=np.float32) / quarter)).astype(np.float32)
    ar, ac = r[:, None] * freqs, c[:, None] * freqs
    pos = np.zeros((P, D), np.float32)
    pos[:, :] = np.concatenate([np.sin(ar), np.cos(ar), np.sin(ac), np.cos(ac)], axis=-1)
    return cst, pos


def kernel(**inputs):
    import concourse.bacc as bacc
    from concourse.bass_utils import run_bass_kernel_spmd

    a = {k: np.asarray(v) for k, v in inputs.items()}

    def chunks(v):
        return v.reshape(-1, P).T

    cond = np.stack([a["c_ctx"], a["c"][0]], axis=0).reshape(G, KD, P).transpose(2, 1, 0).reshape(P, KD * G)
    vecs = np.concatenate([chunks(a["b_ada"]), chunks(a["norm_mix"]), chunks(a["norm_ffn"]), chunks(a["a_gn"]),
                           chunks(a["b_b_dw"]), chunks(a["b_norm"]), chunks(a["a_w_conv"]), chunks(a["b_w_dw"]),
                           cond], axis=1)
    consts, pos = _constants()
    rowc = np.zeros((ROWS, 4), np.float32)
    w_gate = np.zeros((P, KD, 2, ROWS), np.float32)
    gw = a["a_w_in"][0][:, 6144:].reshape(KD, P, 4, HEADS).transpose(1, 0, 2, 3)
    for d in range(DIR):
        rowc[32 * d:32 * d + HEADS, 0] = a["a_b_gate"][0, 2 * d]
        rowc[32 * d:32 * d + HEADS, 1] = a["a_b_gate"][0, 2 * d + 1]
        rowc[32 * d:32 * d + HEADS, 2] = a["state_m"][0, 0, d]
        w_gate[:, :, 0, 32 * d:32 * d + HEADS] = gw[:, :, 2 * d]
        w_gate[:, :, 1, 32 * d:32 * d + HEADS] = gw[:, :, 2 * d + 1]

    def columns(w, width):
        n = w.shape[1] // width
        return w.reshape(KD, P, n, width).transpose(2, 1, 0, 3).reshape(n, P, KD * width)

    def rows_of(w, per):
        n = w.shape[0] // P // per
        return w.reshape(n, per, P, D).transpose(0, 2, 1, 3).reshape(n, P, per * D)

    ada = np.concatenate([columns(a["w_ada"][0], 256), columns(a["w_ada"][1], 256)])
    pw1 = a["b_w_pw1"][0]
    pw1 = np.concatenate([columns(pw1[:, :D], P), columns(pw1[:, D:], P)], axis=2)
    beside = [part for s in range(N_PW1) for part in (pw1[s:s + 1], ada[ada_beside(s - 1):ada_beside(s)])]
    mix = np.concatenate([ada[:ADA_FIRST], columns(a["a_w_in"][0][:, :6144], 256),
                          ada[ADA_FIRST:ADA_FIRST + ADA_MID], rows_of(a["a_w_out"][0], 2), *beside,
                          rows_of(a["b_w_pw2"][0], 2)])

    def swiglu(w1, w2):
        return np.concatenate([columns(w1[:, :FF], P), columns(w1[:, FF:], P), rows_of(w2, 1)], axis=2)

    ff = swiglu(a["ff_w1"][0], a["ff_w2"][0])
    moe = np.empty((EXPERTS, FC, P, PER, ROW), np.float32)
    for e in range(EXPERTS):
        w1 = a["moe_w1"][0, e].reshape(KD, P, 2, GROUPS, ROW)
        w2 = a["moe_w2"][0, e].reshape(GROUPS, GC, P, 2, ROW)
        for r, (kind, q, k, half) in enumerate(EXPERT_ROWS):
            moe[e, r // PER, :, r % PER] = w2[q, k, :, half] if kind == "down" else w1[k, :, int(kind == "up"), q]
    moe = moe.reshape(EXPERTS * FC, P, STAGE)
    c0 = np.concatenate([a["state_C"][0, 0], a["state_n"][0, 0][..., None]], axis=-1).transpose(1, 2, 0, 3)
    arrays = dict(vecs=vecs, consts=consts, rowc=rowc,
                  x_in=np.stack([a["x_prompt"][0], a["x_sample"][0]], axis=1), pos=pos, w_gate=w_gate,
                  w_router=a["moe_router"][0].reshape(KD, P, EXPERTS).transpose(1, 0, 2), mix=mix, ff=ff, moe=moe,
                  c0=c0, norm_out=np.broadcast_to(a["norm_out"], (P, D)))
    arrays = {k: np.ascontiguousarray(v) for k, v in arrays.items()}

    nc = bacc.Bacc("TRN2", target_bir_lowering=False, num_devices=1)
    f32 = mybir.dt.float32
    args = [nc.dram_tensor(k, arrays[k].shape, f32, kind="ExternalInput").ap() for k in _INPUTS]
    args += [nc.dram_tensor(k, s, f32, kind="ExternalOutput").ap() for k, s in _OUTPUTS]
    mlstm_conformer_kernel(nc, *args)
    r = run_bass_kernel_spmd(nc, [arrays], core_ids=[0]).results[0]
    y, c, m = (np.asarray(r[k]) for k, _ in _OUTPUTS)
    state = c.transpose(2, 0, 1, 3)
    m2 = np.stack([m[32 * d:32 * d + HEADS, 0] for d in range(DIR)])
    return (np.ascontiguousarray(y[:, 0])[None], np.ascontiguousarray(y[:, 1])[None],
            np.ascontiguousarray(state[..., :DV])[None, None], np.ascontiguousarray(state[..., DV])[None, None],
            m2[None, None])
```
